# Optimizing a Trainium2 kernel written in Bass

```python
import math
import jax, jax.numpy as jnp
from jax import lax
import numpy as np

D_MODEL = 1024
BATCH = 1
SEQ = 1024
DEPTH = 1
DEC_BATCH = 1
DEC_SEQ = 64
PAST_LEN = 256

CHUNK = 64
D_SSM = D_MODEL // 2
SSM_GROUP = 16
N_SSM_GROUPS = D_SSM // SSM_GROUP
SSM_STATE = 64
D_CONV = D_MODEL // 2
CONV_WIDTH = 31
N_BRANCH = 2
D_IN = D_SSM + 2 * D_CONV + N_BRANCH * D_MODEL
N_KEYS = 128
N_EXPERTS = N_KEYS * N_KEYS
PEER_HEADS = 8
PEER_TOPK = 16
D_QUERY = 256
PEER_BLOCK = 128
EPS = 1e-6

kernel_name = 'hybrid_s5_conformer_peer_stream_step'

def _rmsnorm(x, g):
    xf = x.astype(jnp.float32)
    xf = xf * lax.rsqrt(jnp.mean(xf * xf, axis=-1, keepdims=True) + EPS)
    return xf.astype(x.dtype) * g

def _layernorm(x, g, b):
    xf = x.astype(jnp.float32)
    mu = jnp.mean(xf, axis=-1, keepdims=True)
    xc = xf - mu
    xf = xc * lax.rsqrt(jnp.mean(xc * xc, axis=-1, keepdims=True) + EPS)
    return xf.astype(x.dtype) * g + b

def _cplx_affine_combine(e1, e2):
    a1r, a1i, b1r, b1i = e1
    a2r, a2i, b2r, b2i = e2
    return (a2r * a1r - a2i * a1i,
            a2r * a1i + a2i * a1r,
            a2r * b1r - a2i * b1i + b2r,
            a2r * b1i + a2i * b1r + b2i)

def _s5(u, h0_re, h0_im, lam_re, lam_im, log_step, b_re, b_im, c_re, c_im, d_skip):
    n, l, _ = u.shape
    f32 = jnp.float32
    lam_re = lam_re.astype(f32)
    lam_im = lam_im.astype(f32)
    step = jnp.exp(log_step.astype(f32))[:, None]
    decay = jnp.exp(lam_re * step)
    ab_re = decay * jnp.cos(lam_im * step)
    ab_im = decay * jnp.sin(lam_im * step)
    inv = 1.0 / (lam_re * lam_re + lam_im * lam_im)
    k_re = ((ab_re - 1.0) * lam_re + ab_im * lam_im) * inv
    k_im = (ab_im * lam_re - (ab_re - 1.0) * lam_im) * inv
    b_re = b_re.astype(f32)
    b_im = b_im.astype(f32)
    bb_re = k_re[..., None] * b_re - k_im[..., None] * b_im
    bb_im = k_re[..., None] * b_im + k_im[..., None] * b_re
    ug = u.astype(f32).reshape(n, l, N_SSM_GROUPS, SSM_GROUP)
    bu_re = jnp.einsum('nlgh,gph->nlgp', ug, bb_re)
    bu_im = jnp.einsum('nlgh,gph->nlgp', ug, bb_im)
    h0_re = h0_re.astype(f32)
    h0_im = h0_im.astype(f32)
    bu_re = bu_re.at[:, 0].add(ab_re * h0_re - ab_im * h0_im)
    bu_im = bu_im.at[:, 0].add(ab_re * h0_im + ab_im * h0_re)
    a_re = jnp.broadcast_to(ab_re, bu_re.shape)
    a_im = jnp.broadcast_to(ab_im, bu_im.shape)
    _, _, h_re, h_im = lax.associative_scan(_cplx_affine_combine, (a_re, a_im, bu_re, bu_im), axis=1)
    y = (jnp.einsum('nlgp,ghp->nlgh', h_re, c_re.astype(f32))
         - jnp.einsum('nlgp,ghp->nlgh', h_im, c_im.astype(f32))
         + d_skip.astype(f32) * ug)
    return y.reshape(n, l, D_SSM).astype(u.dtype), h_re[:, -1], h_im[:, -1]

def _conv_module(v_in, conv_buf, conv_w, conv_b, ln_g, ln_b, w_conv_out):
    p, q = jnp.split(v_in, 2, axis=-1)
    v = p * jax.nn.sigmoid(q)
    full = jnp.concatenate([conv_buf.astype(v.dtype), v], axis=1)
    out = lax.conv_general_dilated(full, conv_w.astype(v.dtype)[:, None, :], window_strides=(1,),
                                   padding='VALID', dimension_numbers=('NWC', 'WIO', 'NWC'),
                                   feature_group_count=D_CONV) + conv_b
    new_buf = full[:, -(CONV_WIDTH - 1):]
    out = jax.nn.silu(_layernorm(out, ln_g, ln_b))
    return out @ w_conv_out, new_buf

def _peer(xn, w_q, keys1, keys2, u_tab, v_tab):
    n, l, d = xn.shape
    t = n * l
    n_blk = -(-t // PEER_BLOCK)
    flat = jnp.pad(xn.reshape(t, d), ((0, n_blk * PEER_BLOCK - t), (0, 0)))
    half = D_QUERY // 2
    k1 = keys1.astype(jnp.float32)
    k2 = keys2.astype(jnp.float32)

    def block(xb):
        q = (xb @ w_q).astype(jnp.float32).reshape(PEER_BLOCK, PEER_HEADS, 2, half)
        s1 = jnp.einsum('thd,kd->thk', q[:, :, 0], k1)
        s2 = jnp.einsum('thd,kd->thk', q[:, :, 1], k2)
        v1, i1 = lax.top_k(s1, PEER_TOPK)
        v2, i2 = lax.top_k(s2, PEER_TOPK)
        cand = (v1[..., :, None] + v2[..., None, :]).reshape(PEER_BLOCK, PEER_HEADS, PEER_TOPK * PEER_TOPK)
        cidx = (i1[..., :, None] * N_KEYS + i2[..., None, :]).reshape(PEER_BLOCK, PEER_HEADS, PEER_TOPK * PEER_TOPK)
        sc, pos = lax.top_k(cand, PEER_TOPK)
        eidx = jnp.take_along_axis(cidx, pos, axis=-1)
        g = jax.nn.softmax(sc, axis=-1)
        u = jnp.take(u_tab, eidx, axis=0)
        act = jax.nn.gelu(jnp.einsum('thkd,td->thk', u, xb), approximate=False)
        coef = (g * act.astype(jnp.float32)).astype(xb.dtype)
        return jnp.einsum('thk,thkd->td', coef, jnp.take(v_tab, eidx, axis=0))

    out = lax.map(block, flat.reshape(n_blk, PEER_BLOCK, d))
    return out.reshape(n_blk * PEER_BLOCK, d)[:t].reshape(n, l, d)

def _layer(x, h0_re, h0_im, conv_buf, norm_mix, w_in, b_gate, lam_re, lam_im, log_step,
           b_re, b_im, c_re, c_im, d_skip, w_ssm_glu, conv_w, conv_b, ln_g, ln_b, w_conv_out,
           w_out, norm_ffn, w_q, keys1, keys2, u_tab, v_tab):
    xn = _rmsnorm(x, norm_mix)
    z = xn @ w_in
    u_ssm = z[..., :D_SSM]
    v_conv = z[..., D_SSM:D_SSM + 2 * D_CONV]
    gate_pre = z[..., D_SSM + 2 * D_CONV:] + b_gate
    y_ssm, h_re, h_im = _s5(u_ssm, h0_re, h0_im, lam_re, lam_im, log_step, b_re, b_im, c_re, c_im, d_skip)
    pa, qa = jnp.split(jax.nn.gelu(y_ssm, approximate=False) @ w_ssm_glu, 2, axis=-1)
    branch_a = pa * jax.nn.sigmoid(qa)
    branch_b, new_buf = _conv_module(v_conv, conv_buf, conv_w, conv_b, ln_g, ln_b, w_conv_out)
    ga, gb = jnp.split(jax.nn.sigmoid(gate_pre), 2, axis=-1)
    x = x + (ga * branch_a + gb * branch_b) @ w_out
    x = x + _peer(_rmsnorm(x, norm_ffn), w_q, keys1, keys2, u_tab, v_tab)
    return x, h_re, h_im, new_buf

def setup_inputs(seed: int = 0) -> dict:
    key = jax.random.key(seed)
    ks = jax.random.split(key, 32)
    nrm = jax.random.normal
    f32 = jnp.float32
    G, P, H = N_SSM_GROUPS, SSM_STATE, SSM_GROUP
    lam_im0 = math.pi * jnp.arange(P, dtype=f32)
    log_lo, log_hi = math.log(1e-3), math.log(1e-1)
    return {
        'x_prompt': nrm(ks[0], (BATCH, SEQ, D_MODEL), f32),
        'x_sample': nrm(ks[1], (DEC_BATCH, DEC_SEQ, D_MODEL), f32),
        'state_ssm_re': 0.1 * nrm(ks[2], (DEPTH, DEC_BATCH, G, P), f32),
        'state_ssm_im': 0.1 * nrm(ks[3], (DEPTH, DEC_BATCH, G, P), f32),
        'cache_conv': nrm(ks[4], (DEPTH, DEC_BATCH, CONV_WIDTH - 1, D_CONV), f32),
        'norm_mix': 1.0 + 0.02 * nrm(ks[5], (DEPTH, D_MODEL), f32),
        'w_in': nrm(ks[6], (DEPTH, D_MODEL, D_IN), f32) * D_MODEL ** -0.5,
        'b_gate': 0.02 * nrm(ks[7], (DEPTH, N_BRANCH * D_MODEL), f32),
        'ssm_lambda_re': -0.5 + 0.01 * nrm(ks[8], (DEPTH, G, P), f32),
        'ssm_lambda_im': lam_im0 + 0.01 * nrm(ks[9], (DEPTH, G, P), f32),
        'ssm_log_step': jax.random.uniform(ks[10], (DEPTH, G), f32, log_lo, log_hi),
        'ssm_b_re': nrm(ks[11], (DEPTH, G, P, H), f32) * (2.0 * H) ** -0.5,
        'ssm_b_im': nrm(ks[12], (DEPTH, G, P, H), f32) * (2.0 * H) ** -0.5,
        'ssm_c_re': nrm(ks[13], (DEPTH, G, H, P), f32) * P ** -0.5,
        'ssm_c_im': nrm(ks[14], (DEPTH, G, H, P), f32) * P ** -0.5,
        'ssm_d': nrm(ks[15], (DEPTH, G, H), f32),
        'w_ssm_glu': nrm(ks[16], (DEPTH, D_SSM, 2 * D_MODEL), f32) * D_SSM ** -0.5,
        'conv_w': nrm(ks[17], (DEPTH, CONV_WIDTH, D_CONV), f32) * CONV_WIDTH ** -0.5,
        'conv_b': 0.02 * nrm(ks[18], (DEPTH, D_CONV), f32),
        'conv_ln_g': 1.0 + 0.02 * nrm(ks[19], (DEPTH, D_CONV), f32),
        'conv_ln_b': 0.02 * nrm(ks[20], (DEPTH, D_CONV), f32),
        'w_conv_out': nrm(ks[21], (DEPTH, D_CONV, D_MODEL), f32) * D_CONV ** -0.5,
        'w_out': nrm(ks[22], (DEPTH, D_MODEL, D_MODEL), f32) * D_MODEL ** -0.5,
        'norm_ffn': 1.0 + 0.02 * nrm(ks[23], (DEPTH, D_MODEL), f32),
        'peer_w_q': nrm(ks[24], (DEPTH, D_MODEL, PEER_HEADS * D_QUERY), f32) * D_MODEL ** -0.5,
        'peer_keys1': nrm(ks[25], (DEPTH, N_KEYS, D_QUERY // 2), f32) * (D_QUERY // 2) ** -0.5,
        'peer_keys2': nrm(ks[26], (DEPTH, N_KEYS, D_QUERY // 2), f32) * (D_QUERY // 2) ** -0.5,
        'peer_u': nrm(ks[27], (DEPTH, N_EXPERTS, D_MODEL), f32) * D_MODEL ** -0.5,
        'peer_v': nrm(ks[28], (DEPTH, N_EXPERTS, D_MODEL), f32) * PEER_HEADS ** -0.5,
        'norm_final': 1.0 + 0.02 * nrm(ks[29], (D_MODEL,), f32),
    }

def reference(x_prompt, x_sample, state_ssm_re, state_ssm_im, cache_conv, norm_mix, w_in, b_gate,
              ssm_lambda_re, ssm_lambda_im, ssm_log_step, ssm_b_re, ssm_b_im, ssm_c_re, ssm_c_im,
              ssm_d, w_ssm_glu, conv_w, conv_b, conv_ln_g, conv_ln_b, w_conv_out, w_out, norm_ffn,
              peer_w_q, peer_keys1, peer_keys2, peer_u, peer_v, norm_final):
    n_p = x_prompt.shape[0]
    zero_ssm = jnp.zeros((n_p, N_SSM_GROUPS, SSM_STATE), jnp.float32)
    zero_conv = jnp.zeros((n_p, CONV_WIDTH - 1, D_CONV), x_prompt.dtype)
    hp, hs = x_prompt, x_sample
    re_p, im_p, cv_p, re_s, im_s, cv_s = [], [], [], [], [], []
    for l in range(DEPTH):
        w = (norm_mix[l], w_in[l], b_gate[l], ssm_lambda_re[l], ssm_lambda_im[l], ssm_log_step[l],
             ssm_b_re[l], ssm_b_im[l], ssm_c_re[l], ssm_c_im[l], ssm_d[l], w_ssm_glu[l], conv_w[l],
             conv_b[l], conv_ln_g[l], conv_ln_b[l], w_conv_out[l], w_out[l], norm_ffn[l],
             peer_w_q[l], peer_keys1[l], peer_keys2[l], peer_u[l], peer_v[l])
        hp, r_p, i_p, c_p = _layer(hp, zero_ssm, zero_ssm, zero_conv, *w)
        hs, r_s, i_s, c_s = _layer(hs, state_ssm_re[l], state_ssm_im[l], cache_conv[l], *w)
        re_p.append(r_p); im_p.append(i_p); cv_p.append(c_p)
        re_s.append(r_s); im_s.append(i_s); cv_s.append(c_s)
    y_prompt = _rmsnorm(hp, norm_final)
    y_sample = _rmsnorm(hs, norm_final)
    return (y_prompt, y_sample, jnp.stack(re_p), jnp.stack(im_p), jnp.stack(cv_p),
            jnp.stack(re_s), jnp.stack(im_s), jnp.stack(cv_s))


_drawn_inputs = setup_inputs


def setup_inputs(seed=0):
    import zlib

    import numpy as np

    out = dict(_drawn_inputs(seed))
    spreads = {}
    factors = {'b_gate': 5.412,
     'ssm_lambda_re': 49.459,
     'conv_b': 2.689,
     'conv_ln_g': 3.287,
     'conv_ln_b': 3.709,
     'norm_final': 25.291,
     'ssm_c_re': 3.969,
     'ssm_c_im': 4.249,
     'norm_ffn': 3.441}
    for name, (base, spread) in spreads.items():
        noise = np.random.default_rng([zlib.crc32(name.encode()), seed]).standard_normal(out[name].shape)
        drawn = base * np.exp(spread * noise) if base else spread * noise
        out[name] = __import__('jax').numpy.asarray(drawn.astype(out[name].dtype))
    for name, factor in factors.items():
        out[name] = (out[name] * factor).astype(out[name].dtype)
    return out
```

```python
from contextlib import ExitStack

import concourse.bass as bass
from concourse import mybir

F32 = mybir.dt.float32
U32 = mybir.dt.uint32
ALU = mybir.AluOpType
ACT = mybir.ActivationFunctionType

P = 128
D = 1024
DT = D // P
SEQ, DEC = 1024, 64
GROUPS = 4
NP, NS = SEQ // GROUPS, DEC // GROUPS
N = NP + NS
DC = 512
CT = DC // P
PAIRS = 16
SG = 16
TAPS = 31
HALO = TAPS - 1
NV = HALO + NP + HALO + NS
NC = NV - HALO
SOFF = NP + HALO
HEADS, KEYS, TOPK = 8, 128, 16
EPS = 1e-6
NEG = -3.0e38

SLABS = 64
SLOTS = 8
S_CONV, S_GATE, S_GLU, S_COUT, S_OUT, S_Q = 4, 12, 28, 36, 40, 48

A_XN, A_U, A_CQ, A_GATE, A_GLU, A_OUT, A_XN2, A_Q = 0, 8, 12, 16, 32, 40, 48, 56
A_ALL = 88
A_BANKS = 2
V_CP, V_B, V_GLU, V_LN, V_COUT, V_TOK = 0, 4, 36, 44, 46, 54
V_ALL = 60
V_BANKS = 4
Y_BANKS = 2


def a_q(m):
    return A_Q if m == 0 else A_Q - 1 + 2 * m


def a_score(m):
    return A_Q + 2 + 2 * m if m < 15 else A_ALL - 1


_WIDTHS = [("lam_re", PAIRS), ("lam_im", PAIRS), ("log_step", PAIRS), ("h0_re", PAIRS), ("h0_im", PAIRS),
           ("b_re", PAIRS * SG), ("b_im", PAIRS * SG), ("c_re", PAIRS * SG), ("c_im", PAIRS * SG),
           ("d_skip", CT), ("norm_mix", DT), ("norm_ffn", DT), ("b_gate", 2 * DT), ("conv_w", CT * TAPS),
           ("conv_b", CT), ("ln_g", CT), ("ln_b", CT), ("cache", CT * HALO), ("eye", P), ("keys", 2 * KEYS)]
PACK = {}
_at = 0
for _name, _w in _WIDTHS:
    PACK[_name] = (_at, _w)
    _at += _w
PACK_W = _at


def mixing_block(nc, x_prompt, x_sample, packed, slabs, x2_d, xh_d, score_d, ssm_out, conv_out):
    with ExitStack() as ctx:
        def sb(name, shape, dt=F32):
            return ctx.enter_context(nc.sbuf_tensor(name, shape, dt))

        def sem(name):
            return ctx.enter_context(nc.semaphore(name))

        pk = sb("pk", [P, PACK_W])

        def par(name):
            a, w = PACK[name]
            return pk[:, a:a + w]

        ring = sb("ring", [P, SLOTS, D])
        xt = sb("xt", [P, 3, D])
        xh = sb("xh", [P, 3, D])
        xnT = sb("xnT", [P, DT, N])
        uT = sb("uT", [P, CT, N])
        vbuf = sb("vbuf", [P, CT, NV])
        tails = sb("tails", [P, CT, 2 * HALO])
        acc = sb("acc", [P, CT, NC])
        sq = sb("sq", [P, CT, NC])
        gates = sb("gates", [P, 2 * DT, N])
        outT = gates[:, 0:DT, :]
        cosT = sb("cosT", [P, PAIRS, N])
        sinT = sb("sinT", [P, PAIRS, N])
        rot = sb("rot", [P, 4, N])
        rin = sb("rin", [P, 2, N])
        grot = sb("grot", [P, 2, 2, N])
        prod = sb("prod", [P, 4, N])
        hst = sb("hst", [P, 2, 2, N])
        carry = sb("carry", [P, 2, PAIRS, 2])
        yT = sb("yT", [P, CT, N])
        cs = yT
        sig = sb("sig", [P, 2, NC])
        merged = sb("merged", [P, DT, N])
        qT = sb("qT", [P, 2, N])
        scsb = sb("scsb", [P, 2, 3, 2 * KEYS])
        rho = sb("rho", [P, PAIRS])
        bpad = sb("bpad", [P, 2, PAIRS, 2 * SG])
        bst = sb("bst", [P, 2, CT, P])
        cst = sb("cst", [P, 2, PAIRS, 2 * SG])
        mean_w = sb("mean_w", [P, P])
        ssq = sb("ssq", [P, 3])
        rstd = sb("rstd", [P, 3])
        half = sb("half", [P, 1])
        lnr = sb("lnr", [P, 2, NC])
        sm = sb("sm", [P, 13, PAIRS])

        ps_a = ctx.enter_context(nc.psum_tensor("ps_a", [P, A_BANKS, 512], F32))
        ps_v = ctx.enter_context(nc.psum_tensor("ps_v", [P, V_BANKS, 512], F32))
        ps_y = ctx.enter_context(nc.psum_tensor("ps_y", [P, Y_BANKS, 512], F32))

        packed_in = sem("packed_in")
        slab_in = [sem(f"slab_in{i}") for i in range(SLOTS)]
        x_in = sem("x_in")
        a_ready = sem("a_ready")
        a_done = sem("a_done")
        v_ready = sem("v_ready")
        v_done = sem("v_done")
        c_done = sem("c_done")
        y_summed = sem("y_summed")
        merged_done = sem("merged_done")
        y_gelu = sem("y_gelu")
        setup_v = sem("setup_v")
        setup_a = sem("setup_a")
        setup_t = sem("setup_t")
        setup_done = sem("setup_done")
        sq_x = sem("sq_x")
        ms_x = sem("ms_x")
        rs_x = sem("rs_x")
        xh_ready = sem("xh_ready")
        scanned = sem("scanned")
        unrotated = sem("unrotated")
        conv_ready = sem("conv_ready")
        xc_sq = sem("xc_sq")
        std_ready = sem("std_ready")
        ln_ready = sem("ln_ready")
        ln_sig = sem("ln_sig")
        cs_ready = sem("cs_ready")
        rows_out = sem("rows_out")
        score_out = [sem(f"score_out{i}") for i in range(2)]
        v_chain = sem("v_chain")
        p_chain = sem("p_chain")
        state_out = sem("state_out")
        block = ctx.enter_context(nc.Block())

        SEGS = ((0, NP), (NP, N))
        xp_rows = x_prompt.rearrange("b (g t p) d -> (b g) p t d", g=GROUPS, p=P)
        xs_rows = x_sample.rearrange("b (g p) d -> (b g) p d", g=GROUPS)
        x2_rows = x2_d[0:SEQ, :].rearrange("(g t p) d -> g p t d", g=GROUPS, p=P)
        xh_rows = xh_d[0:SEQ, :].rearrange("(g t p) d -> g p t d", g=GROUPS, p=P)
        x2_srows = x2_d[SEQ:SEQ + DEC, :].rearrange("(g p) d -> g p d", g=GROUPS)
        xh_srows = xh_d[SEQ:SEQ + DEC, :].rearrange("(g p) d -> g p d", g=GROUPS)
        sc_rows = score_d[0:8 * HEADS].rearrange("(g t h) p c -> g h p t c", g=GROUPS, h=HEADS)
        sc_srows = score_d[8 * HEADS:8 * HEADS + 4].rearrange("k (f g p) c -> g f k p c", f=2, g=GROUPS)


        def slab_through(eng, s, g):
            if s < S_CONV:
                eng.wait_ge(a_ready, A_ALL * g + A_U + s + 1)
            elif s < S_GATE:
                j, second = divmod(s - S_CONV, 2)
                if second:
                    eng.wait_ge(v_ready, V_ALL * g + V_CP + j + 1)
                else:
                    eng.wait_ge(a_ready, A_ALL * g + A_CQ + j + 1)
            elif s < S_GLU:
                eng.wait_ge(a_ready, A_ALL * g + A_GATE + s - S_GATE + 1)
            elif s < S_COUT:
                eng.wait_ge(v_ready, V_ALL * g + V_GLU + s - S_GLU + 1)
            elif s < S_OUT:
                eng.wait_ge(v_ready, V_ALL * g + V_COUT + 2 * (s - S_COUT) + 2)
            elif s < S_Q:
                eng.wait_ge(a_ready, A_ALL * g + A_OUT + s - S_OUT + 1)
            else:
                eng.wait_ge(a_ready, A_ALL * g + a_q(s - S_Q) + 1)

        @block.sync
        def _(sp):
            sp.dma_start(pk[:, :], packed).then_inc(packed_in, 16)
            sp.dma_start(xt[:, 0:2, :], xp_rows[0]).then_inc(x_in, 16)
            sp.dma_start(xt[0:NS, 2, :], xs_rows[0]).then_inc(x_in, 16)
            for s in range(SLOTS):
                sp.dma_start(ring[:, s, :], slabs[s]).then_inc(slab_in[s], 16)
            with sp.Fori(0, GROUPS) as g:
                for s in range(SLABS):
                    slab_through(sp, s, g)
                    sp.dma_start(ring[:, s % SLOTS, :], slabs[(s + SLOTS) % SLABS]).then_inc(slab_in[s % SLOTS], 16)
                    if s == S_Q + 7:
                        sp.wait_ge(rows_out, 64 * (g + 1))
                        sp.dma_start(xt[:, 0:2, :], xp_rows[(g + 1) % GROUPS]).then_inc(x_in, 16)
                        sp.dma_start(xt[0:NS, 2, :], xs_rows[(g + 1) % GROUPS]).then_inc(x_in, 16)
            sp.wait_ge(unrotated, PAIRS * (GROUPS + 1))
            sp.dma_start(ssm_out, carry[:, :, :, :].rearrange("p a b c -> p (a b c)")).then_inc(state_out, 16)
            sp.wait_ge(conv_ready, GROUPS)
            sp.dma_start(conv_out, tails[:, :, :].rearrange("p a b -> p (a b)")).then_inc(state_out, 16)
            sp.wait_ge(state_out, 32)
            for i in range(2):
                sp.wait_ge(score_out[i], 32 * 4 * GROUPS)
            for i in range(SLOTS):
                sp.wait_ge(slab_in[i], 16 * (1 + GROUPS * SLABS // SLOTS))
            sp.wait_ge(x_in, 32 * (1 + GROUPS))

        @block.tensor
        def _(pe):
            eye = par("eye")
            pe.wait_ge(packed_in, 16)
            pe.wait_ge(setup_v, 3)
            for c in range(2):
                for t in range(CT):
                    last = pe.transpose(ps_v[:, c, t * P:(t + 1) * P],
                                        bpad[:, c, 4 * t:4 * t + 4, :].rearrange("p a b -> p (a b)"), eye)
            last.then_inc(setup_t, 1)
            pe.wait_ge(setup_done, 1)

            with pe.Fori(0, GROUPS) as g:
                def a_tile(n):
                    pe.wait_ge(a_done, A_ALL * g + n + 1)
                    return ps_a[:, n % A_BANKS, :]

                def a_emptied(n):
                    pe.wait_ge(a_done, A_ALL * g + n + 1 + A_BANKS)

                def v_tile(n):
                    pe.wait_ge(v_done, V_ALL * g + n + 1)
                    return ps_v[:, n % V_BANKS, :]

                def slab(s):
                    pe.wait_ge(slab_in[s % SLOTS], 16 * ((SLABS // SLOTS) * g + s // SLOTS + 1))

                def product(out, s, k0, rhs):
                    kt = rhs.shape[1]
                    for k in range(kt):
                        w = ring[:, s % SLOTS, (k0 + k) * P:(k0 + k + 1) * P]
                        last = pe.matmul(out[:, 0:N], w, rhs[:, k, :], start=(k == 0), stop=(k == kt - 1))
                    return last

                def to_channels(n0, turn):
                    pe.wait_ge(xh_ready, 2 * g + turn)
                    for k in range(DT):
                        out = a_tile(n0 + k)
                        for t in range(2):
                            pe.transpose(out[:, t * P:(t + 1) * P], xh[:, t, k * P:(k + 1) * P], eye)
                        pe.transpose(out[:, NP:N], xh[0:NS, 2, k * P:(k + 1) * P],
                                     eye[0:NS, 0:NS]).then_inc(a_ready, 1)
                    a_emptied(n0 + DT - 1)

                to_channels(A_XN, 1)
                for m in range(CT):
                    out = a_tile(A_U + m)
                    slab(m)
                    product(out, m, 0, xnT[:, :, :]).then_inc(a_ready, 1)
                for j in range(CT):
                    out = a_tile(A_CQ + j)
                    slab(S_CONV + 2 * j)
                    product(out, S_CONV + 2 * j, 0, xnT[:, :, :]).then_inc(a_ready, 1)
                    out = v_tile(V_CP + j)
                    slab(S_CONV + 2 * j + 1)
                    product(out, S_CONV + 2 * j + 1, 0, xnT[:, :, :]).then_inc(v_ready, 1)

                def b_product(j):
                    q, t = 32 * (j % 4), j // 4
                    if j == 0:
                        a_emptied(A_U + CT - 1)
                    for c in range(2):
                        out = v_tile(V_B + 2 * j + c)
                        pe.matmul(out[:, 0:N], bst[q:q + 32, c, t, :], uT[q:q + 32, t, :],
                                  start=True, stop=True).then_inc(v_ready, 1)

                def c_product(j):
                    q, t = 32 * (j % 4), j // 4
                    if j % 4 == 0 and j >= 8:
                        pe.wait_ge(y_summed, CT * g + t - 1)
                    pe.wait_ge(unrotated, PAIRS * g + PAIRS + j + 1)
                    for c in range(2):
                        last = pe.matmul(ps_y[q:q + 32, t % Y_BANKS, 0:N], cst[:, c, j, :], hst[:, j % 2, c, :],
                                         start=(c == 0), stop=(c == 1))
                    last.then_inc(c_done, 1)

                for j in range(PAIRS):
                    b_product(j)
                    out = a_tile(A_GATE + j)
                    slab(S_GATE + j)
                    product(out, S_GATE + j, 0, xnT[:, :, :]).then_inc(a_ready, 1)
                    if j >= 2:
                        c_product(j - 2)
                c_product(PAIRS - 2)
                c_product(PAIRS - 1)

                pe.wait_ge(y_gelu, CT * (g + 1))
                for j in range(DT):
                    out = a_tile(A_GLU + j)
                    slab(S_GLU + j)
                    product(out, S_GLU + j, 0, yT[:, :, :]).then_inc(a_ready, 1)
                    out = v_tile(V_GLU + j)
                    product(out, S_GLU + j, CT, yT[:, :, :]).then_inc(v_ready, 1)

                def channel_mean(n, src):
                    out = v_tile(n)
                    for c in range(CT):
                        last = pe.matmul(out[:, 0:NC], mean_w[:, :], src[:, c, :], start=(c == 0), stop=(c == CT - 1))
                    last.then_inc(v_ready, 1)

                pe.wait_ge(conv_ready, g + 1)
                channel_mean(V_LN, acc)
                pe.wait_ge(xc_sq, g + 1)
                channel_mean(V_LN + 1, sq)

                pe.wait_ge(cs_ready, CT * (g + 1))
                for j in range(DT):
                    out = v_tile(V_COUT + j)
                    if j % 2 == 0:
                        slab(S_COUT + j // 2)
                    product(out, S_COUT + j // 2, CT * (j % 2), cs[:, :, :]).then_inc(v_ready, 1)

                pe.wait_ge(merged_done, DT * (g + 1))
                for j in range(DT):
                    out = a_tile(A_OUT + j)
                    slab(S_OUT + j)
                    product(out, S_OUT + j, 0, merged[:, :, :]).then_inc(a_ready, 1)
                a_emptied(A_OUT + DT - 1)
                for t, (n, width) in enumerate(((0, P), (P, P), (NP, NS))):
                    for h in range(2):
                        out = v_tile(V_TOK + 2 * t + h)
                        for m in range(4):
                            last = pe.transpose(out[0:width, m * P:(m + 1) * P], outT[:, 4 * h + m, n:n + width], eye)
                        last.then_inc(v_ready, 1)

                to_channels(A_XN2, 2)

                def scores(m):
                    out = a_tile(a_score(m))
                    a_emptied(a_q(m))
                    keys = par("keys")[:, (m % 2) * KEYS:(m % 2 + 1) * KEYS]
                    for t, (n, width) in enumerate(((0, P), (P, P), (NP, NS))):
                        last = pe.matmul(out[0:width, t * KEYS:(t + 1) * KEYS], qT[:, m % 2, n:n + width], keys,
                                         start=True, stop=True)
                    last.then_inc(a_ready, 1)

                for m in range(2 * HEADS):
                    out = a_tile(a_q(m))
                    slab(S_Q + m)
                    product(out, S_Q + m, 0, xnT[:, :, :]).then_inc(a_ready, 1)
                    if m:
                        scores(m - 1)
                scores(2 * HEADS - 1)

        @block.scalar
        def _(act):
            act.wait_ge(packed_in, 16)
            act.activation(sm[:, 0, :], par("log_step"), ACT.Exp).then_inc(setup_a, 1)
            act.wait_ge(setup_v, 1)
            act.activation(rho[:, :], sm[:, 4, :], ACT.Exp).then_inc(setup_a, 1)
            act.wait_ge(setup_v, 2)
            act.activation(sm[:, 6, :], sm[:, 3, :], ACT.Sin).then_inc(setup_a, 1)
            act.activation(sm[:, 7, :], sm[:, 5, :], ACT.Sin).then_inc(setup_a, 1)
            act.wait_ge(setup_done, 1)
            act.sem_inc(a_done, A_BANKS)

            with act.Fori(0, GROUPS) as g:
                def ready(n):
                    act.wait_ge(a_ready, A_ALL * g + n + 1)
                    return ps_a[:, n % A_BANKS, :]

                def squares():
                    flat = merged[:, :, :].rearrange("p a b -> p (a b)")
                    spare = sq[:, :, :].rearrange("p a b -> p (a b)")
                    act.activation(flat[:, 0:D], xt[:, 0, :], ACT.Square, accum_out=ssq[:, 0:1])
                    act.activation(flat[:, D:2 * D], xt[:, 1, :], ACT.Square, accum_out=ssq[:, 1:2])
                    act.activation(spare[0:NS, 0:D], xt[0:NS, 2, :], ACT.Square,
                                   accum_out=ssq[0:NS, 2:3]).then_inc(sq_x, 1)

                act.wait_ge(x_in, 32 * (g + 1))
                squares()
                for k in range(DT):
                    act.activation(xnT[:, k, :], ready(A_XN + k)[:, 0:N], ACT.Copy,
                                   scale=par("norm_mix")[:, k:k + 1]).then_inc(a_done, 1)
                for m in range(CT):
                    act.activation(uT[:, m, :], ready(A_U + m)[:, 0:N], ACT.Copy).then_inc(a_done, 1)
                for j in range(CT):
                    if j >= 2:
                        act.wait_ge(v_done, V_ALL * g + V_BANKS + V_CP + j - 1)
                    act.activation(sig[:, j % 2, 0:N], ready(A_CQ + j)[:, 0:N], ACT.Sigmoid).then_inc(a_done, 1)
                for m in range(2 * DT):
                    act.activation(gates[:, m, :], ready(A_GATE + m)[:, 0:N], ACT.Sigmoid,
                                   bias=par("b_gate")[:, m:m + 1]).then_inc(a_done, 1)
                for t in range(CT):
                    act.wait_ge(y_summed, CT * g + t + 1)
                    act.activation(yT[:, t, :], yT[:, t, :], ACT.Gelu).then_inc(y_gelu, 1)
                for j in range(DT):
                    if j >= 2:
                        act.wait_ge(v_done, V_ALL * g + V_BANKS + V_GLU + j - 1)
                    act.activation(sig[:, j % 2, 0:N], ready(A_GLU + j)[:, 0:N], ACT.Sigmoid).then_inc(a_done, 1)
                act.wait_ge(v_done, V_ALL * g + V_BANKS + V_LN + 1)
                act.activation(sq[:, :, :], acc[:, :, :], ACT.Square).then_inc(xc_sq, 1)
                act.wait_ge(v_done, V_ALL * g + V_BANKS + V_LN + 2)
                act.activation(lnr[:, 1, :], lnr[:, 0, :], ACT.Sqrt).then_inc(std_ready, 1)
                act.wait_ge(ln_ready, g + 1)
                for c in range(CT):
                    act.activation(sq[:, c, :], acc[:, c, :], ACT.Sigmoid, bias=par("ln_b")[:, c:c + 1],
                                   scale=par("ln_g")[:, c:c + 1]).then_inc(ln_sig, 1)
                for j in range(DT):
                    act.activation(outT[:, j, :], ready(A_OUT + j)[:, 0:N], ACT.Copy).then_inc(a_done, 1)
                act.wait_ge(v_done, V_ALL * g + V_BANKS + V_ALL)
                squares()
                for k in range(DT):
                    act.activation(xnT[:, k, :], ready(A_XN2 + k)[:, 0:N], ACT.Copy,
                                   scale=par("norm_ffn")[:, k:k + 1]).then_inc(a_done, 1)
                act.wait_ge(xh_ready, 2 * g + 2)
                act.dma_start(x2_rows[g], xt[:, 0:2, :]).then_inc(rows_out, 16)
                act.dma_start(x2_srows[g], xt[0:NS, 2, :]).then_inc(rows_out, 16)
                act.dma_start(xh_rows[g], xh[:, 0:2, :]).then_inc(rows_out, 16)
                act.dma_start(xh_srows[g], xh[0:NS, 2, :]).then_inc(rows_out, 16)

                def keep_scores(m):
                    h, b = m // 2, (m // 2) % 2
                    cols = slice((m % 2) * KEYS, (m % 2 + 1) * KEYS)
                    if m % 2 == 0 and h >= 2:
                        act.wait_ge(score_out[b], 128 * g + 32 * (h // 2))
                    src = ready(a_score(m))
                    act.activation(scsb[:, b, 0:2, cols], src[:, 0:2 * KEYS].rearrange("p (t c) -> p t c", t=2), ACT.Copy)
                    act.activation(scsb[0:NS, b, 2, cols], src[0:NS, 2 * KEYS:3 * KEYS], ACT.Copy).then_inc(a_done, 1)
                    if m % 2:
                        act.wait_ge(a_done, A_ALL * g + A_BANKS + a_score(m) + 1)
                        act.dma_start(sc_rows[g, h], scsb[:, b, 0:2, :]).then_inc(score_out[b], 16)
                        act.dma_start(sc_srows[g, h // 4, h % 4], scsb[0:NS, b, 2, :]).then_inc(score_out[b], 16)

                for m in range(2 * HEADS):
                    act.activation(qT[:, m % 2, :], ready(a_q(m))[:, 0:N], ACT.Copy).then_inc(a_done, 1)
                    if m:
                        keep_scores(m - 1)
                keep_scores(2 * HEADS - 1)
                for b in range(2):
                    act.wait_ge(score_out[b], 128 * g + 128)

        @block.vector
        def _(dve):
            count = [0]

            def step(ins):
                count[0] += 1
                ins.then_inc(v_chain, 1)
                dve.wait_ge(v_chain, count[0])

            def mark(ins):
                count[0] += 1
                ins.then_inc(v_chain, 1)
                return count[0]

            def after(n):
                dve.wait_ge(v_chain, n)

            dve.memset(mean_w[:, :], 1.0 / DC)
            dve.memset(bpad[:, :, :, :], 0.0)
            dve.memset(cst[:, :, :, :], 0.0)
            dve.memset(carry[:, :, :, :], 0.0)
            dve.memset(ssq[:, :], float(D))
            dve.memset(half[:, :], -0.5)
            step(dve.memset(tails[:, :, 0:HALO], 0.0))
            dve.wait_ge(packed_in, 16)
            dve.tensor_copy(tails[:, :, HALO:2 * HALO], par("cache").rearrange("p (c k) -> p c k", c=CT))
            dve.tensor_copy(carry[:, 0, :, 1], par("h0_re"))
            dve.tensor_copy(carry[:, 1, :, 1], par("h0_im"))
            lr, li = par("lam_re"), par("lam_im")
            dve.wait_ge(setup_a, 1)
            dve.tensor_tensor(sm[:, 1, :], li, sm[:, 0, :], ALU.mult)
            dve.tensor_tensor(sm[:, 4, :], lr, sm[:, 0, :], ALU.mult).then_inc(setup_v, 1)
            dve.wait_ge(setup_v, 1)
            magic = float(3 * 2 ** 22)
            step(dve.tensor_scalar(sm[:, 2, :], sm[:, 1, :], 0.15915494309189535, magic, ALU.mult, ALU.add))
            step(dve.tensor_scalar(sm[:, 2, :], sm[:, 2, :], magic, None, ALU.subtract))
            step(dve.scalar_tensor_tensor(sm[:, 3, :], sm[:, 2, :], -6.28125, sm[:, 1, :], ALU.mult, ALU.add))
            step(dve.scalar_tensor_tensor(sm[:, 3, :], sm[:, 2, :], -0.0019353071795864769, sm[:, 3, :],
                                          ALU.mult, ALU.add))
            step(dve.tensor_scalar(sm[:, 3, :], sm[:, 3, :], 3.1415925, -3.1415925, ALU.min, ALU.max))
            step(dve.tensor_scalar(sm[:, 5, :], sm[:, 3, :], -1.0, None, ALU.mult))
            step(dve.tensor_tensor(sm[:, 5, :], sm[:, 5, :], sm[:, 3, :], ALU.min))
            dve.tensor_scalar(sm[:, 5, :], sm[:, 5, :], 1.5707963267948966, None, ALU.add).then_inc(setup_v, 1)
            dve.wait_ge(setup_a, 4)
            sin, cos = sm[:, 6, :], sm[:, 7, :]
            dve.tensor_copy(cosT[:, :, 0], cos)
            dve.tensor_copy(sinT[:, :, 0], sin)
            step(dve.tensor_tensor(sm[:, 0, :], rho[:, :], cos, ALU.mult))
            dve.tensor_scalar(sm[:, 0, :], sm[:, 0, :], -1.0, None, ALU.add)
            dve.tensor_tensor(sm[:, 1, :], rho[:, :], sin, ALU.mult)
            dve.tensor_tensor(sm[:, 2, :], lr, lr, ALU.mult)
            step(dve.tensor_tensor(sm[:, 3, :], li, li, ALU.mult))
            step(dve.tensor_tensor(sm[:, 2, :], sm[:, 2, :], sm[:, 3, :], ALU.add))
            step(dve.reciprocal(sm[:, 8, :], sm[:, 2, :]))
            dve.tensor_tensor(sm[:, 2, :], sm[:, 0, :], lr, ALU.mult)
            dve.tensor_tensor(sm[:, 3, :], sm[:, 1, :], li, ALU.mult)
            dve.tensor_tensor(sm[:, 9, :], sm[:, 1, :], lr, ALU.mult)
            step(dve.tensor_tensor(sm[:, 10, :], sm[:, 0, :], li, ALU.mult))
            dve.tensor_tensor(sm[:, 2, :], sm[:, 2, :], sm[:, 3, :], ALU.add)
            step(dve.tensor_tensor(sm[:, 9, :], sm[:, 9, :], sm[:, 10, :], ALU.subtract))
            dve.tensor_tensor(sm[:, 11, :], sm[:, 2, :], sm[:, 8, :], ALU.mult)
            step(dve.tensor_tensor(sm[:, 12, :], sm[:, 9, :], sm[:, 8, :], ALU.mult))
            for half_pair in range(2):
                rows = slice(64 * half_pair, 64 * half_pair + 64)
                cols = slice(SG * half_pair, SG * half_pair + SG)

                def v3(name):
                    return par(name)[rows].rearrange("p (j h) -> p j h", j=PAIRS)

                def bc(n):
                    return sm[rows, n, :].unsqueeze(2).to_broadcast([64, PAIRS, SG])

                tmp = [rot[rows, n, 0:PAIRS * SG].rearrange("p (j h) -> p j h", j=PAIRS) for n in range(4)]
                dve.tensor_tensor(tmp[0], v3("b_re"), bc(11), ALU.mult)
                dve.tensor_tensor(tmp[1], v3("b_im"), bc(12), ALU.mult)
                dve.tensor_tensor(tmp[2], v3("b_im"), bc(11), ALU.mult)
                step(dve.tensor_tensor(tmp[3], v3("b_re"), bc(12), ALU.mult))
                dve.tensor_tensor(bpad[rows, 0, :, cols], tmp[0], tmp[1], ALU.subtract)
                step(dve.tensor_tensor(bpad[rows, 1, :, cols], tmp[2], tmp[3], ALU.add))
                dve.tensor_copy(cst[rows, 0, :, cols], v3("c_re"))
                step(dve.tensor_scalar(cst[rows, 1, :, cols], v3("c_im"), -1.0, None, ALU.mult))
            dve.sem_inc(setup_v, 1)
            scratch = gates[:, :, :].rearrange("p a b -> p (a b)")
            w = 1
            while w < NP:
                t0 = scratch[:, 0:PAIRS * w].rearrange("p (j n) -> p j n", j=PAIRS)
                t1 = scratch[:, PAIRS * w:2 * PAIRS * w].rearrange("p (j n) -> p j n", j=PAIRS)
                cw = cosT[:, :, w - 1:w].to_broadcast([P, PAIRS, w])
                sw = sinT[:, :, w - 1:w].to_broadcast([P, PAIRS, w])
                dve.tensor_tensor(t0, cosT[:, :, 0:w], cw, ALU.mult)
                step(dve.tensor_tensor(t1, sinT[:, :, 0:w], sw, ALU.mult))
                step(dve.tensor_tensor(cosT[:, :, w:2 * w], t0, t1, ALU.subtract))
                dve.tensor_tensor(t0, sinT[:, :, 0:w], cw, ALU.mult)
                step(dve.tensor_tensor(t1, cosT[:, :, 0:w], sw, ALU.mult))
                step(dve.tensor_tensor(sinT[:, :, w:2 * w], t0, t1, ALU.add))
                w *= 2
            dve.tensor_copy(cosT[:, :, NP:N], cosT[:, :, 0:NS])
            dve.tensor_copy(sinT[:, :, NP:N], sinT[:, :, 0:NS])
            dve.wait_ge(setup_t, 1)
            step(dve.tensor_copy(bst[:, :, :, :].rearrange("p c t q -> p c (t q)"), ps_v[:, 0:2, :]))
            dve.sem_inc(v_done, V_BANKS)
            dve.sem_inc(setup_done, 1)

            with dve.Fori(0, GROUPS) as g:
                dve.sem_clear(v_chain)
                count[0] = 0

                def ready(n):
                    dve.wait_ge(v_ready, V_ALL * g + n + 1)
                    return ps_v[:, n % V_BANKS, :]

                def emptied(n):
                    dve.wait_ge(v_done, V_ALL * g + V_BANKS + n + 1)

                def normalise(turn):
                    dve.wait_ge(sq_x, 2 * g + turn)
                    dve.tensor_scalar(rstd[:, :], ssq[:, :], 1.0 / D, EPS, ALU.mult, ALU.add).then_inc(ms_x, 1)
                    dve.wait_ge(rs_x, 2 * g + turn)
                    for t, w in ((0, P), (1, P), (2, NS)):
                        last = dve.tensor_scalar(xh[0:w, t, :], xt[0:w, t, :], rstd[0:w, t:t + 1], None, ALU.mult)
                    last.then_inc(xh_ready, 1)

                normalise(1)
                dve.tensor_copy(vbuf[:, :, 0:HALO], tails[:, :, 0:HALO])
                step(dve.tensor_copy(vbuf[:, :, SOFF:SOFF + HALO], tails[:, :, HALO:2 * HALO]))
                for j in range(CT):
                    dve.wait_ge(a_done, A_ALL * g + A_BANKS + A_CQ + j + 1)
                    src = ready(V_CP + j)
                    dve.tensor_tensor(vbuf[:, j, HALO:HALO + NP], src[:, 0:NP], sig[:, j % 2, 0:NP], ALU.mult)
                    dve.tensor_tensor(vbuf[:, j, SOFF + HALO:NV], src[:, NP:N], sig[:, j % 2, NP:N],
                                      ALU.mult).then_inc(v_done, 1)
                emptied(V_CP + CT - 1)
                dve.tensor_copy(tails[:, :, 0:HALO], vbuf[:, :, NP:NP + HALO])
                step(dve.tensor_copy(tails[:, :, HALO:2 * HALO], vbuf[:, :, NV - HALO:NV]))

                def scan(j):
                    re, im = ready(V_B + 2 * j + 1 - 1), ready(V_B + 2 * j + 1)
                    c, s = cosT[:, j, :], sinT[:, j, :]
                    dve.tensor_tensor(rot[:, 0, :], re[:, 0:N], c, ALU.mult)
                    dve.tensor_tensor(rot[:, 1, :], im[:, 0:N], s, ALU.mult)
                    dve.tensor_tensor(rot[:, 2, :], im[:, 0:N], c, ALU.mult)
                    dve.tensor_tensor(rot[:, 3, :], re[:, 0:N], s, ALU.mult).then_inc(v_done, 2)
                    emptied(V_B + 2 * j + 1)
                    a = mark(dve.tensor_tensor(rin[:, 0, :], rot[:, 0, :], rot[:, 1, :], ALU.add))
                    b = mark(dve.tensor_tensor(rin[:, 1, :], rot[:, 2, :], rot[:, 3, :], ALU.subtract))
                    dve.wait_ge(unrotated, PAIRS * g + PAIRS + j - 1)
                    for part, n in ((0, a), (1, b)):
                        after(n)
                        for stream, (lo, hi) in enumerate(SEGS):
                            last = dve.tensor_tensor_scan(
                                grot[:, j % 2, part, lo:hi], rho[:, j:j + 1].to_broadcast([P, hi - lo]),
                                rin[:, part, lo:hi], carry[:, part, j, stream:stream + 1], ALU.mult, ALU.add)
                    last.then_inc(scanned, 1)

                def skip(t):
                    dve.wait_ge(c_done, PAIRS * g + 2 + 4 * t + 4)
                    dve.scalar_tensor_tensor(yT[:, t, :], uT[:, t, :], par("d_skip")[:, t:t + 1],
                                             ps_y[:, t % Y_BANKS, 0:N], ALU.mult, ALU.add).then_inc(y_summed, 1)

                for j in range(PAIRS):
                    scan(j)
                    if j >= 6 and j % 4 == 2:
                        skip((j - 6) // 4)
                skip(CT - 1)

                def glu(j):
                    dve.wait_ge(a_done, A_ALL * g + A_BANKS + A_GLU + j + 1)
                    src = ready(V_GLU + j)
                    dve.tensor_tensor(rot[:, j % 4, :], src[:, 0:N], sig[:, j % 2, 0:N], ALU.mult).then_inc(v_done, 1)
                    emptied(V_GLU + j)
                    mark(dve.tensor_tensor(merged[:, j, :], rot[:, j % 4, :], gates[:, j, :], ALU.mult))

                taps = par("conv_w")
                before = [0] * CT
                for k in range(TAPS):
                    for c in range(CT):
                        src, wk = vbuf[:, c, k:k + NC], taps[:, c * TAPS + k:c * TAPS + k + 1]
                        if k == 0:
                            before[c] = mark(dve.tensor_scalar(acc[:, c, :], src, wk, par("conv_b")[:, c:c + 1],
                                                               ALU.mult, ALU.add))
                        elif k < TAPS - 1:
                            after(before[c])
                            before[c] = mark(dve.scalar_tensor_tensor(acc[:, c, :], src, wk, acc[:, c, :],
                                                                      ALU.mult, ALU.add))
                        else:
                            after(before[c])
                            last = dve.scalar_tensor_tensor(acc[:, c, :], src, wk, acc[:, c, :], ALU.mult, ALU.add)
                    if k % 3 == 2 and k // 3 < DT:
                        glu(k // 3)
                last.then_inc(conv_ready, 1)
                dve.wait_ge(conv_ready, g + 1)

                src = ready(V_LN)
                for c in range(CT):
                    last = dve.tensor_tensor(acc[:, c, :], acc[:, c, :], src[:, 0:NC], ALU.subtract)
                last.then_inc(v_done, 1)
                src = ready(V_LN + 1)
                dve.tensor_scalar(lnr[:, 0, :], src[:, 0:NC], EPS, None, ALU.add).then_inc(v_done, 1)
                dve.wait_ge(std_ready, g + 1)
                step(dve.reciprocal(lnr[:, 0, :], lnr[:, 1, :]))
                for c in range(CT):
                    last = dve.tensor_tensor(acc[:, c, :], acc[:, c, :], lnr[:, 0, :], ALU.mult)
                last.then_inc(ln_ready, 1)
                dve.wait_ge(ln_ready, g + 1)
                for c in range(CT):
                    dve.wait_ge(ln_sig, CT * g + c + 1)
                    step(dve.tensor_scalar(acc[:, c, :], acc[:, c, :], par("ln_g")[:, c:c + 1],
                                           par("ln_b")[:, c:c + 1], ALU.mult, ALU.add))
                    dve.tensor_tensor(cs[:, c, 0:NP], acc[:, c, 0:NP], sq[:, c, 0:NP], ALU.mult)
                    dve.tensor_tensor(cs[:, c, NP:N], acc[:, c, SOFF:NC], sq[:, c, SOFF:NC],
                                      ALU.mult).then_inc(cs_ready, 1)
                for j in range(DT):
                    src = ready(V_COUT + j)
                    dve.tensor_tensor(rot[:, j % 4, :], src[:, 0:N], gates[:, DT + j, :], ALU.mult).then_inc(v_done, 1)
                    emptied(V_COUT + j)
                    dve.tensor_tensor(merged[:, j, :], merged[:, j, :], rot[:, j % 4, :], ALU.add).then_inc(merged_done, 1)
                for t, w in ((0, P), (1, P), (2, NS)):
                    ready(V_TOK + 2 * t + 1)
                    b = (V_TOK + 2 * t) % V_BANKS
                    rows = xt[0:w, t, :].rearrange("p (a b) -> p a b", a=2)
                    dve.tensor_tensor(rows, rows, ps_v[0:w, b:b + 2, :], ALU.add).then_inc(v_done, 2)
                normalise(2)

        @block.gpsimd
        def _(pool):
            pool.wait_ge(setup_done, 1)
            pool.sem_inc(unrotated, PAIRS)
            pool.sem_inc(c_done, 2)
            with pool.Fori(0, GROUPS) as g:
                pool.sem_clear(p_chain)
                count = [0]

                def after_all():
                    pool.wait_ge(p_chain, count[0])

                def mark(ins):
                    count[0] += 1
                    ins.then_inc(p_chain, 1)
                    return count[0]

                def inverse_root(turn):
                    pool.wait_ge(ms_x, 2 * g + turn)
                    pool.tensor_tensor(rstd[:, :], rstd[:, :], half[:, 0:1].to_broadcast([P, 3]),
                                       ALU.pow).then_inc(rs_x, 1)

                inverse_root(1)
                for j in range(PAIRS):
                    pool.wait_ge(scanned, PAIRS * g + j + 1)
                    c, s, b = cosT[:, j, :], sinT[:, j, :], j % 2
                    mark(pool.tensor_tensor(prod[:, 0, :], grot[:, b, 0, :], c, ALU.mult))
                    mark(pool.tensor_tensor(prod[:, 1, :], grot[:, b, 1, :], s, ALU.mult))
                    re = count[0]
                    mark(pool.tensor_tensor(prod[:, 2, :], grot[:, b, 0, :], s, ALU.mult))
                    mark(pool.tensor_tensor(prod[:, 3, :], grot[:, b, 1, :], c, ALU.mult))
                    im = count[0]
                    pool.wait_ge(c_done, PAIRS * g + j + 1)
                    pool.wait_ge(p_chain, re)
                    mark(pool.tensor_tensor(hst[:, b, 0, :], prod[:, 0, :], prod[:, 1, :], ALU.subtract))
                    pool.wait_ge(p_chain, im)
                    mark(pool.tensor_tensor(hst[:, b, 1, :], prod[:, 2, :], prod[:, 3, :], ALU.add))
                    after_all()
                    pool.tensor_copy(carry[:, :, j, :], hst[:, b, :, NP - 1:N:NS]).then_inc(unrotated, 1)
                inverse_root(2)


def _lay_out(inputs):
    import numpy as np

    def a(name):
        return np.asarray(inputs[name])

    def state_major(x):
        return x.reshape(PAIRS, P).T

    def channel_major(x):
        return x.reshape(-1, P).T

    def tiles(w):
        k, m = w.shape
        return w.reshape(k // P, P, m // P, P).transpose(2, 1, 0, 3)

    parts = {
        "lam_re": state_major(a("ssm_lambda_re")), "lam_im": state_major(a("ssm_lambda_im")),
        "log_step": state_major(np.repeat(a("ssm_log_step").reshape(-1), 64)),
        "h0_re": state_major(a("state_ssm_re")), "h0_im": state_major(a("state_ssm_im")),
        "b_re": a("ssm_b_re").reshape(PAIRS, P, SG).transpose(1, 0, 2).reshape(P, -1),
        "b_im": a("ssm_b_im").reshape(PAIRS, P, SG).transpose(1, 0, 2).reshape(P, -1),
        "c_re": a("ssm_c_re").reshape(PAIRS, 2, SG, 64).transpose(1, 3, 0, 2).reshape(P, -1),
        "c_im": a("ssm_c_im").reshape(PAIRS, 2, SG, 64).transpose(1, 3, 0, 2).reshape(P, -1),
        "d_skip": channel_major(a("ssm_d")), "norm_mix": channel_major(a("norm_mix")),
        "norm_ffn": channel_major(a("norm_ffn")), "b_gate": channel_major(a("b_gate")),
        "conv_w": a("conv_w").reshape(TAPS, CT, P).transpose(2, 1, 0).reshape(P, -1),
        "conv_b": channel_major(a("conv_b")), "ln_g": channel_major(a("conv_ln_g")),
        "ln_b": channel_major(a("conv_ln_b")),
        "cache": a("cache_conv").reshape(HALO, CT, P).transpose(2, 1, 0).reshape(P, -1),
        "eye": np.eye(P, dtype=np.float32),
        "keys": np.concatenate([a("peer_keys1")[0].T, a("peer_keys2")[0].T], axis=1),
    }
    packed = np.concatenate([parts[name] for name, _ in _WIDTHS], axis=1)
    w_in = tiles(a("w_in")[0])
    glu = tiles(a("w_ssm_glu")[0])
    cout = tiles(a("w_conv_out")[0])
    order = [0, 1, 2, 3, 8, 4, 9, 5, 10, 6, 11, 7, *range(12, 28)]
    slabs = [w_in[m] for m in order]
    slabs += [np.concatenate([glu[DT + j], glu[j]], axis=1) for j in range(DT)]
    slabs += [np.concatenate([cout[2 * j], cout[2 * j + 1]], axis=1) for j in range(DT // 2)]
    slabs += list(tiles(a("w_out")[0])) + list(tiles(a("peer_w_q")[0]))
    slabs = np.stack([s.reshape(P, D) for s in slabs])
    return packed, slabs


RING = 16
BATCH = 2
PAIR = 2 * TOPK
PB = PAIR // BATCH
TILES = SEQ // P
TPAIRS = HEADS // 2
SPAIRS = HEADS // 4


def peer_block(nc, x2_d, xh_d, score_d, g_ffn, g_final, consts, experts, y_prompt, y_sample):
    with ExitStack() as ctx:
        def sb(name, shape, dt=F32):
            return ctx.enter_context(nc.sbuf_tensor(name, shape, dt))

        def sem(name):
            return ctx.enter_context(nc.semaphore(name))

        cn = sb("cn", [P, 2 * P + TOPK])
        eye, fold, iota = cn[:, 0:P], cn[:, P:2 * P], cn[:, 2 * P:2 * P + TOPK]
        gf = sb("gf", [P, D])
        gl = sb("gl", [P, D])
        rows = sb("rows", [P, RING, 2 * D])
        x2t = sb("x2t", [P, D])
        xht = sb("xht", [P, D])
        xn = sb("xn", [P, D])
        yt = sb("yt", [P, D])
        sc = sb("sc", [P, 2, 2 * KEYS])
        topv = sb("topv", [P, 2, TOPK])
        topi = sb("topi", [P, 2, TOPK], U32)
        cand = sb("cand", [P, TOPK, TOPK])
        best = sb("best", [P, TOPK])
        pos = sb("pos", [P, TOPK], U32)
        hilo = sb("hilo", [P, 2, TOPK], U32)
        hot = sb("hot", [P, 2, TOPK, TOPK])
        part = sb("part", [P, 2, TOPK])
        idx = sb("idx", [P, 2, TOPK], U32)
        shifted = sb("shifted", [P, 2, TOPK])
        ex = sb("ex", [P, 2, TOPK])
        den = sb("den", [P, 2, 2])
        soft = sb("soft", [P, 2, TOPK])
        dots = sb("dots", [P, PAIR])
        act_v = sb("act_v", [P, PAIR])
        coef = sb("coef", [P, PAIR])
        diag = sb("diag", [P, RING, P])
        fin = sb("fin", [P, 4])
        acc_ps = ctx.enter_context(nc.psum_tensor("acc_ps", [P, 2, 512], F32))

        consts_in = sem("consts_in")
        x2_in = sem("x2_in")
        xh_in = sem("xh_in")
        score_in = [sem(f"score_in{i}") for i in range(2)]
        score_used = sem("score_used")
        xn_ready = sem("xn_ready")
        acc_begun = sem("acc_begun")
        idx_ready = sem("idx_ready")
        landed = [sem(f"landed{i}") for i in range(RING)]
        slot_free = sem("slot_free")
        gathers = sem("gathers")
        dots_done = sem("dots_done")
        gelu_done = sem("gelu_done")
        coef_done = sem("coef_done")
        diag_done = sem("diag_done")
        shift_done = sem("shift_done")
        exp_done = sem("exp_done")
        y_sq = sem("y_sq")
        y_ms = sem("y_ms")
        y_std = sem("y_std")
        y_ready = sem("y_ready")
        y_out = sem("y_out")
        yt_free = sem("yt_free")
        chain = sem("chain")
        v_passed = sem("v_passed")
        block = ctx.enter_context(nc.Block())

        STEPS = TPAIRS * PAIR
        x2_rows = x2_d[0:SEQ, :].rearrange("(t p) d -> t p d", p=P)
        xh_rows = xh_d[0:SEQ, :].rearrange("(t p) d -> t p d", p=P)
        y_rows = y_prompt.rearrange("b (t p) d -> (b t) p d", p=P)
        sc_rows = score_d.rearrange("(n a) p c -> n a p c", a=2)

        def tiles(eng, start, pair, end):
            with eng.Fori(0, TILES) as t:
                start(t, False)
                with eng.Fori(0, TPAIRS) as i:
                    pair(t * TPAIRS + i, False)
                end(t, False)
            start(TILES, True)
            for i in range(SPAIRS):
                pair(TILES * TPAIRS + i, i == SPAIRS - 1)
            end(TILES, True)

        @block.sync
        def _(sp):
            sp.sem_inc(yt_free, 1)
            sp.dma_start(cn[:, :], consts).then_inc(consts_in, 16)
            sp.dma_start(gf[:, :], g_ffn.broadcast_to([P, D])).then_inc(consts_in, 16)
            sp.dma_start(gl[:, :], g_final.broadcast_to([P, D])).then_inc(consts_in, 16)
            for a in range(2):
                sp.dma_start(sc[:, a, :], sc_rows[0, a]).then_inc(score_in[a], 16)

            def score_loads(n, last):
                if last:
                    return
                for a in range(2):
                    sp.wait_ge(score_used, 2 * n + a + 1)
                    sp.dma_start(sc[:, a, :], sc_rows[n + 1, a]).then_inc(score_in[a], 16)

            def store(t, sample):
                sp.wait_ge(y_ready, t + 2)
                if sample:
                    sp.dma_start(y_sample.rearrange("b p d -> (b p) d"), yt[0:DEC, :]).then_inc(y_out, 16)
                else:
                    sp.dma_start(y_rows[t], yt[:, :]).then_inc(y_out, 16)
                sp.wait_ge(y_out, 16 * t + 16)
                sp.sem_inc(yt_free, 1)

            def load(t, sample):
                sp.wait_ge(acc_begun, t + 1)
                sp.wait_ge(xn_ready, t + 1)
                if sample:
                    sp.dma_start(x2t[0:DEC, :], x2_d[SEQ:SEQ + DEC, :]).then_inc(x2_in, 16)
                    sp.dma_start(xht[0:DEC, :], xh_d[SEQ:SEQ + DEC, :]).then_inc(xh_in, 16)
                    sp.dma_start(xht[DEC:P, :], xh_d[SEQ:SEQ + DEC, :]).then_inc(xh_in, 16)
                else:
                    sp.dma_start(x2t[:, :], x2_rows[t]).then_inc(x2_in, 16)
                    sp.dma_start(xht[0:DEC, :], xh_rows[t][0:DEC]).then_inc(xh_in, 16)
                    sp.dma_start(xht[DEC:P, :], xh_rows[t][DEC:P]).then_inc(xh_in, 16)

            tiles(sp, load, score_loads, store)

        @block.gpsimd
        def _(pool):
            def pair(n, last):
                for s in range(PAIR):
                    a, k = divmod(s, TOPK)
                    if k == 0:
                        pool.wait_ge(idx_ready, 2 * n + a + 1)
                    pool.wait_ge(slot_free, PAIR * n + s + 1)
                    pool.sem_inc(gathers, 1)
                    pool.indirect_dma_start(
                        out=rows[:, s % RING, :], out_offset=None, in_=experts,
                        in_offset=bass.IndirectOffsetOnAxis(ap=idx[:, a, k:k + 1], axis=0),
                    ).then_inc(landed[s % RING], 16)

            tiles(pool, lambda t, sample: None, pair, lambda t, sample: None)

        @block.vector
        def _(dve):
            count = [0]

            def step(ins):
                count[0] += 1
                ins.then_inc(chain, 1)
                dve.wait_ge(chain, count[0])

            def choose(n, a):
                dve.sem_clear(chain)
                count[0] = 0
                dve.wait_ge(score_in[a], 16 * (n + 1))
                dve.sem_inc(v_passed, 1)
                for f in range(2):
                    s = sc[:, a, f * KEYS:(f + 1) * KEYS]
                    step(dve.max(topv[:, f, 0:8], s))
                    step(dve.max_index(topi[:, f, 0:8], topv[:, f, 0:8], s))
                    step(dve.match_replace(s, topv[:, f, 0:8], s, NEG))
                    step(dve.max(topv[:, f, 8:16], s))
                    step(dve.max_index(topi[:, f, 8:16], topv[:, f, 8:16], s))
                grid = [P, TOPK, TOPK]
                step(dve.tensor_tensor(cand[:, :, :], topv[:, 0, :].unsqueeze(2).to_broadcast(grid),
                                       topv[:, 1, :].unsqueeze(1).to_broadcast(grid), ALU.add))
                flat = cand[:, :, :].rearrange("p a b -> p (a b)")
                step(dve.max(best[:, 0:8], flat))
                step(dve.max_index(pos[:, 0:8], best[:, 0:8], flat))
                step(dve.match_replace(flat, best[:, 0:8], flat, NEG))
                step(dve.max(best[:, 8:16], flat))
                dve.tensor_scalar(shifted[:, a, :], best[:, :], best[:, 0:1], None, ALU.subtract).then_inc(shift_done, 1)
                step(dve.max_index(pos[:, 8:16], best[:, 8:16], flat))
                dve.tensor_scalar(hilo[:, 0, :], pos[:, :], 4, None, ALU.logical_shift_right).then_inc(score_used, 1)
                step(dve.tensor_scalar(hilo[:, 1, :], pos[:, :], TOPK - 1, None, ALU.bitwise_and))
                for f in range(2):
                    last = dve.tensor_tensor(hot[:, f, :, :], hilo[:, f, :].unsqueeze(2).to_broadcast(grid),
                                             iota.unsqueeze(1).to_broadcast(grid), ALU.is_equal)
                step(last)
                for f in range(2):
                    last = dve.tensor_tensor(hot[:, f, :, :], hot[:, f, :, :],
                                             topi[:, f, :].unsqueeze(1).to_broadcast(grid), ALU.mult)
                step(last)
                step(dve.tensor_reduce(part[:, :, :], hot[:, :, :, :], mybir.AxisListType.X, ALU.add))
                dve.scalar_tensor_tensor(idx[:, a, :], part[:, 0, :], float(KEYS), part[:, 1, :],
                                         ALU.mult, ALU.add).then_inc(idx_ready, 1)

            def weights(n):
                dve.wait_ge(exp_done, n + 1)
                step(dve.tensor_reduce(den[:, 0, :], ex[:, :, :], mybir.AxisListType.X, ALU.add))
                step(dve.reciprocal(den[:, 1, :], den[:, 0, :]))
                step(dve.tensor_tensor(soft[:, :, :], ex[:, :, :],
                                       den[:, 1, :].unsqueeze(2).to_broadcast([P, 2, TOPK]), ALU.mult))

            def coefficients(n, b):
                dve.wait_ge(gelu_done, PB * n + b + 1)
                cols = slice(b * BATCH, (b + 1) * BATCH)
                dve.tensor_tensor(coef[:, cols], act_v[:, cols],
                                  soft[:, :, :].rearrange("p a k -> p (a k)")[:, cols], ALU.mult).then_inc(coef_done, 1)

            def start(t, sample):
                dve.wait_ge(xh_in, 32 * t + 32)
                dve.tensor_tensor(xn[:, :], xht[:, :], gf[:, :], ALU.mult).then_inc(xn_ready, 1)
                dve.wait_ge(xn_ready, t + 2)
                dve.sem_inc(v_passed, 1)

            def pair(n, last):
                for b in range(PB):
                    for s in range(b * BATCH, (b + 1) * BATCH):
                        if s % BATCH == 1 and b % (PB // 2):
                            coefficients(n, b - 1)
                        r = s % RING
                        dve.wait_ge(landed[r], 16 * (PAIR // RING * n + s // RING + 1))
                        ins = dve.tensor_tensor_reduce(rows[:, r, 0:D], rows[:, r, 0:D], xn[:, :], 1.0, 0.0,
                                                       ALU.mult, ALU.add, dots[:, s:s + 1])
                    ins.then_inc(dots_done, 1)
                    if b % (PB // 2) == PB // 2 - 1:
                        coefficients(n, b)
                        if not last:
                            choose(n + 1, b // (PB // 2))
                if not last:
                    weights(n + 1)

            def end(t, sample):
                dve.sem_clear(chain)
                count[0] = 0
                dve.wait_ge(y_sq, 1 * t + 1)
                dve.tensor_scalar(fin[:, 1:2], fin[:, 0:1], 1.0 / D, EPS, ALU.mult, ALU.add).then_inc(y_ms, 1)
                dve.wait_ge(y_std, 1 * t + 1)
                step(dve.reciprocal(fin[:, 3:4], fin[:, 2:3]))
                dve.wait_ge(yt_free, t + 1)
                dve.scalar_tensor_tensor(yt[:, :], acc_ps[:, :, :].rearrange("p a b -> p (a b)"), fin[:, 3:4],
                                         gl[:, :], ALU.mult, ALU.mult).then_inc(y_ready, 1)

            dve.sem_inc(xn_ready, 1)
            dve.sem_inc(y_ready, 1)
            dve.wait_ge(consts_in, 48)
            for a in range(2):
                choose(0, a)
            weights(0)
            tiles(dve, start, pair, end)

        @block.scalar
        def _(act):
            act.wait_ge(consts_in, 48)

            def exps(n):
                act.wait_ge(shift_done, 2 * n + 2)
                act.activation(ex[:, :, :], shifted[:, :, :], ACT.Exp).then_inc(exp_done, 1)

            def pair(n, last):
                shape = fold if n_is_sample[0] else eye
                for b in range(PB):
                    cols = slice(b * BATCH, (b + 1) * BATCH)
                    act.wait_ge(dots_done, PB * n + b + 1)
                    act.activation(act_v[:, cols], dots[:, cols], ACT.Gelu).then_inc(gelu_done, 1)
                    act.wait_ge(coef_done, PB * n + b + 1)
                    for s in range(b * BATCH, (b + 1) * BATCH):
                        act.activation(diag[:, s % RING, :], shape, ACT.Copy, scale=coef[:, s:s + 1]).then_inc(diag_done, 1)
                if not last:
                    exps(n + 1)

            n_is_sample = [False]

            def start(t, sample):
                n_is_sample[0] = sample

            def end(t, sample):
                act.wait_ge(yt_free, t + 1)
                act.wait_ge(slot_free, RING + PAIR * ((TILES * TPAIRS + SPAIRS) if sample else TPAIRS * (t + 1)))
                act.activation(yt[:, :], acc_ps[:, :, :].rearrange("p a b -> p (a b)"), ACT.Square,
                               accum_out=fin[:, 0:1]).then_inc(y_sq, 1)
                act.wait_ge(y_ms, 1 * t + 1)
                act.activation(fin[:, 2:3], fin[:, 1:2], ACT.Sqrt).then_inc(y_std, 1)

            exps(0)
            tiles(act, start, pair, end)

        @block.tensor
        def _(pe):
            pe.wait_ge(consts_in, 48)
            pe.sem_inc(slot_free, RING)
            pe.sem_inc(acc_begun, 1)

            def start(t, sample):
                k = DEC if sample else P
                pe.wait_ge(x2_in, 16 * t + 16)
                pe.wait_ge(y_ready, t + 1)
                for h in range(2):
                    last = pe.matmul(acc_ps[:, h, :], eye[0:k, :], x2t[0:k, h * 512:(h + 1) * 512],
                                     start=True, stop=False, skip_group_check=True)
                last.then_inc(acc_begun, 1)

            def pair(n, last):
                for s in range(PAIR):
                    r = s % RING
                    pe.wait_ge(diag_done, PAIR * n + s + 1)
                    for h in range(2):
                        ins = pe.matmul(acc_ps[:, h, :], diag[:, r, :], rows[:, r, D + h * 512:D + (h + 1) * 512],
                                        start=False, stop=False, skip_group_check=True)
                    ins.then_inc(slot_free, 1)

            tiles(pe, start, pair, lambda t, sample: None)


def kernel(**inputs):
    import numpy as np
    import concourse.bacc as bacc
    from concourse.bass_utils import run_bass_kernel_spmd

    packed, slabs = _lay_out(inputs)
    experts = np.concatenate([np.asarray(inputs["peer_u"])[0], np.asarray(inputs["peer_v"])[0]], axis=1)
    fold = np.zeros((P, P), np.float32)
    fold[np.arange(P), np.arange(P) % DEC] = 1.0
    consts = np.concatenate([np.eye(P, dtype=np.float32), fold,
                             np.tile(np.arange(TOPK, dtype=np.float32), (P, 1))], axis=1)
    arrays = {
        "in_x_prompt": np.asarray(inputs["x_prompt"]), "in_x_sample": np.asarray(inputs["x_sample"]),
        "in_packed": packed, "in_slabs": slabs, "in_experts": experts, "in_consts": consts,
        "in_g_ffn": np.asarray(inputs["norm_ffn"]), "in_g_final": np.asarray(inputs["norm_final"]).reshape(1, D),
    }
    arrays = {k: np.ascontiguousarray(v) for k, v in arrays.items()}
    outs = {"out_y_prompt": (1, SEQ, D), "out_y_sample": (1, DEC, D), "out_ssm": (P, 4 * PAIRS),
            "out_conv": (P, 2 * CT * HALO)}

    nc = bacc.Bacc("TRN2", target_bir_lowering=False, num_devices=1)
    d = {k: nc.dram_tensor(k, v.shape, F32, kind="ExternalInput").ap() for k, v in arrays.items()}
    d |= {k: nc.dram_tensor(k, s, F32, kind="ExternalOutput").ap() for k, s in outs.items()}
    x2_d = nc.dram_tensor("x2_rows", (SEQ + DEC, D), F32, kind="Internal").ap()
    xh_d = nc.dram_tensor("xh_rows", (SEQ + DEC, D), F32, kind="Internal").ap()
    score_d = nc.dram_tensor("score_rows", (HEADS * SEQ // P + HEADS // 2, P, 2 * KEYS), F32, kind="Internal").ap()
    mixing_block(nc, d["in_x_prompt"], d["in_x_sample"], d["in_packed"], d["in_slabs"], x2_d, xh_d, score_d,
                 d["out_ssm"], d["out_conv"])
    peer_block(nc, x2_d, xh_d, score_d, d["in_g_ffn"], d["in_g_final"], d["in_consts"], d["in_experts"],
               d["out_y_prompt"], d["out_y_sample"])
    r = run_bass_kernel_spmd(nc, [arrays], core_ids=[0]).results[0]

    ssm = np.asarray(r["out_ssm"]).reshape(P, 2, PAIRS, 2).transpose(3, 1, 2, 0).reshape(2, 2, 1, 1, 2 * PAIRS, 64)
    conv = np.asarray(r["out_conv"]).reshape(P, CT, 2, HALO).transpose(2, 3, 1, 0).reshape(2, 1, 1, HALO, DC)
    return (r["out_y_prompt"], r["out_y_sample"], ssm[0, 0], ssm[0, 1], conv[0], ssm[1, 0], ssm[1, 1], conv[1])
```

```python
from contextlib import ExitStack

import concourse.bass as bass
from concourse import mybir

F32 = mybir.dt.float32
U32 = mybir.dt.uint32
ALU = mybir.AluOpType
ACT = mybir.ActivationFunctionType
AXIS = mybir.AxisListType.X

P = 128
D = 1024
DT = D // P
SEQ, DEC = 1024, 64
GROUPS = 4
NP, NS = SEQ // GROUPS, DEC // GROUPS
N = NP + NS
SPANS = ((0, P), (P, P), (NP, NS))
DC = 512
CT = DC // P
PAIRS = 16
SG = 16
TAPS = 31
HALO = TAPS - 1
NV = HALO + NP + HALO + NS
NC = NV - HALO
SOFF = NP + HALO
HEADS, KEYS, TOPK = 8, 128, 16
EPS = 1e-6
NEG = -3.0e38

TURNS = 32
STEPS = 8
PAIR = 2 * TOPK
QUARTERS = PAIR // STEPS
TPAIRS = HEADS // 2
SPAIRS = HEADS // 4
TILES = SEQ // P
GPAIRS = 2 * TPAIRS
RING = STEPS
BATCH = 2
TB = STEPS // BATCH
BLOCKS = TILES * HEADS + HEADS // 2

SLABS = 64
SLOTS = 4
S_CONV, S_GATE, S_GLU, S_COUT, S_OUT, S_Q = 4, 12, 28, 36, 40, 48

T_XN, T_U2, T_CONV, T_SSM, T_SSM_END, T_GLU, T_COUT, T_ROWS, T_Q = 1, 2, 3, 7, 15, 16, 20, 24, 25
TAPS_OF = {k: range(3 * (k - T_SSM), 3 * (k - T_SSM) + 3) for k in range(T_SSM, T_GLU)} | {T_GLU: range(27, TAPS)}
OUT_OF = {21: (0, 1, 2), 22: (3, 4, 5), 23: (6, 7)}
SLABS_OF = {1: (0, 1), 2: (2, 3)}
SLABS_OF |= {T_CONV + j: (S_CONV + 2 * j, S_CONV + 2 * j + 1) for j in range(CT)}
SLABS_OF |= {T_SSM + i: (S_GATE + 2 * i, S_GATE + 2 * i + 1) for i in range(DT)}
SLABS_OF |= {T_GLU + i: (S_GLU + 2 * i, S_GLU + 2 * i + 1) for i in range(DT // 2)}
SLABS_OF |= {T_COUT: tuple(range(S_COUT, S_OUT))}
Q_OF = {25: (0, 1), 26: (2, 3), 27: (4, 5, 6), 28: (7, 8), 29: (9, 10, 11), 30: (12, 13), 31: (14, 15)}
SLABS_OF |= {k: tuple(S_OUT + m for m in ms) for k, ms in OUT_OF.items()}
SLABS_OF |= {k: tuple(S_Q + m for m in ms) for k, ms in Q_OF.items()}

A_XN, A_U, A_CQ, A_GATE, A_GLU, A_OUT, A_XN2, A_Q = 0, 8, 12, 16, 32, 40, 48, 56
A_ALL = 88
A_BANKS = 2
V_CP, V_B, V_COUT, V_TOK = 0, 4, 46, 54
V_MEAN, V_VAR = 38, 41
V_GLU = (36, 37, 39, 40, 42, 43, 44, 45)
V_ALL = 60
V_BANKS = 3


def a_q(m):
    return A_Q if m == 0 else A_Q - 1 + 2 * m


def a_score(m):
    return A_Q + 2 + 2 * m if m < 15 else A_ALL - 1


def layout(widths):
    out, at = {}, 0
    for name, w in widths:
        out[name] = (at, w)
        at += w
    return out, at


KEPT = [("d_skip", CT), ("norm_mix", DT), ("norm_ffn", DT), ("b_gate", 2 * DT), ("conv_w", CT * TAPS),
        ("conv_b", CT), ("ln_g", CT), ("ln_b", CT), ("cache", CT * HALO), ("eye", P), ("fold", P),
        ("iota", TOPK), ("keys", 2 * KEYS)]
FIRST = [("lam_re", PAIRS), ("lam_im", PAIRS), ("log_step", PAIRS), ("h0_re", PAIRS), ("h0_im", PAIRS),
         ("b_re", PAIRS * SG), ("b_im", PAIRS * SG), ("c_re", PAIRS * SG), ("c_im", PAIRS * SG)]
KEPT_AT, KEPT_W = layout(KEPT)
FIRST_AT, FIRST_W = layout(FIRST)


def program(nc, x_prompt, x_sample, kept, first, slabs, experts, g_ffn, g_final, x2_d, xh_d, score_d, trig_d,
            y_prompt, y_sample, ssm_out, conv_out):
    with ExitStack() as ctx:
        def sb(name, shape, dt=F32):
            return ctx.enter_context(nc.sbuf_tensor(name, shape, dt))

        def sem(name):
            return ctx.enter_context(nc.semaphore(name))

        def flat(ap):
            return ap.rearrange("p a b -> p (a b)")

        pk = sb("pk", [P, KEPT_W])

        def par(name):
            a, w = KEPT_AT[name]
            return pk[:, a:a + w]

        ring = sb("ring", [P, SLOTS, D])
        xt = sb("xt", [P, 3, D])
        xnT = sb("xnT", [P, DT, N])
        merged = xnT
        gates = sb("gates", [P, 2 * DT, N])
        outT = gates[:, 0:DT, :]
        va = sb("va", [P, CT * (NV + NC)])
        vbuf = va[:, 0:CT * NV].rearrange("p (c n) -> p c n", c=CT)
        acc = va[:, CT * NV:].rearrange("p (c n) -> p c n", c=CT)
        xh = [va[:, 0:D], va[:, D:2 * D], flat(gates[:, :, :])[0:NS, DT * N:DT * N + D]]
        uy = sb("uy", [P, 2 * CT, N])
        uT, yT = uy[:, 0:CT, :], uy[:, CT:2 * CT, :]
        cs = yT
        scsb = flat(uy[:, :, :])[:, 0:2 * 3 * 2 * KEYS].rearrange("p (b t c) -> p b t c", b=2, t=3)
        tails = sb("tails", [P, CT, 2 * HALO])
        trig = sb("trig", [P, 2, 2, N])
        rot = sb("rot", [P, 2, N])
        rin = sb("rin", [P, 2, N])
        gp = sb("gp", [P, 6 * N])
        grot = gp[:, 0:4 * N].rearrange("p (b c n) -> p b c n", b=2, c=2)
        prod = gp[:, 4 * N:6 * N].rearrange("p (c n) -> p c n", c=2)
        sq = gp[:, 0:CT * NC].rearrange("p (c n) -> p c n", c=CT)
        hst = sb("hst", [P, 2, 2, N])
        lnr = flat(hst[:, 0, :, :]), flat(hst[:, 1, :, :])
        carry = sb("carry", [P, 2, PAIRS, 2])
        sig = sb("sig", [P, 2, N])
        qT = sig
        rho = sb("rho", [P, PAIRS])
        bst = sb("bst", [P, 2, CT, P])
        cst = sb("cst", [P, 2, PAIRS, 2 * SG])
        mean_w = sb("mean_w", [P, P])
        ssq = sb("ssq", [P, 3])
        rstd = sb("rstd", [P, 3])
        half = sb("half", [P, 1])
        sm = sb("sm", [P, 13, PAIRS])
        gf = sb("gf", [P, D])
        gl = sb("gl", [P, D])
        rows = sb("rows", [P, RING, 2 * D])
        x2t = sb("x2t", [P, D])
        xn = sb("xn", [P, 2, D])
        yt = sb("yt", [P, D])
        sc = sb("sc", [P, 2, 2 * KEYS])
        topv = sb("topv", [P, 2, TOPK])
        topi = sb("topi", [P, 2, TOPK], U32)
        cand = sb("cand", [P, TOPK, TOPK])
        best = sb("best", [P, TOPK])
        pos = sb("pos", [P, TOPK], U32)
        hilo = sb("hilo", [P, 2, TOPK], U32)
        hot = sb("hot", [P, TOPK, TOPK])
        part = sb("part", [P, 2, TOPK])
        idx = sb("idx", [P, 2, TOPK], U32)
        shifted = sb("shifted", [P, 2, TOPK])
        ex = sb("ex", [P, 2, TOPK])
        den = sb("den", [P, 2, 2])
        soft = sb("soft", [P, 2, TOPK])
        dots = sb("dots", [P, PAIR])
        act_v = sb("act_v", [P, PAIR])
        coef = sb("coef", [P, PAIR])
        diag = sb("diag", [P, RING, P])
        fin = sb("fin", [P, 4])
        spare = rows[:, :, :].rearrange("p a b -> p (a b)")
        table = spare[:, 0:PAIRS * 2 * N].rearrange("p (j c n) -> p j c n", j=PAIRS, c=2)
        cosT, sinT = table[:, :, 0, :], table[:, :, 1, :]
        flat_table = spare[:, 0:PAIRS * 2 * N].rearrange("p (j m) -> p j m", j=PAIRS)
        scratch = spare[:, 5 * 2 * D:7 * 2 * D]
        pf = spare[:, 7 * 2 * D:7 * 2 * D + FIRST_W]
        bpad = flat(gates[:, :, :])[:, 0:2 * PAIRS * 2 * SG].rearrange("p (c j h) -> p c j h", c=2, j=PAIRS)

        def par1(name):
            a, w = FIRST_AT[name]
            return pf[:, a:a + w]

        ps_a = ctx.enter_context(nc.psum_tensor("ps_a", [P, A_BANKS, 512], F32))
        ps_v = ctx.enter_context(nc.psum_tensor("ps_v", [P, V_BANKS, 512], F32))
        ps_y = ctx.enter_context(nc.psum_tensor("ps_y", [P, 512], F32))
        ps_acc = ctx.enter_context(nc.psum_tensor("ps_acc", [P, 2, 512], F32))

        kept_in = sem("kept_in")
        first_in = sem("first_in")
        norms_in = sem("norms_in")
        slab_in = [sem(f"slab_in{i}") for i in range(SLOTS)]
        trig_in = [sem(f"trig_in{i}") for i in range(2)]
        trig_stored = sem("trig_stored")
        x_in = sem("x_in")
        a_ready = sem("a_ready")
        a_done = sem("a_done")
        v_ready = sem("v_ready")
        v_done = sem("v_done")
        c_done = sem("c_done")
        y_summed = sem("y_summed")
        y_gelu = sem("y_gelu")
        merged_done = sem("merged_done")
        setup_v = sem("setup_v")
        setup_a = sem("setup_a")
        setup_t = sem("setup_t")
        setup_b = sem("setup_b")
        table_done = sem("table_done")
        sq_x = sem("sq_x")
        ms_x = sem("ms_x")
        rs_x = sem("rs_x")
        xh_ready = sem("xh_ready")
        scanned = sem("scanned")
        unrotated = sem("unrotated")
        conv_ready = sem("conv_ready")
        xc_sq = sem("xc_sq")
        std_ready = sem("std_ready")
        ln_ready = sem("ln_ready")
        ln_sig = sem("ln_sig")
        cs_ready = sem("cs_ready")
        rows_out = sem("rows_out")
        xh_out = sem("xh_out")
        score_out = [sem(f"score_out{i}") for i in range(2)]
        state_out = sem("state_out")
        v_chain = sem("v_chain")
        v_passed = sem("v_passed")
        p_chain = sem("p_chain")
        x2_in = sem("x2_in")
        xn_in = [sem(f"xn_in{i}") for i in range(2)]
        score_in = [sem(f"score_in{i}") for i in range(2)]
        score_used = sem("score_used")
        xn_ready = sem("xn_ready")
        cleared = sem("cleared")
        sp_passed = sem("sp_passed")
        acc_begun = sem("acc_begun")
        idx_ready = sem("idx_ready")
        landed = [sem(f"landed{i}") for i in range(RING)]
        slot_free = sem("slot_free")
        gathers = sem("gathers")
        dots_done = sem("dots_done")
        gelu_done = sem("gelu_done")
        coef_done = sem("coef_done")
        diag_done = sem("diag_done")
        shift_done = sem("shift_done")
        exp_done = sem("exp_done")
        y_sq = sem("y_sq")
        y_ms = sem("y_ms")
        y_std = sem("y_std")
        y_ready = sem("y_ready")
        y_out = sem("y_out")
        block = ctx.enter_context(nc.Block())

        SEGS = ((0, NP), (NP, N))
        xp_rows = x_prompt.rearrange("b (g t p) d -> (b g) p t d", g=GROUPS, p=P)
        xs_rows = x_sample.rearrange("b (g p) d -> (b g) p d", g=GROUPS)
        x2_g = x2_d[0:SEQ, :].rearrange("(g t p) d -> g p t d", g=GROUPS, p=P)
        xh_g = xh_d[0:SEQ, :].rearrange("(g t p) d -> g p t d", g=GROUPS, p=P)
        x2_s = x2_d[SEQ:SEQ + DEC, :].rearrange("(g p) d -> g p d", g=GROUPS)
        xh_s = xh_d[SEQ:SEQ + DEC, :].rearrange("(g p) d -> g p d", g=GROUPS)
        x2_t = x2_d[0:SEQ, :].rearrange("(t p) d -> t p d", p=P)
        xh_t = xh_d[0:SEQ, :].rearrange("(t f p) d -> t f p d", f=2, p=DEC)
        y_t = y_prompt.rearrange("b (t p) d -> (b t) p d", p=P)
        sc_g = score_d[0:TILES * HEADS].rearrange("(g t h) p c -> g h p t c", g=GROUPS, h=HEADS)
        sc_s = score_d[TILES * HEADS:BLOCKS].rearrange("k (f g p) c -> g f k p c", f=2, g=GROUPS)


        def last_tiles(eng, start, quarter, end):
            for t in (TILES - 2, TILES - 1):
                start(t, t % 2)
                with eng.Fori(0, TPAIRS) as i:
                    for q in range(QUARTERS):
                        quarter(t * TPAIRS + i, q)
                end(t)
            start(TILES, 0)
            for i in range(SPAIRS):
                for q in range(QUARTERS):
                    quarter(TILES * TPAIRS + i, q, last=i == SPAIRS - 1)
            end(TILES)

        @block.sync
        def _(sp):
            def pass_wait():
                sp.sem_inc(sp_passed, 1)

            def slab_through(s, g):
                if s < S_CONV:
                    sp.wait_ge(a_ready, A_ALL * g + A_U + s + 1)
                elif s < S_GATE:
                    j, second = divmod(s - S_CONV, 2)
                    if second:
                        sp.wait_ge(v_ready, V_ALL * g + V_CP + j + 1)
                    else:
                        sp.wait_ge(a_ready, A_ALL * g + A_CQ + j + 1)
                elif s < S_GLU:
                    sp.wait_ge(a_ready, A_ALL * g + A_GATE + s - S_GATE + 1)
                elif s < S_COUT:
                    sp.wait_ge(v_ready, V_ALL * g + V_GLU[s - S_GLU] + 1)
                elif s < S_OUT:
                    sp.wait_ge(v_ready, V_ALL * g + V_COUT + 2 * (s - S_COUT) + 2)
                elif s < S_Q:
                    sp.wait_ge(a_ready, A_ALL * g + A_OUT + s - S_OUT + 1)
                else:
                    sp.wait_ge(a_ready, A_ALL * g + a_q(s - S_Q) + 1)

            def load_x(g):
                sp.dma_start(xt[:, 0:2, :], xp_rows[g]).then_inc(x_in, 16)
                sp.dma_start(xt[0:NS, 2, :], xs_rows[g]).then_inc(x_in, 16)

            def load_trig(j):
                sp.dma_start(flat(trig[:, j % 2, :, :]), trig_d[j]).then_inc(trig_in[j % 2], 16)

            def mix(k, g):
                for s in SLABS_OF.get(k, ()):
                    slab_through(s, g)
                    sp.dma_start(ring[:, s % SLOTS, :], slabs[(s + SLOTS) % SLABS]).then_inc(slab_in[s % SLOTS], 16)
                if T_SSM <= k < T_SSM_END:
                    for j in (2 * (k - T_SSM), 2 * (k - T_SSM) + 1):
                        sp.wait_ge(unrotated, PAIRS * g + PAIRS + j + 1)
                        pass_wait()
                        load_trig((j + 2) % PAIRS)
                if k == TURNS - 2:
                    sp.wait_ge(rows_out, 32 * (g + 1))
                    pass_wait()
                    sp.wait_ge(xh_out, 48 * (g + 1))
                    pass_wait()
                    load_x((g + 1) % GROUPS)

            def load_scores(n, a):
                sp.dma_start(sc[:, a, :], score_d[2 * n + a]).then_inc(score_in[a], 16)

            def load_rows(t, b):
                sp.wait_ge(acc_begun, t + 1)
                pass_wait()
                sp.dma_start(x2t[:, :], x2_t[t]).then_inc(x2_in, 16)
                for f in range(2):
                    sp.dma_start(xn[f * DEC:(f + 1) * DEC, b, :], xh_t[t, f]).then_inc(xn_in[b], 16)

            def quarter(n, q, last=False, more=True):
                if q == 1 and not last:
                    sp.wait_ge(score_used, 2 * n + 2)
                    pass_wait()
                    load_scores(n + 1, 1)
                if q == 3 and more and not last:
                    sp.wait_ge(score_used, 2 * n + 3)
                    pass_wait()
                    load_scores(n + 2, 0)

            def store(t):
                sp.wait_ge(y_ready, t + 2)
                pass_wait()
                sp.dma_start(y_t[t], yt[:, :]).then_inc(y_out, 16)

            load_x(0)
            sp.dma_start(pk[:, :], kept).then_inc(kept_in, 16)
            sp.dma_start(pf, first).then_inc(first_in, 16)
            for s in range(SLOTS):
                sp.dma_start(ring[:, s, :], slabs[s]).then_inc(slab_in[s], 16)
            sp.dma_start(gf[:, :], g_ffn.broadcast_to([P, D])).then_inc(norms_in, 16)
            sp.dma_start(gl[:, :], g_final.broadcast_to([P, D])).then_inc(y_out, 16)
            for k in range(TURNS):
                if k == T_CONV + 2:
                    sp.wait_ge(table_done, 1)
                    sp.dma_start(trig_d.rearrange("j p m -> p j m"), flat_table).then_inc(trig_stored, 16)
                    sp.wait_ge(trig_stored, 16)
                    for j in range(2):
                        load_trig(j)
                mix(k, 0)
            for b in range(2):
                sp.wait_ge(score_out[b], 128)
                load_scores(0, b)
            load_rows(0, 0)
            sp.wait_ge(score_used, 1)
            load_scores(1, 0)

            with sp.Fori(0, GROUPS - 1) as g:
                for k in range(TURNS):
                    mix(k, g + 1)
                    if k == 0:
                        load_rows(2 * g + 1, 1)
                    if k == 1:
                        for b in range(2):
                            sp.wait_ge(score_out[b], 128 * g + 128)
                            pass_wait()
                    if k >= TURNS - QUARTERS and k % 2:
                        h = {27: 0, 29: 1, 31: 2}[k]
                        sp.wait_ge(score_out[h % 2], 128 * g + 128 + 32 * (h // 2 + 1))
                        pass_wait()
                    if k == TURNS - 5:
                        sp.wait_ge(score_out[0], 128 * g + 128 + 32)
                        pass_wait()
                        sp.wait_ge(rows_out, 32 * (g + 2))
                        pass_wait()
                        sp.wait_ge(xh_out, 48 * (g + 2))
                        pass_wait()
                        load_rows(2 * g + 2, 0)
                    quarter(GPAIRS * g + k // QUARTERS, k % QUARTERS)
                    if k == TURNS // 2:
                        store(2 * g)
                    if k == TURNS - 1:
                        store(2 * g + 1)

            sp.wait_ge(unrotated, PAIRS * (GROUPS + 1))
            sp.dma_start(ssm_out, carry[:, :, :, :].rearrange("p a b c -> p (a b c)")).then_inc(state_out, 16)
            sp.wait_ge(conv_ready, GROUPS)
            sp.dma_start(conv_out, flat(tails[:, :, :])).then_inc(state_out, 16)
            for b in range(2):
                sp.wait_ge(score_out[b], 128 * GROUPS)

            def start(t, b):
                if t == TILES - 2:
                    load_rows(t + 1, 1)
                if t == TILES - 1:
                    sp.wait_ge(acc_begun, t + 2)
                    pass_wait()
                    sp.dma_start(x2t[0:DEC, :], x2_d[SEQ:SEQ + DEC, :]).then_inc(x2_in, 16)
                    for f in range(2):
                        sp.dma_start(xn[f * DEC:(f + 1) * DEC, 0, :], xh_d[SEQ:SEQ + DEC, :]).then_inc(xn_in[0], 16)

            def end(t):
                if t == TILES:
                    sp.wait_ge(y_ready, t + 2)
                    pass_wait()
                    sp.dma_start(y_sample.rearrange("b p d -> (b p) d"), yt[0:DEC, :]).then_inc(y_out, 16)
                else:
                    store(t)

            def sp_quarter(n, q, last=False):
                quarter(n, q, last, more=not (isinstance(n, int) and n == TILES * TPAIRS))

            last_tiles(sp, start, sp_quarter, end)
            sp.wait_ge(y_out, 16 * (TILES + 2))
            sp.wait_ge(state_out, 32)
            for i in range(SLOTS):
                sp.wait_ge(slab_in[i], 16 * (1 + GROUPS * SLABS // SLOTS))
            for i in range(2):
                sp.wait_ge(trig_in[i], 16 * (1 + GROUPS * PAIRS // 2))
            sp.wait_ge(x_in, 32 * (1 + GROUPS))

        @block.tensor
        def _(pe):
            eye = par("eye")

            def a_tile(n, g):
                pe.wait_ge(a_done, A_ALL * g + n + 1)
                return ps_a[:, n % A_BANKS, :]

            def a_emptied(n, g):
                pe.wait_ge(a_done, A_ALL * g + n + 1 + A_BANKS)

            def v_tile(n, g):
                pe.wait_ge(v_done, V_ALL * g + n + 1)
                return ps_v[:, n % V_BANKS, :]

            def slab(s, g):
                pe.wait_ge(slab_in[s % SLOTS], 16 * ((SLABS // SLOTS) * g + s // SLOTS + 1))

            def product(out, s, k0, rhs):
                kt = rhs.shape[1]
                for k in range(kt):
                    w = ring[:, s % SLOTS, (k0 + k) * P:(k0 + k + 1) * P]
                    last = pe.matmul(out[:, 0:N], w, rhs[:, k, :], start=(k == 0), stop=(k == kt - 1))
                return last

            def to_channels(n0, turn, g):
                pe.wait_ge(xh_ready, 2 * g + turn)
                for k in range(DT):
                    out = a_tile(n0 + k, g)
                    for t in range(2):
                        pe.transpose(out[:, t * P:(t + 1) * P], xh[t][:, k * P:(k + 1) * P], eye)
                    pe.transpose(out[:, NP:N], xh[2][:, k * P:(k + 1) * P], eye[0:NS, 0:NS]).then_inc(a_ready, 1)
                a_emptied(n0 + DT - 1, g)

            def b_product(j, g):
                q, t = 32 * (j % 4), j // 4
                for c in range(2):
                    out = v_tile(V_B + 2 * j + c, g)
                    pe.matmul(out[:, 0:N], bst[q:q + 32, c, t, :], uT[q:q + 32, t, :],
                              start=True, stop=True).then_inc(v_ready, 1)

            def c_product(j, g):
                q, t = 32 * (j % 4), j // 4
                if j % 4 == 0 and t:
                    pe.wait_ge(y_summed, CT * g + t)
                pe.wait_ge(unrotated, PAIRS * g + PAIRS + j + 1)
                for c in range(2):
                    last = pe.matmul(ps_y[q:q + 32, 0:N], cst[:, c, j, :], hst[:, j % 2, c, :],
                                     start=(c == 0), stop=(c == 1))
                last.then_inc(c_done, 1)

            def gate(j, g):
                out = a_tile(A_GATE + j, g)
                slab(S_GATE + j, g)
                product(out, S_GATE + j, 0, xnT[:, :, :]).then_inc(a_ready, 1)

            def channel_mean(n, src, g):
                out = v_tile(n, g)
                for c in range(CT):
                    last = pe.matmul(out[:, 0:NC], mean_w[:, :], src[:, c, :], start=(c == 0), stop=(c == CT - 1))
                last.then_inc(v_ready, 1)

            def glu(j, g):
                out = a_tile(A_GLU + j, g)
                slab(S_GLU + j, g)
                product(out, S_GLU + j, 0, yT[:, :, :]).then_inc(a_ready, 1)
                out = v_tile(V_GLU[j], g)
                product(out, S_GLU + j, CT, yT[:, :, :]).then_inc(v_ready, 1)

            def scores(m, g):
                out = a_tile(a_score(m), g)
                a_emptied(a_q(m), g)
                keys = par("keys")[:, (m % 2) * KEYS:(m % 2 + 1) * KEYS]
                for t, (n, width) in enumerate(SPANS):
                    last = pe.matmul(out[0:width, t * KEYS:(t + 1) * KEYS], qT[:, m % 2, n:n + width], keys,
                                     start=True, stop=True)
                last.then_inc(a_ready, 1)

            def mix(k, g):
                if k == T_XN:
                    to_channels(A_XN, 1, g)
                if k in (T_XN, T_U2):
                    for m in SLABS_OF[k]:
                        out = a_tile(A_U + m, g)
                        slab(m, g)
                        product(out, m, 0, xnT[:, :, :]).then_inc(a_ready, 1)
                if T_CONV <= k < T_SSM:
                    j = k - T_CONV
                    out = a_tile(A_CQ + j, g)
                    slab(S_CONV + 2 * j, g)
                    product(out, S_CONV + 2 * j, 0, xnT[:, :, :]).then_inc(a_ready, 1)
                    out = v_tile(V_CP + j, g)
                    slab(S_CONV + 2 * j + 1, g)
                    product(out, S_CONV + 2 * j + 1, 0, xnT[:, :, :]).then_inc(v_ready, 1)
                if T_SSM <= k < T_SSM_END:
                    j = 2 * (k - T_SSM)
                    if j == 0:
                        a_emptied(A_U + CT - 1, g)
                    b_product(j, g)
                    if j:
                        c_product(j - 1, g)
                    gate(j, g)
                    b_product(j + 1, g)
                    c_product(j, g)
                    gate(j + 1, g)
                if k == T_SSM_END:
                    c_product(PAIRS - 1, g)
                if T_GLU <= k < T_COUT:
                    i = k - T_GLU
                    if i == 0:
                        pe.wait_ge(y_gelu, CT * (g + 1))
                    if i == 1:
                        pe.wait_ge(conv_ready, g + 1)
                        channel_mean(V_MEAN, acc, g)
                    if i == 2:
                        pe.wait_ge(xc_sq, g + 1)
                        channel_mean(V_VAR, sq, g)
                    glu(2 * i, g)
                    glu(2 * i + 1, g)
                if k == T_COUT:
                    pe.wait_ge(cs_ready, CT * (g + 1))
                    for j in range(DT):
                        out = v_tile(V_COUT + j, g)
                        if j % 2 == 0:
                            slab(S_COUT + j // 2, g)
                        product(out, S_COUT + j // 2, CT * (j % 2), cs[:, :, :]).then_inc(v_ready, 1)
                for j in OUT_OF.get(k, ()):
                    if j == 0:
                        pe.wait_ge(merged_done, DT * (g + 1))
                    out = a_tile(A_OUT + j, g)
                    slab(S_OUT + j, g)
                    product(out, S_OUT + j, 0, merged[:, :, :]).then_inc(a_ready, 1)
                if k == T_ROWS:
                    a_emptied(A_OUT + DT - 1, g)
                    for t, (n, width) in enumerate(SPANS):
                        for h in range(2):
                            out = v_tile(V_TOK + 2 * t + h, g)
                            for m in range(4):
                                last = pe.transpose(out[0:width, m * P:(m + 1) * P], outT[:, 4 * h + m, n:n + width], eye)
                            last.then_inc(v_ready, 1)
                if k == T_Q:
                    to_channels(A_XN2, 2, g)
                for m in Q_OF.get(k, ()):
                    out = a_tile(a_q(m), g)
                    slab(S_Q + m, g)
                    product(out, S_Q + m, 0, xnT[:, :, :]).then_inc(a_ready, 1)
                    if m:
                        scores(m - 1, g)
                if k == TURNS - 1:
                    scores(2 * HEADS - 1, g)

            def start(t, b):
                w = DEC if isinstance(t, int) and t == TILES else P
                pe.wait_ge(x2_in, 16 * t + 16)
                pe.wait_ge(y_ready, t + 1)
                for h in range(2):
                    last = pe.matmul(ps_acc[:, h, :], eye[0:w, :], x2t[0:w, h * 512:(h + 1) * 512],
                                     start=True, stop=False, skip_group_check=True)
                last.then_inc(acc_begun, 1)

            def quarter(n, q, last=False):
                for s in range(STEPS):
                    pe.wait_ge(diag_done, PAIR * n + STEPS * q + s + 1)
                    for h in range(2):
                        ins = pe.matmul(ps_acc[:, h, :], diag[:, s, :], rows[:, s, D + h * 512:D + (h + 1) * 512],
                                        start=False, stop=False, skip_group_check=True)
                    ins.then_inc(slot_free, 1)

            pe.wait_ge(kept_in, 16)
            pe.sem_inc(slot_free, RING)
            pe.sem_inc(acc_begun, 1)
            for k in range(TURNS):
                if k == T_SSM:
                    pe.wait_ge(setup_v, 3)
                    for c in range(2):
                        for t in range(CT):
                            last = pe.transpose(ps_acc[:, c, t * P:(t + 1) * P],
                                                bpad[:, c, 4 * t:4 * t + 4, :].rearrange("p a b -> p (a b)"), eye)
                    last.then_inc(setup_t, 1)
                    pe.wait_ge(setup_b, 1)
                mix(k, 0)
            with pe.Fori(0, GROUPS - 1) as g:
                for k in range(TURNS):
                    mix(k, g + 1)
                    if k % (TURNS // 2) == 0:
                        start(2 * g + k // (TURNS // 2), 0)
                    quarter(GPAIRS * g + k // QUARTERS, k % QUARTERS)
            last_tiles(pe, start, quarter, lambda t: None)

        @block.scalar
        def _(act):
            def ready(n, g):
                act.wait_ge(a_ready, A_ALL * g + n + 1)
                return ps_a[:, n % A_BANKS, :]

            def squares():
                act.activation(flat(merged[:, :, :])[:, 0:D], xt[:, 0, :], ACT.Square, accum_out=ssq[:, 0:1])
                act.activation(flat(merged[:, :, :])[:, D:2 * D], xt[:, 1, :], ACT.Square, accum_out=ssq[:, 1:2])
                act.activation(gp[0:NS, 0:D], xt[0:NS, 2, :], ACT.Square, accum_out=ssq[0:NS, 2:3]).then_inc(sq_x, 1)

            def to_channels(n0, name, g):
                for k in range(DT):
                    act.activation(xnT[:, k, :], ready(n0 + k, g)[:, 0:N], ACT.Copy,
                                   scale=par(name)[:, k:k + 1]).then_inc(a_done, 1)

            def v_emptied(n, g):
                act.wait_ge(v_done, V_ALL * g + V_BANKS + n + 1)

            def glu(j, g):
                if j >= 2:
                    v_emptied(V_GLU[j - 2], g)
                act.activation(sig[:, j % 2, :], ready(A_GLU + j, g)[:, 0:N], ACT.Sigmoid).then_inc(a_done, 1)

            def keep_scores(m, g):
                h, b = m // 2, (m // 2) % 2
                cols = slice((m % 2) * KEYS, (m % 2 + 1) * KEYS)
                if m % 2 == 0 and h >= 2:
                    act.wait_ge(score_out[b], 128 * g + 32 * (h // 2))
                src = ready(a_score(m), g)
                act.activation(scsb[:, b, 0:2, cols], src[:, 0:2 * KEYS].rearrange("p (t c) -> p t c", t=2), ACT.Copy)
                act.activation(scsb[0:NS, b, 2, cols], src[0:NS, 2 * KEYS:3 * KEYS], ACT.Copy).then_inc(a_done, 1)
                if m % 2:
                    act.wait_ge(a_done, A_ALL * g + A_BANKS + a_score(m) + 1)
                    act.dma_start(sc_g[g, h], scsb[:, b, 0:2, :]).then_inc(score_out[b], 16)
                    act.dma_start(sc_s[g, h // 4, h % 4], scsb[0:NS, b, 2, :]).then_inc(score_out[b], 16)

            def mix(k, g):
                if k == 0:
                    act.wait_ge(x_in, 32 * (g + 1))
                    squares()
                if k == T_XN:
                    to_channels(A_XN, "norm_mix", g)
                    if not isinstance(g, int):
                        for b in range(2):
                            act.wait_ge(score_out[b], 128 * g)
                if k in (T_XN, T_U2):
                    for m in SLABS_OF[k]:
                        act.activation(uT[:, m, :], ready(A_U + m, g)[:, 0:N], ACT.Copy).then_inc(a_done, 1)
                if T_CONV <= k < T_SSM:
                    j = k - T_CONV
                    if j >= 2:
                        v_emptied(V_CP + j - 2, g)
                    act.activation(sig[:, j % 2, :], ready(A_CQ + j, g)[:, 0:N], ACT.Sigmoid).then_inc(a_done, 1)
                if T_SSM <= k < T_SSM_END:
                    for m in (2 * (k - T_SSM), 2 * (k - T_SSM) + 1):
                        act.activation(gates[:, m, :], ready(A_GATE + m, g)[:, 0:N], ACT.Sigmoid,
                                       bias=par("b_gate")[:, m:m + 1]).then_inc(a_done, 1)
                if k == T_SSM_END:
                    for t in range(CT):
                        act.wait_ge(y_summed, CT * g + t + 1)
                        act.activation(yT[:, t, :], yT[:, t, :], ACT.Gelu).then_inc(y_gelu, 1)
                if T_GLU <= k < T_COUT:
                    i = k - T_GLU
                    if i == 1:
                        v_emptied(V_MEAN, g)
                        act.activation(sq[:, :, :], acc[:, :, :], ACT.Square).then_inc(xc_sq, 1)
                    glu(2 * i, g)
                    glu(2 * i + 1, g)
                    if i == 2:
                        v_emptied(V_VAR, g)
                        act.activation(lnr[1][:, 0:NC], lnr[0][:, 0:NC], ACT.Sqrt).then_inc(std_ready, 1)
                    if i == 3:
                        act.wait_ge(ln_ready, g + 1)
                        for c in range(CT):
                            act.activation(sq[:, c, :], acc[:, c, :], ACT.Sigmoid, bias=par("ln_b")[:, c:c + 1],
                                           scale=par("ln_g")[:, c:c + 1]).then_inc(ln_sig, 1)
                for j in OUT_OF.get(k, ()):
                    act.activation(outT[:, j, :], ready(A_OUT + j, g)[:, 0:N], ACT.Copy).then_inc(a_done, 1)
                if k == T_ROWS:
                    v_emptied(V_ALL - 1, g)
                    act.dma_start(x2_g[g], xt[:, 0:2, :]).then_inc(rows_out, 16)
                    act.dma_start(x2_s[g], xt[0:NS, 2, :]).then_inc(rows_out, 16)
                    squares()
                if k == T_Q:
                    to_channels(A_XN2, "norm_ffn", g)
                    act.wait_ge(xh_ready, 2 * g + 2)
                    for t in range(2):
                        act.dma_start(xh_g[g, :, t], xh[t]).then_inc(xh_out, 16)
                    act.dma_start(xh_s[g], xh[2]).then_inc(xh_out, 16)
                for m in Q_OF.get(k, ()):
                    act.activation(qT[:, m % 2, :], ready(a_q(m), g)[:, 0:N], ACT.Copy).then_inc(a_done, 1)
                    if m:
                        keep_scores(m - 1, g)
                if k == TURNS - 1:
                    keep_scores(2 * HEADS - 1, g)

            def exps(n):
                act.wait_ge(shift_done, 2 * n + 2)
                act.activation(ex[:, :, :], shifted[:, :, :], ACT.Exp).then_inc(exp_done, 1)

            shape = [par("eye")]

            def quarter(n, q, last=False):
                for b in range(TB):
                    batch = TB * q + b
                    cols = slice(batch * BATCH, (batch + 1) * BATCH)
                    act.wait_ge(dots_done, TB * QUARTERS * n + batch + 1)
                    act.activation(act_v[:, cols], dots[:, cols], ACT.Gelu).then_inc(gelu_done, 1)
                    act.wait_ge(coef_done, TB * QUARTERS * n + batch + 1)
                    for s in range(b * BATCH, (b + 1) * BATCH):
                        c = STEPS * q + s
                        act.activation(diag[:, s, :], shape[0], ACT.Copy, scale=coef[:, c:c + 1]).then_inc(diag_done, 1)
                if q == QUARTERS - 1 and not last:
                    exps(n + 1)

            def start(t, b):
                if isinstance(t, int) and t == TILES:
                    shape[0] = par("fold")

            def end(t):
                steps = PAIR * (TILES * TPAIRS + SPAIRS) if isinstance(t, int) and t == TILES else PAIR * TPAIRS * (t + 1)
                act.wait_ge(y_out, 16 * t + 16)
                act.wait_ge(slot_free, RING + steps)
                act.activation(yt[:, :], flat(ps_acc[:, :, :]), ACT.Square, accum_out=fin[:, 0:1]).then_inc(y_sq, 1)
                act.wait_ge(y_ms, 1 * t + 1)
                act.activation(fin[:, 2:3], fin[:, 1:2], ACT.Sqrt).then_inc(y_std, 1)

            act.sem_inc(a_done, A_BANKS)
            act.wait_ge(cleared, 1)
            mix(0, 0)
            act.wait_ge(kept_in, 16)
            act.wait_ge(first_in, 16)
            act.activation(sm[:, 0, :], par1("log_step"), ACT.Exp).then_inc(setup_a, 1)
            act.wait_ge(setup_v, 1)
            act.activation(rho[:, :], sm[:, 4, :], ACT.Exp).then_inc(setup_a, 1)
            act.wait_ge(setup_v, 2)
            act.activation(sm[:, 6, :], sm[:, 3, :], ACT.Sin).then_inc(setup_a, 1)
            act.activation(sm[:, 7, :], sm[:, 5, :], ACT.Sin).then_inc(setup_a, 1)
            for k in range(1, TURNS):
                mix(k, 0)
            exps(0)
            with act.Fori(0, GROUPS - 1) as g:
                for k in range(TURNS):
                    mix(k, g + 1)
                    if k == TURNS // 2:
                        end(2 * g)
                    quarter(GPAIRS * g + k // QUARTERS, k % QUARTERS)
                    if k == TURNS - 1:
                        end(2 * g + 1)
            last_tiles(act, start, quarter, end)

        @block.vector
        def _(dve):
            count = [0]

            def restart():
                dve.sem_clear(v_chain)
                count[0] = 0

            def mark(ins):
                count[0] += 1
                ins.then_inc(v_chain, 1)
                return count[0]

            def after(n):
                dve.wait_ge(v_chain, n)

            def step(ins):
                after(mark(ins))

            def setup_constants():
                step(dve.memset(ssq[:, :], float(D)))
                dve.memset(half[:, :], -0.5)
                dve.memset(mean_w[:, :], 1.0 / DC)
                dve.memset(tails[:, :, 0:HALO], 0.0).then_inc(cleared, 1)
                dve.memset(bpad[:, :, :, :], 0.0)
                dve.memset(cst[:, :, :, :], 0.0)
                step(dve.memset(carry[:, :, :, :], 0.0))

            def setup():
                dve.wait_ge(kept_in, 16)
                dve.tensor_copy(tails[:, :, HALO:2 * HALO], par("cache").rearrange("p (c k) -> p c k", c=CT))
                dve.wait_ge(first_in, 16)
                dve.tensor_copy(carry[:, 0, :, 1], par1("h0_re"))
                step(dve.tensor_copy(carry[:, 1, :, 1], par1("h0_im")))
                lr, li = par1("lam_re"), par1("lam_im")
                dve.wait_ge(setup_a, 1)
                dve.tensor_tensor(sm[:, 1, :], li, sm[:, 0, :], ALU.mult)
                dve.tensor_tensor(sm[:, 4, :], lr, sm[:, 0, :], ALU.mult).then_inc(setup_v, 1)
                dve.wait_ge(setup_v, 1)
                magic = float(3 * 2 ** 22)
                step(dve.tensor_scalar(sm[:, 2, :], sm[:, 1, :], 0.15915494309189535, magic, ALU.mult, ALU.add))
                step(dve.tensor_scalar(sm[:, 2, :], sm[:, 2, :], magic, None, ALU.subtract))
                step(dve.scalar_tensor_tensor(sm[:, 3, :], sm[:, 2, :], -6.28125, sm[:, 1, :], ALU.mult, ALU.add))
                step(dve.scalar_tensor_tensor(sm[:, 3, :], sm[:, 2, :], -0.0019353071795864769, sm[:, 3, :],
                                              ALU.mult, ALU.add))
                step(dve.tensor_scalar(sm[:, 3, :], sm[:, 3, :], 3.1415925, -3.1415925, ALU.min, ALU.max))
                step(dve.tensor_scalar(sm[:, 5, :], sm[:, 3, :], -1.0, None, ALU.mult))
                step(dve.tensor_tensor(sm[:, 5, :], sm[:, 5, :], sm[:, 3, :], ALU.min))
                dve.tensor_scalar(sm[:, 5, :], sm[:, 5, :], 1.5707963267948966, None, ALU.add).then_inc(setup_v, 1)
                dve.wait_ge(setup_a, 4)
                sin, cos = sm[:, 6, :], sm[:, 7, :]
                dve.tensor_copy(cosT[:, :, 0], cos)
                dve.tensor_copy(sinT[:, :, 0], sin)
                step(dve.tensor_tensor(sm[:, 0, :], rho[:, :], cos, ALU.mult))
                dve.tensor_scalar(sm[:, 0, :], sm[:, 0, :], -1.0, None, ALU.add)
                dve.tensor_tensor(sm[:, 1, :], rho[:, :], sin, ALU.mult)
                dve.tensor_tensor(sm[:, 2, :], lr, lr, ALU.mult)
                step(dve.tensor_tensor(sm[:, 3, :], li, li, ALU.mult))
                step(dve.tensor_tensor(sm[:, 2, :], sm[:, 2, :], sm[:, 3, :], ALU.add))
                step(dve.reciprocal(sm[:, 8, :], sm[:, 2, :]))
                dve.tensor_tensor(sm[:, 2, :], sm[:, 0, :], lr, ALU.mult)
                dve.tensor_tensor(sm[:, 3, :], sm[:, 1, :], li, ALU.mult)
                dve.tensor_tensor(sm[:, 9, :], sm[:, 1, :], lr, ALU.mult)
                step(dve.tensor_tensor(sm[:, 10, :], sm[:, 0, :], li, ALU.mult))
                dve.tensor_tensor(sm[:, 2, :], sm[:, 2, :], sm[:, 3, :], ALU.add)
                step(dve.tensor_tensor(sm[:, 9, :], sm[:, 9, :], sm[:, 10, :], ALU.subtract))
                dve.tensor_tensor(sm[:, 11, :], sm[:, 2, :], sm[:, 8, :], ALU.mult)
                step(dve.tensor_tensor(sm[:, 12, :], sm[:, 9, :], sm[:, 8, :], ALU.mult))
                for half_pair in range(2):
                    part_rows = slice(64 * half_pair, 64 * half_pair + 64)
                    cols = slice(SG * half_pair, SG * half_pair + SG)

                    def v3(name):
                        return par1(name)[part_rows].rearrange("p (j h) -> p j h", j=PAIRS)

                    def bc(n):
                        return sm[part_rows, n, :].unsqueeze(2).to_broadcast([64, PAIRS, SG])

                    tmp = [scratch[part_rows, n * PAIRS * SG:(n + 1) * PAIRS * SG].rearrange("p (j h) -> p j h", j=PAIRS)
                           for n in range(4)]
                    dve.tensor_tensor(tmp[0], v3("b_re"), bc(11), ALU.mult)
                    dve.tensor_tensor(tmp[1], v3("b_im"), bc(12), ALU.mult)
                    dve.tensor_tensor(tmp[2], v3("b_im"), bc(11), ALU.mult)
                    step(dve.tensor_tensor(tmp[3], v3("b_re"), bc(12), ALU.mult))
                    dve.tensor_tensor(bpad[part_rows, 0, :, cols], tmp[0], tmp[1], ALU.subtract)
                    step(dve.tensor_tensor(bpad[part_rows, 1, :, cols], tmp[2], tmp[3], ALU.add))
                    dve.tensor_copy(cst[part_rows, 0, :, cols], v3("c_re"))
                    step(dve.tensor_scalar(cst[part_rows, 1, :, cols], v3("c_im"), -1.0, None, ALU.mult))
                dve.sem_inc(setup_v, 1)
                w = 1
                while w < NP:
                    t0 = scratch[:, 0:PAIRS * w].rearrange("p (j n) -> p j n", j=PAIRS)
                    t1 = scratch[:, PAIRS * w:2 * PAIRS * w].rearrange("p (j n) -> p j n", j=PAIRS)
                    cw = cosT[:, :, w - 1:w].to_broadcast([P, PAIRS, w])
                    sw = sinT[:, :, w - 1:w].to_broadcast([P, PAIRS, w])
                    dve.tensor_tensor(t0, cosT[:, :, 0:w], cw, ALU.mult)
                    step(dve.tensor_tensor(t1, sinT[:, :, 0:w], sw, ALU.mult))
                    step(dve.tensor_tensor(cosT[:, :, w:2 * w], t0, t1, ALU.subtract))
                    dve.tensor_tensor(t0, sinT[:, :, 0:w], cw, ALU.mult)
                    step(dve.tensor_tensor(t1, cosT[:, :, 0:w], sw, ALU.mult))
                    step(dve.tensor_tensor(sinT[:, :, w:2 * w], t0, t1, ALU.add))
                    w *= 2
                dve.tensor_copy(cosT[:, :, NP:N], cosT[:, :, 0:NS])
                dve.tensor_copy(sinT[:, :, NP:N], sinT[:, :, 0:NS]).then_inc(table_done, 1)

            def ready(n, g):
                dve.wait_ge(v_ready, V_ALL * g + n + 1)
                return ps_v[:, n % V_BANKS, :]

            def emptied(n, g):
                dve.wait_ge(v_done, V_ALL * g + V_BANKS + n + 1)

            def normalise(turn, g):
                dve.wait_ge(sq_x, 2 * g + turn)
                dve.tensor_scalar(rstd[:, :], ssq[:, :], 1.0 / D, EPS, ALU.mult, ALU.add).then_inc(ms_x, 1)
                dve.wait_ge(rs_x, 2 * g + turn)
                for t, (_, w) in enumerate(SPANS):
                    last = dve.tensor_scalar(xh[t], xt[0:w, t, :], rstd[0:w, t:t + 1], None, ALU.mult)
                last.then_inc(xh_ready, 1)

            def scan(j, g):
                re, im = ready(V_B + 2 * j, g), ready(V_B + 2 * j + 1, g)
                dve.wait_ge(trig_in[j % 2], 16 * (PAIRS // 2 * g + j // 2 + 1))
                c, s = trig[:, j % 2, 0, :], trig[:, j % 2, 1, :]
                dve.tensor_tensor(rot[:, 0, :], re[:, 0:N], c, ALU.mult)
                step(dve.tensor_tensor(rot[:, 1, :], im[:, 0:N], s, ALU.mult))
                step(dve.tensor_tensor(rin[:, 0, :], rot[:, 0, :], rot[:, 1, :], ALU.add))
                dve.tensor_tensor(rot[:, 0, :], im[:, 0:N], c, ALU.mult)
                dve.tensor_tensor(rot[:, 1, :], re[:, 0:N], s, ALU.mult).then_inc(v_done, 2)
                emptied(V_B + 2 * j + 1, g)
                b = mark(dve.tensor_tensor(rin[:, 1, :], rot[:, 0, :], rot[:, 1, :], ALU.subtract))
                dve.wait_ge(unrotated, PAIRS * g + PAIRS + j - 1)
                for p in range(2):
                    if p:
                        after(b)
                    for stream, (lo, hi) in enumerate(SEGS):
                        last = dve.tensor_tensor_scan(
                            grot[:, j % 2, p, lo:hi], rho[:, j:j + 1].to_broadcast([P, hi - lo]),
                            rin[:, p, lo:hi], carry[:, p, j, stream:stream + 1], ALU.mult, ALU.add)
                last.then_inc(scanned, 1)

            def skip(t, g):
                dve.wait_ge(c_done, PAIRS * g + 2 + 4 * t + 4)
                dve.scalar_tensor_tensor(yT[:, t, :], uT[:, t, :], par("d_skip")[:, t:t + 1],
                                         ps_y[:, 0:N], ALU.mult, ALU.add).then_inc(y_summed, 1)

            before = [0] * CT

            def tap(k):
                taps = par("conv_w")
                for c in range(CT):
                    src, wk = vbuf[:, c, k:k + NC], taps[:, c * TAPS + k:c * TAPS + k + 1]
                    if k == 0:
                        before[c] = mark(dve.tensor_scalar(acc[:, c, :], src, wk, par("conv_b")[:, c:c + 1],
                                                           ALU.mult, ALU.add))
                    else:
                        after(before[c])
                        last = dve.scalar_tensor_tensor(acc[:, c, :], src, wk, acc[:, c, :], ALU.mult, ALU.add)
                        if k < TAPS - 1:
                            before[c] = mark(last)
                if k == TAPS - 1:
                    last.then_inc(conv_ready, 1)

            def glu(j, g):
                dve.wait_ge(a_done, A_ALL * g + A_BANKS + A_GLU + j + 1)
                src = ready(V_GLU[j], g)
                dve.tensor_tensor(rot[:, j % 2, :], src[:, 0:N], sig[:, j % 2, :], ALU.mult).then_inc(v_done, 1)
                emptied(V_GLU[j], g)
                mark(dve.tensor_tensor(merged[:, j, :], rot[:, j % 2, :], gates[:, j, :], ALU.mult))

            def mix(k, g):
                if k == 0:
                    normalise(1, g)
                if T_CONV <= k < T_SSM:
                    j = k - T_CONV
                    dve.wait_ge(a_done, A_ALL * g + A_BANKS + A_CQ + j + 1)
                    src = ready(V_CP + j, g)
                    if j == 0:
                        dve.tensor_copy(vbuf[:, :, 0:HALO], tails[:, :, 0:HALO])
                        step(dve.tensor_copy(vbuf[:, :, SOFF:SOFF + HALO], tails[:, :, HALO:2 * HALO]))
                    dve.tensor_tensor(vbuf[:, j, HALO:HALO + NP], src[:, 0:NP], sig[:, j % 2, 0:NP], ALU.mult)
                    dve.tensor_tensor(vbuf[:, j, SOFF + HALO:NV], src[:, NP:N], sig[:, j % 2, NP:N],
                                      ALU.mult).then_inc(v_done, 1)
                    if j == CT - 1:
                        emptied(V_CP + CT - 1, g)
                        dve.tensor_copy(tails[:, :, 0:HALO], vbuf[:, :, NP:NP + HALO])
                        step(dve.tensor_copy(tails[:, :, HALO:2 * HALO], vbuf[:, :, NV - HALO:NV]))
                if T_SSM <= k < T_SSM_END:
                    scan(2 * (k - T_SSM), g)
                    if k >= T_SSM + 2 and (k - T_SSM) % 2 == 0:
                        skip((k - T_SSM) // 2 - 1, g)
                    scan(2 * (k - T_SSM) + 1, g)
                if k == T_SSM_END:
                    skip(CT - 1, g)
                i = k - T_GLU
                if i == 1:
                    src = ready(V_MEAN, g)
                    for c in range(CT):
                        last = dve.tensor_tensor(acc[:, c, :], acc[:, c, :], src[:, 0:NC], ALU.subtract)
                    last.then_inc(v_done, 1)
                if i == 2:
                    src = ready(V_VAR, g)
                    dve.tensor_scalar(lnr[0][:, 0:NC], src[:, 0:NC], EPS, None, ALU.add).then_inc(v_done, 1)
                if i == 3:
                    dve.wait_ge(std_ready, g + 1)
                    step(dve.reciprocal(lnr[0][:, 0:NC], lnr[1][:, 0:NC]))
                    for c in range(CT):
                        last = dve.tensor_tensor(acc[:, c, :], acc[:, c, :], lnr[0][:, 0:NC], ALU.mult)
                    last.then_inc(ln_ready, 1)
                if 0 <= i < 4:
                    glu(2 * i, g)
                    glu(2 * i + 1, g)
                for tap_k in TAPS_OF.get(k, ()):
                    tap(tap_k)
                if i == 0:
                    dve.wait_ge(conv_ready, g + 1)
                    dve.sem_inc(v_passed, 1)
                if i == 3:
                    dve.wait_ge(ln_ready, g + 1)
                    for c in range(CT):
                        dve.wait_ge(ln_sig, CT * g + c + 1)
                        step(dve.tensor_scalar(acc[:, c, :], acc[:, c, :], par("ln_g")[:, c:c + 1],
                                               par("ln_b")[:, c:c + 1], ALU.mult, ALU.add))
                        dve.tensor_tensor(cs[:, c, 0:NP], acc[:, c, 0:NP], sq[:, c, 0:NP], ALU.mult)
                        dve.tensor_tensor(cs[:, c, NP:N], acc[:, c, SOFF:NC], sq[:, c, SOFF:NC],
                                          ALU.mult).then_inc(cs_ready, 1)
                if k == T_COUT:
                    for j in range(DT):
                        src = ready(V_COUT + j, g)
                        dve.tensor_tensor(rot[:, j % 2, :], src[:, 0:N], gates[:, DT + j, :], ALU.mult).then_inc(v_done, 1)
                        emptied(V_COUT + j, g)
                        dve.tensor_tensor(merged[:, j, :], merged[:, j, :], rot[:, j % 2, :], ALU.add).then_inc(merged_done, 1)
                if k == T_ROWS:
                    for t, (_, w) in enumerate(SPANS):
                        for h in range(2):
                            src = ready(V_TOK + 2 * t + h, g)
                            half_rows = xt[0:w, t, h * 512:(h + 1) * 512]
                            dve.tensor_tensor(half_rows, half_rows, src[0:w, :], ALU.add).then_inc(v_done, 1)
                    normalise(2, g)

            grid = [P, TOPK, TOPK]
            iota = par("iota")

            def key_top(n, a):
                dve.wait_ge(score_in[a], 16 * (n + 1))
                dve.sem_inc(v_passed, 1)
                for f in range(2):
                    s = sc[:, a, f * KEYS:(f + 1) * KEYS]
                    step(dve.max(topv[:, f, 0:8], s))
                    step(dve.max_index(topi[:, f, 0:8], topv[:, f, 0:8], s))
                    step(dve.match_replace(s, topv[:, f, 0:8], s, NEG))
                    step(dve.max(topv[:, f, 8:16], s))
                    step(dve.max_index(topi[:, f, 8:16], topv[:, f, 8:16], s))
                dve.sem_inc(score_used, 1)

            def choose(n, a):
                step(dve.tensor_tensor(cand[:, :, :], topv[:, 0, :].unsqueeze(2).to_broadcast(grid),
                                       topv[:, 1, :].unsqueeze(1).to_broadcast(grid), ALU.add))
                pairs = flat(cand[:, :, :])
                step(dve.max(best[:, 0:8], pairs))
                step(dve.max_index(pos[:, 0:8], best[:, 0:8], pairs))
                step(dve.match_replace(pairs, best[:, 0:8], pairs, NEG))
                step(dve.max(best[:, 8:16], pairs))
                dve.tensor_scalar(shifted[:, a, :], best[:, :], best[:, 0:1], None, ALU.subtract).then_inc(shift_done, 1)
                step(dve.max_index(pos[:, 8:16], best[:, 8:16], pairs))
                dve.tensor_scalar(hilo[:, 0, :], pos[:, :], 4, None, ALU.logical_shift_right)
                step(dve.tensor_scalar(hilo[:, 1, :], pos[:, :], TOPK - 1, None, ALU.bitwise_and))
                for f in range(2):
                    step(dve.tensor_tensor(hot[:, :, :], hilo[:, f, :].unsqueeze(2).to_broadcast(grid),
                                           iota.unsqueeze(1).to_broadcast(grid), ALU.is_equal))
                    step(dve.tensor_tensor(hot[:, :, :], hot[:, :, :],
                                           topi[:, f, :].unsqueeze(1).to_broadcast(grid), ALU.mult))
                    step(dve.tensor_reduce(part[:, f, :], hot[:, :, :], AXIS, ALU.add))
                dve.scalar_tensor_tensor(idx[:, a, :], part[:, 0, :], float(KEYS), part[:, 1, :],
                                         ALU.mult, ALU.add).then_inc(idx_ready, 1)

            def weights(n):
                dve.wait_ge(exp_done, n + 1)
                step(dve.tensor_reduce(den[:, 0, :], ex[:, :, :], AXIS, ALU.add))
                step(dve.reciprocal(den[:, 1, :], den[:, 0, :]))
                step(dve.tensor_tensor(soft[:, :, :], ex[:, :, :],
                                       den[:, 1, :].unsqueeze(2).to_broadcast([P, 2, TOPK]), ALU.mult))

            def coefficients(n, batch):
                dve.wait_ge(gelu_done, TB * QUARTERS * n + batch + 1)
                cols = slice(batch * BATCH, (batch + 1) * BATCH)
                dve.tensor_tensor(coef[:, cols], act_v[:, cols], flat(soft[:, :, :])[:, cols],
                                  ALU.mult).then_inc(coef_done, 1)

            here = [0]

            def quarter(n, q, last=False):
                if q == 0:
                    weights(n)
                for s in range(STEPS):
                    b = TB * q + s // BATCH
                    if s % BATCH == 1 and s > BATCH:
                        coefficients(n, b - 1)
                    c = STEPS * q + s
                    dve.wait_ge(landed[s], 16 * (QUARTERS * n + q + 1))
                    ins = dve.tensor_tensor_reduce(rows[:, s, 0:D], rows[:, s, 0:D], xn[:, here[0], :], 1.0, 0.0,
                                                   ALU.mult, ALU.add, dots[:, c:c + 1])
                    if s % BATCH == BATCH - 1:
                        ins.then_inc(dots_done, 1)
                coefficients(n, b)
                if not last:
                    (choose if q % 2 else key_top)(n + 1, q // 2)

            def start(t, b):
                here[0] = b
                dve.wait_ge(xn_in[b], 16 * (t - b) + 32)
                dve.tensor_tensor(xn[:, b, :], xn[:, b, :], gf[:, :], ALU.mult).then_inc(xn_ready, 1)
                dve.wait_ge(xn_ready, 1 * t + 1)
                dve.sem_inc(v_passed, 1)

            def end(t):
                dve.wait_ge(y_sq, 1 * t + 1)
                dve.tensor_scalar(fin[:, 1:2], fin[:, 0:1], 1.0 / D, EPS, ALU.mult, ALU.add).then_inc(y_ms, 1)
                dve.wait_ge(y_std, 1 * t + 1)
                step(dve.reciprocal(fin[:, 3:4], fin[:, 2:3]))
                dve.scalar_tensor_tensor(yt[:, :], flat(ps_acc[:, :, :]), fin[:, 3:4],
                                         gl[:, :], ALU.mult, ALU.mult).then_inc(y_ready, 1)

            setup_constants()
            dve.sem_inc(v_done, V_BANKS)
            dve.sem_inc(y_ready, 1)
            mix(0, 0)
            setup()
            for k in range(1, TURNS):
                if k == T_SSM:
                    dve.wait_ge(setup_t, 1)
                    dve.tensor_copy(bst[:, :, :, :].rearrange("p c t q -> p c (t q)"), ps_acc[:, :, :]).then_inc(setup_b, 1)
                mix(k, 0)
            dve.wait_ge(norms_in, 16)
            for a in range(2):
                key_top(0, a)
                choose(0, a)
            with dve.Fori(0, GROUPS - 1) as g:
                restart()
                for k in range(TURNS):
                    mix(k, g + 1)
                    if k == TURNS // 2:
                        end(2 * g)
                    if k % (TURNS // 2) == 0:
                        start(2 * g + k // (TURNS // 2), k // (TURNS // 2))
                    quarter(GPAIRS * g + k // QUARTERS, k % QUARTERS)
                    if k == TURNS - 1:
                        end(2 * g + 1)

            def v_quarter(n, q, last=False):
                if q == 0:
                    restart()
                quarter(n, q, last)

            last_tiles(dve, start, v_quarter, end)

        @block.gpsimd
        def _(pool):
            count = [0]

            def mark(ins):
                count[0] += 1
                ins.then_inc(p_chain, 1)
                return count[0]

            def rotate_back(j, g):
                pool.wait_ge(scanned, PAIRS * g + j + 1)
                b = j % 2
                c, s = trig[:, b, 0, :], trig[:, b, 1, :]
                mark(pool.tensor_tensor(prod[:, 0, :], grot[:, b, 0, :], c, ALU.mult))
                re = mark(pool.tensor_tensor(prod[:, 1, :], grot[:, b, 1, :], s, ALU.mult))
                pool.wait_ge(c_done, PAIRS * g + j + 1)
                pool.wait_ge(p_chain, re)
                first_half = mark(pool.tensor_tensor(hst[:, b, 0, :], prod[:, 0, :], prod[:, 1, :], ALU.subtract))
                pool.wait_ge(p_chain, first_half)
                mark(pool.tensor_tensor(prod[:, 0, :], grot[:, b, 0, :], s, ALU.mult))
                im = mark(pool.tensor_tensor(prod[:, 1, :], grot[:, b, 1, :], c, ALU.mult))
                pool.wait_ge(p_chain, im)
                end = mark(pool.tensor_tensor(hst[:, b, 1, :], prod[:, 0, :], prod[:, 1, :], ALU.add))
                pool.wait_ge(p_chain, end)
                pool.tensor_copy(carry[:, :, j, :], hst[:, b, :, NP - 1:N:NS]).then_inc(unrotated, 1)

            def mix(k, g):
                if k in (0, T_ROWS):
                    turn = 1 if k == 0 else 2
                    pool.wait_ge(ms_x, 2 * g + turn)
                    pool.tensor_tensor(rstd[:, :], rstd[:, :], half[:, 0:1].to_broadcast([P, 3]),
                                       ALU.pow).then_inc(rs_x, 1)
                if T_SSM <= k < T_SSM_END:
                    rotate_back(2 * (k - T_SSM), g)
                    rotate_back(2 * (k - T_SSM) + 1, g)

            def gather(n, q):
                a, k0 = q // 2, (q % 2) * STEPS
                for s in range(STEPS):
                    if s == 0 and k0 == 0:
                        pool.wait_ge(idx_ready, 2 * n + a + 1)
                    pool.wait_ge(slot_free, PAIR * n + STEPS * q + s + 1)
                    pool.sem_inc(gathers, 1)
                    pool.indirect_dma_start(
                        out=rows[:, s, :], out_offset=None, in_=experts,
                        in_offset=bass.IndirectOffsetOnAxis(ap=idx[:, a, k0 + s:k0 + s + 1], axis=0),
                    ).then_inc(landed[s], 16)

            def next_gathers(n, q, last=False):
                if q < QUARTERS - 1:
                    gather(n, q + 1)
                elif not last:
                    gather(n + 1, 0)

            pool.sem_inc(unrotated, PAIRS)
            pool.sem_inc(c_done, 2)
            for k in range(TURNS):
                mix(k, 0)
            gather(0, 0)
            with pool.Fori(0, GROUPS - 1) as g:
                pool.sem_clear(p_chain)
                count[0] = 0
                for k in range(TURNS):
                    mix(k, g + 1)
                    next_gathers(GPAIRS * g + k // QUARTERS, k % QUARTERS)
            last_tiles(pool, lambda t, b: None, next_gathers, lambda t: None)



def _lay_out(inputs):
    import numpy as np

    def a(name):
        return np.asarray(inputs[name])

    def state_major(x):
        return x.reshape(PAIRS, P).T

    def channel_major(x):
        return x.reshape(-1, P).T

    def tiles(w):
        k, m = w.shape
        return w.reshape(k // P, P, m // P, P).transpose(2, 1, 0, 3)

    fold = np.zeros((P, P), np.float32)
    fold[np.arange(P), np.arange(P) % DEC] = 1.0
    parts = {
        "lam_re": state_major(a("ssm_lambda_re")), "lam_im": state_major(a("ssm_lambda_im")),
        "log_step": state_major(np.repeat(a("ssm_log_step").reshape(-1), 64)),
        "h0_re": state_major(a("state_ssm_re")), "h0_im": state_major(a("state_ssm_im")),
        "b_re": a("ssm_b_re").reshape(PAIRS, P, SG).transpose(1, 0, 2).reshape(P, -1),
        "b_im": a("ssm_b_im").reshape(PAIRS, P, SG).transpose(1, 0, 2).reshape(P, -1),
        "c_re": a("ssm_c_re").reshape(PAIRS, 2, SG, 64).transpose(1, 3, 0, 2).reshape(P, -1),
        "c_im": a("ssm_c_im").reshape(PAIRS, 2, SG, 64).transpose(1, 3, 0, 2).reshape(P, -1),
        "d_skip": channel_major(a("ssm_d")), "norm_mix": channel_major(a("norm_mix")),
        "norm_ffn": channel_major(a("norm_ffn")), "b_gate": channel_major(a("b_gate")),
        "conv_w": a("conv_w").reshape(TAPS, CT, P).transpose(2, 1, 0).reshape(P, -1),
        "conv_b": channel_major(a("conv_b")), "ln_g": channel_major(a("conv_ln_g")),
        "ln_b": channel_major(a("conv_ln_b")),
        "cache": a("cache_conv").reshape(HALO, CT, P).transpose(2, 1, 0).reshape(P, -1),
        "eye": np.eye(P, dtype=np.float32), "fold": fold,
        "iota": np.tile(np.arange(TOPK, dtype=np.float32), (P, 1)),
        "keys": np.concatenate([a("peer_keys1")[0].T, a("peer_keys2")[0].T], axis=1),
    }
    kept = np.concatenate([parts[name] for name, _ in KEPT], axis=1)
    first = np.concatenate([parts[name] for name, _ in FIRST], axis=1)
    w_in = tiles(a("w_in")[0])
    glu = tiles(a("w_ssm_glu")[0])
    cout = tiles(a("w_conv_out")[0])
    order = [0, 1, 2, 3, 8, 4, 9, 5, 10, 6, 11, 7, *range(12, 28)]
    slabs = [w_in[m] for m in order]
    slabs += [np.concatenate([glu[DT + j], glu[j]], axis=1) for j in range(DT)]
    slabs += [np.concatenate([cout[2 * j], cout[2 * j + 1]], axis=1) for j in range(DT // 2)]
    slabs += list(tiles(a("w_out")[0])) + list(tiles(a("peer_w_q")[0]))
    slabs = np.stack([s.reshape(P, D) for s in slabs])
    return kept, first, slabs


def kernel(**inputs):
    import numpy as np
    import concourse.bacc as bacc
    from concourse.bass_utils import run_bass_kernel_spmd

    kept, first, slabs = _lay_out(inputs)
    experts = np.concatenate([np.asarray(inputs["peer_u"])[0], np.asarray(inputs["peer_v"])[0]], axis=1)
    arrays = {
        "in_x_prompt": np.asarray(inputs["x_prompt"]), "in_x_sample": np.asarray(inputs["x_sample"]),
        "in_kept": kept, "in_first": first, "in_slabs": slabs, "in_experts": experts,
        "in_g_ffn": np.asarray(inputs["norm_ffn"]), "in_g_final": np.asarray(inputs["norm_final"]).reshape(1, D),
    }
    arrays = {k: np.ascontiguousarray(v) for k, v in arrays.items()}
    outs = {"out_y_prompt": (1, SEQ, D), "out_y_sample": (1, DEC, D), "out_ssm": (P, 4 * PAIRS),
            "out_conv": (P, 2 * CT * HALO)}

    nc = bacc.Bacc("TRN2", target_bir_lowering=False, num_devices=1)
    d = {k: nc.dram_tensor(k, v.shape, F32, kind="ExternalInput").ap() for k, v in arrays.items()}
    d |= {k: nc.dram_tensor(k, s, F32, kind="ExternalOutput").ap() for k, s in outs.items()}
    x2_d = nc.dram_tensor("x2_rows", (SEQ + DEC, D), F32, kind="Internal").ap()
    xh_d = nc.dram_tensor("xh_rows", (SEQ + DEC, D), F32, kind="Internal").ap()
    score_d = nc.dram_tensor("score_rows", (BLOCKS, P, 2 * KEYS), F32, kind="Internal").ap()
    trig_d = nc.dram_tensor("trig_rows", (PAIRS, P, 2 * N), F32, kind="Internal").ap()
    program(nc, d["in_x_prompt"], d["in_x_sample"], d["in_kept"], d["in_first"], d["in_slabs"], d["in_experts"],
            d["in_g_ffn"], d["in_g_final"], x2_d, xh_d, score_d, trig_d,
            d["out_y_prompt"], d["out_y_sample"], d["out_ssm"], d["out_conv"])
    r = run_bass_kernel_spmd(nc, [arrays], core_ids=[0]).results[0]

    ssm = np.asarray(r["out_ssm"]).reshape(P, 2, PAIRS, 2).transpose(3, 1, 2, 0).reshape(2, 2, 1, 1, 2 * PAIRS, 64)
    conv = np.asarray(r["out_conv"]).reshape(P, CT, 2, HALO).transpose(2, 3, 1, 0).reshape(2, 1, 1, HALO, DC)
    return (r["out_y_prompt"], r["out_y_sample"], ssm[0, 0], ssm[0, 1], conv[0], ssm[1, 0], ssm[1, 1], conv[1])
```

```python
from contextlib import ExitStack

import concourse.bass as bass
from concourse import mybir

F32 = mybir.dt.float32
U32 = mybir.dt.uint32
ALU = mybir.AluOpType
ACT = mybir.ActivationFunctionType
AXIS = mybir.AxisListType.X

P = 128
D = 1024
DT = D // P
SEQ, DEC = 1024, 64
GROUPS = 4
NP, NS = SEQ // GROUPS, DEC // GROUPS
N = NP + NS
SPANS = ((0, P), (P, P), (NP, NS))
DC = 512
CT = DC // P
PAIRS = 16
SG = 16
TRIGS = 4
TAPS = 31
HALO = TAPS - 1
NV = HALO + NP + HALO + NS
NC = NV - HALO
SOFF = NP + HALO
HEADS, KEYS, TOPK = 8, 128, 16
EPS = 1e-6
NEG = -3.0e38

TURNS = 64
STEPS = 4
PAIR = 2 * TOPK
PTURNS = PAIR // STEPS
TPAIRS = HEADS // 2
SPAIRS = HEADS // 4
TILES = SEQ // P
GPAIRS = 2 * TPAIRS
RING = 2 * STEPS
BATCH = 2
TB = STEPS // BATCH
PB = PAIR // BATCH
BLOCKS = TILES * HEADS + HEADS // 2

SLABS = 64
SLOTS = 4
S_CONV, S_GATE, S_GLU, S_COUT, S_OUT, S_Q = 4, 12, 28, 36, 40, 48

T_X = 0
T_XN, T_U, T_CONV = 3, 4, 6
T_SSM = 10
T_GELU, T_GLU = 27, 28
T_MEAN, T_VAR = 32, 34
T_LN, T_SWISH, T_COUT = 36, 37, 37
T_OUT, T_ROWS = 41, 45
T_SQ, T_XN2, T_Q = 48, 50, 51
TAPS_OF = {T_SSM + j: (j,) for j in range(PAIRS)}
TAPS_OF |= {26: (16, 17, 18), 27: (19, 20, 21), 28: (22, 23, 24), 29: (25, 26), 30: (27, 28), 31: (29, 30)}
OUT_OF = {T_OUT + i: (2 * i, 2 * i + 1) for i in range(4)}
Q_OF = {T_Q: (0, 1), T_Q + 1: (2, 3), T_Q + 2: (4,), T_Q + 3: (5,), T_Q + 4: (6,), T_Q + 5: (7, 8)}
Q_OF |= {T_Q + 6 + i: (9 + i,) for i in range(7)}
SLABS_OF = {T_U: (0, 1), T_U + 1: (2, 3)}
SLABS_OF |= {T_CONV + j: (S_CONV + 2 * j, S_CONV + 2 * j + 1) for j in range(CT)}
SLABS_OF |= {T_SSM + j: (S_GATE + j,) for j in range(PAIRS)}
SLABS_OF |= {T_GLU + i: (S_GLU + 2 * i, S_GLU + 2 * i + 1) for i in range(DT // 2)}
SLABS_OF |= {T_COUT + i: (S_COUT + i,) for i in range(4)}
SLABS_OF |= {k: tuple(S_OUT + m for m in ms) for k, ms in OUT_OF.items()}
SLABS_OF |= {k: tuple(S_Q + m for m in ms) for k, ms in Q_OF.items()}

HEAD_LOADS = {TURNS - 10: 0, TURNS - 7: 1, TURNS - 2: 2}

A_XN, A_U, A_CQ, A_GATE, A_GLU, A_OUT, A_XN2, A_Q = 0, 8, 12, 16, 32, 40, 48, 56
A_ALL = 88
A_BANKS = 2
V_CP, V_B, V_GLU, V_MEAN, V_VAR, V_COUT, V_TOK = 0, 4, 36, 44, 45, 46, 54
V_ALL = 60
V_BANKS = 3


def a_q(m):
    return A_Q if m == 0 else A_Q - 1 + 2 * m


def a_score(m):
    return A_Q + 2 + 2 * m if m < 15 else A_ALL - 1


def layout(widths):
    out, at = {}, 0
    for name, w in widths:
        out[name] = (at, w)
        at += w
    return out, at


KEPT = [("d_skip", CT), ("norm_mix", DT), ("norm_ffn", DT), ("b_gate", 2 * DT), ("conv_w", CT * TAPS),
        ("conv_b", CT), ("ln_g", CT), ("ln_b", CT), ("cache", CT * HALO), ("eye", P), ("fold", P),
        ("iota", TOPK), ("keys", 2 * KEYS)]
FIRST = [("lam_re", PAIRS), ("lam_im", PAIRS), ("log_step", PAIRS), ("h0_re", PAIRS), ("h0_im", PAIRS),
         ("b_re", PAIRS * SG), ("b_im", PAIRS * SG), ("c_re", PAIRS * SG), ("c_im", PAIRS * SG)]
KEPT_AT, KEPT_W = layout(KEPT)
FIRST_AT, FIRST_W = layout(FIRST)


def program(nc, x_prompt, x_sample, kept, first, slabs, experts, g_ffn, g_final, x2_d, rs_d, score_d, trig_d,
            y_prompt, y_sample, ssm_out, conv_out):
    with ExitStack() as ctx:
        def sb(name, shape, dt=F32):
            return ctx.enter_context(nc.sbuf_tensor(name, shape, dt))

        def sem(name):
            return ctx.enter_context(nc.semaphore(name))

        def flat(ap):
            return ap.rearrange("p a b -> p (a b)")

        pk = sb("pk", [P, KEPT_W])

        def par(name):
            a, w = KEPT_AT[name]
            return pk[:, a:a + w]

        ring = sb("ring", [P, SLOTS, D])
        xt = sb("xt", [P, 3, D])
        xnT = sb("xnT", [P, DT, N])
        merged = xnT
        gates = sb("gates", [P, 2 * DT, N])
        outT = gates[:, 0:DT, :]
        va = sb("va", [P, CT * (NV + NC)])
        vbuf = va[:, 0:CT * NV].rearrange("p (c n) -> p c n", c=CT)
        acc = va[:, CT * NV:].rearrange("p (c n) -> p c n", c=CT)
        xh = [va[:, 0:D], va[:, D:2 * D], flat(gates[:, :, :])[0:NS, DT * N:DT * N + D]]
        uy = sb("uy", [P, 2 * CT, N])
        uT, yT = uy[:, 0:CT, :], uy[:, CT:2 * CT, :]
        cs = yT
        scsb = flat(uy[:, :, :])[:, 0:2 * 3 * 2 * KEYS].rearrange("p (b t c) -> p b t c", b=2, t=3)
        tails = sb("tails", [P, CT, 2 * HALO])
        trig = sb("trig", [P, TRIGS, 2, N])
        rot = sb("rot", [P, 2, N])
        rin = sb("rin", [P, 2, N])
        gp = sb("gp", [P, 6 * N])
        grot = gp[:, 0:4 * N].rearrange("p (b c n) -> p b c n", b=2, c=2)
        prod = gp[:, 4 * N:6 * N].rearrange("p (c n) -> p c n", c=2)
        sq = gp[:, 0:CT * NC].rearrange("p (c n) -> p c n", c=CT)
        hst = sb("hst", [P, 2, 2, N])
        lnr = flat(hst[:, 0, :, :]), flat(hst[:, 1, :, :])
        carry = sb("carry", [P, 2, PAIRS, 2])
        sig = sb("sig", [P, 2, N])
        qT = sig
        rho = sb("rho", [P, PAIRS])
        bst = sb("bst", [P, 2, CT, P])
        cst = sb("cst", [P, 2, PAIRS, 2 * SG])
        mean_w = sb("mean_w", [P, P])
        ssq = sb("ssq", [P, 3])
        rstd = sb("rstd", [P, 3])
        half = sb("half", [P, 1])
        gf = sb("gf", [P, D])
        gl = sb("gl", [P, D])
        rows = sb("rows", [P, RING, 2 * D])
        x2t = sb("x2t", [P, D])
        xn = sb("xn", [P, D])
        rst = sb("rst", [P, 1])
        yt = sb("yt", [P, D])
        sc = sb("sc", [P, 2, 2 * KEYS])
        topv = sb("topv", [P, 2, TOPK])
        topi = sb("topi", [P, 2, TOPK], U32)
        cand = sb("cand", [P, TOPK, TOPK])
        best = sb("best", [P, TOPK])
        pos = sb("pos", [P, TOPK], U32)
        hilo = sb("hilo", [P, 2, TOPK], U32)
        hot = cand
        part = sb("part", [P, 2, TOPK])
        idx = sb("idx", [P, 2, TOPK], U32)
        shifted = sb("shifted", [P, 2, TOPK])
        ex = sb("ex", [P, 2, TOPK])
        den = sb("den", [P, 2, 2])
        soft = sb("soft", [P, 2, TOPK])
        dots = sb("dots", [P, PAIR])
        act_v = sb("act_v", [P, PAIR])
        coef = sb("coef", [P, PAIR])
        diag = sb("diag", [P, RING, P])
        fin = sb("fin", [P, 4])
        spare = rows[:, :, :].rearrange("p a b -> p (a b)")
        table = spare[:, 0:PAIRS * 2 * N].rearrange("p (j c n) -> p j c n", j=PAIRS, c=2)
        cosT, sinT = table[:, :, 0, :], table[:, :, 1, :]
        flat_table = spare[:, 0:PAIRS * 2 * N].rearrange("p (j m) -> p j m", j=PAIRS)
        scratch = spare[:, 10 * D:14 * D]
        sm = spare[:, 9 * D:9 * D + 13 * PAIRS].rearrange("p (a b) -> p a b", a=13)
        pf = spare[:, 14 * D:14 * D + FIRST_W]
        bpad = flat(gates[:, :, :])[:, 0:2 * PAIRS * 2 * SG].rearrange("p (c j h) -> p c j h", c=2, j=PAIRS)

        def par1(name):
            a, w = FIRST_AT[name]
            return pf[:, a:a + w]

        ps_a = ctx.enter_context(nc.psum_tensor("ps_a", [P, A_BANKS, 512], F32))
        ps_v = ctx.enter_context(nc.psum_tensor("ps_v", [P, V_BANKS, 512], F32))
        ps_y = ctx.enter_context(nc.psum_tensor("ps_y", [P, 512], F32))
        ps_acc = ctx.enter_context(nc.psum_tensor("ps_acc", [P, 2, 512], F32))

        kept_in = sem("kept_in")
        first_in = sem("first_in")
        norms_in = sem("norms_in")
        slab_in = [sem(f"slab_in{i}") for i in range(SLOTS)]
        trig_in = [sem(f"trig_in{i}") for i in range(TRIGS)]
        trig_stored = sem("trig_stored")
        x_in = sem("x_in")
        a_ready = sem("a_ready")
        a_done = sem("a_done")
        v_ready = sem("v_ready")
        v_done = sem("v_done")
        c_done = sem("c_done")
        y_summed = sem("y_summed")
        y_gelu = sem("y_gelu")
        merged_done = sem("merged_done")
        setup_v = sem("setup_v")
        setup_a = sem("setup_a")
        setup_t = sem("setup_t")
        setup_b = sem("setup_b")
        table_done = sem("table_done")
        sq_x = sem("sq_x")
        ms_x = sem("ms_x")
        rs_x = sem("rs_x")
        xh_ready = sem("xh_ready")
        scanned = sem("scanned")
        unrotated = sem("unrotated")
        conv_ready = sem("conv_ready")
        xc_sq = sem("xc_sq")
        std_ready = sem("std_ready")
        ln_ready = sem("ln_ready")
        ln_sig = sem("ln_sig")
        cs_ready = sem("cs_ready")
        rows_out = sem("rows_out")
        rs_out = sem("rs_out")
        score_out = [sem(f"score_out{i}") for i in range(2)]
        state_out = sem("state_out")
        v_chain = sem("v_chain")
        v_passed = sem("v_passed")
        p_chain = sem("p_chain")
        x2_in = sem("x2_in")
        rs_in = sem("rs_in")
        score_in = [sem(f"score_in{i}") for i in range(2)]
        score_used = sem("score_used")
        xn_ready = sem("xn_ready")
        cleared = sem("cleared")
        sp_passed = sem("sp_passed")
        acc_begun = sem("acc_begun")
        idx_ready = sem("idx_ready")
        landed = [sem(f"landed{i}") for i in range(RING)]
        slot_free = sem("slot_free")
        gathers = sem("gathers")
        dots_done = sem("dots_done")
        gelu_done = sem("gelu_done")
        coef_done = sem("coef_done")
        diag_done = sem("diag_done")
        shift_done = sem("shift_done")
        exp_done = sem("exp_done")
        y_sq = sem("y_sq")
        y_ms = sem("y_ms")
        y_std = sem("y_std")
        y_ready = sem("y_ready")
        y_out = sem("y_out")
        block = ctx.enter_context(nc.Block())

        SEGS = ((0, NP), (NP, N))
        xp_rows = x_prompt.rearrange("b (g t p) d -> (b g) p t d", g=GROUPS, p=P)
        xs_rows = x_sample.rearrange("b (g p) d -> (b g) p d", g=GROUPS)
        x2_g = x2_d[0:SEQ, :].rearrange("(g t p) d -> g p t d", g=GROUPS, p=P)
        rs_g = rs_d[0:SEQ, :].rearrange("(g t p) o -> g t p o", g=GROUPS, p=P)
        x2_s = x2_d[SEQ:SEQ + DEC, :].rearrange("(g p) d -> g p d", g=GROUPS)
        rs_s = rs_d[SEQ:SEQ + DEC, :].rearrange("(g p) o -> g p o", g=GROUPS)
        x2_t = x2_d[0:SEQ, :].rearrange("(t p) d -> t p d", p=P)
        rs_t = rs_d[0:SEQ, :].rearrange("(t p) o -> t p o", p=P)
        y_t = y_prompt.rearrange("b (t p) d -> (b t) p d", p=P)
        sc_g = score_d[0:TILES * HEADS].rearrange("(g t h) p c -> g h p t c", g=GROUPS, h=HEADS)
        sc_s = score_d[TILES * HEADS:BLOCKS].rearrange("k (f g p) c -> g f k p c", f=2, g=GROUPS)


        def loads_of(t):
            return 16 * (TILES + 2) if isinstance(t, int) and t == TILES else 16 * t + 16

        def angles(j, g):
            pair = table[:, j] if isinstance(g, int) else trig[:, j % TRIGS]
            return pair[:, 0, :], pair[:, 1, :]

        def last_tiles(eng, start, peer, end):
            for t in (TILES - 2, TILES - 1):
                start(t)
                with eng.Fori(0, TPAIRS) as i:
                    for r in range(PTURNS):
                        peer(t * TPAIRS + i, r)
                end(t)
            start(TILES)
            for i in range(SPAIRS):
                for r in range(PTURNS):
                    peer(TILES * TPAIRS + i, r, last=i == SPAIRS - 1)
            end(TILES)

        @block.sync
        def _(sp):
            def pass_wait():
                sp.sem_inc(sp_passed, 1)

            def slab_through(s, g):
                if s < S_CONV:
                    sp.wait_ge(a_ready, A_ALL * g + A_U + s + 1)
                elif s < S_GATE:
                    j, second = divmod(s - S_CONV, 2)
                    if second:
                        sp.wait_ge(v_ready, V_ALL * g + V_CP + j + 1)
                    else:
                        sp.wait_ge(a_ready, A_ALL * g + A_CQ + j + 1)
                elif s < S_GLU:
                    sp.wait_ge(a_ready, A_ALL * g + A_GATE + s - S_GATE + 1)
                elif s < S_COUT:
                    sp.wait_ge(v_ready, V_ALL * g + V_GLU + s - S_GLU + 1)
                elif s < S_OUT:
                    sp.wait_ge(v_ready, V_ALL * g + V_COUT + 2 * (s - S_COUT) + 2)
                elif s < S_Q:
                    sp.wait_ge(a_ready, A_ALL * g + A_OUT + s - S_OUT + 1)
                else:
                    sp.wait_ge(a_ready, A_ALL * g + a_q(s - S_Q) + 1)

            def load_x(g):
                sp.dma_start(xt[:, 0:2, :], xp_rows[g]).then_inc(x_in, 16)
                sp.dma_start(xt[0:NS, 2, :], xs_rows[g]).then_inc(x_in, 16)

            def load_trig(j):
                sp.dma_start(flat(trig[:, j % TRIGS, :, :]), trig_d[j]).then_inc(trig_in[j % TRIGS], 16)

            def mix(k, g):
                for s in SLABS_OF.get(k, ()):
                    slab_through(s, g)
                    sp.dma_start(ring[:, s % SLOTS, :], slabs[(s + SLOTS) % SLABS]).then_inc(slab_in[s % SLOTS], 16)
                if T_SSM <= k < T_SSM + PAIRS and not isinstance(g, int):
                    j = k - T_SSM
                    sp.wait_ge(unrotated, PAIRS * g + PAIRS + j + 1)
                    pass_wait()
                    load_trig((j + TRIGS) % PAIRS)
                if k == T_Q + 6:
                    sp.wait_ge(rows_out, 32 * (g + 1))
                    pass_wait()
                    sp.wait_ge(rs_out, 48 * (g + 1))
                    pass_wait()
                    load_x((g + 1) % GROUPS)

            def load_scores(n, a):
                sp.dma_start(sc[:, a, :], score_d[2 * n + a]).then_inc(score_in[a], 16)

            def rows_free(t):
                sp.wait_ge(acc_begun, t + 1)
                pass_wait()
                sp.wait_ge(xn_ready, t + 1)
                pass_wait()

            def load_rows(t):
                rows_free(t)
                sp.dma_start(x2t[:, :], x2_t[t]).then_inc(x2_in, 16)
                sp.dma_start(rst[:, :], rs_t[t]).then_inc(rs_in, 16)

            def peer(n, r, last=False):
                if r == 1 and not last:
                    sp.wait_ge(score_used, 2 * n + 2)
                    pass_wait()
                    load_scores(n + 1, 1)
                if r == 6 and not (isinstance(n, int) and n >= TILES * TPAIRS):
                    sp.wait_ge(score_used, 2 * n + 3)
                    pass_wait()
                    load_scores(n + 2, 0)

            def store(t):
                sp.wait_ge(y_ready, t + 2)
                pass_wait()
                sp.dma_start(y_t[t], yt[:, :]).then_inc(y_out, 16)

            load_x(0)
            sp.dma_start(pk[:, :], kept).then_inc(kept_in, 16)
            sp.dma_start(pf, first).then_inc(first_in, 16)
            for s in range(SLOTS):
                sp.dma_start(ring[:, s, :], slabs[s]).then_inc(slab_in[s], 16)
            sp.dma_start(gf[:, :], g_ffn.broadcast_to([P, D])).then_inc(norms_in, 16)
            sp.dma_start(gl[:, :], g_final.broadcast_to([P, D])).then_inc(y_out, 16)
            for k in range(TURNS):
                if k == T_GLU:
                    sp.wait_ge(table_done, 1)
                    sp.dma_start(trig_d.rearrange("j p m -> p j m"), flat_table).then_inc(trig_stored, 16)
                if k == T_COUT:
                    sp.wait_ge(trig_stored, 16)
                    for j in range(TRIGS):
                        load_trig(j)
                mix(k, 0)
                if k == T_Q + 3:
                    for b in range(2):
                        sp.wait_ge(score_out[b], 32)
                        load_scores(0, b)
                if k == T_Q + 4:
                    sp.wait_ge(rows_out, 32)
                    sp.wait_ge(rs_out, 48)
                    load_rows(0)
                if k == TURNS - 1:
                    sp.wait_ge(score_used, 1)
                    sp.wait_ge(score_out[0], 64)
                    load_scores(1, 0)

            with sp.Fori(0, GROUPS - 1) as g:
                for k in range(TURNS):
                    mix(k, g + 1)
                    if k == 0:
                        load_rows(2 * g + 1)
                    if k == 1:
                        sp.wait_ge(score_out[1], 128 * g + 64)
                        pass_wait()
                    if k == 5:
                        for b in range(2):
                            sp.wait_ge(score_out[b], 128 * g + 128)
                            pass_wait()
                    if k in HEAD_LOADS:
                        h = HEAD_LOADS[k]
                        sp.wait_ge(score_out[h % 2], 128 * g + 128 + 32 * (h // 2 + 1))
                        pass_wait()
                    if k == T_Q + 3:
                        sp.wait_ge(rows_out, 32 * (g + 2))
                        pass_wait()
                        sp.wait_ge(rs_out, 48 * (g + 2))
                        pass_wait()
                        load_rows(2 * g + 2)
                    peer(GPAIRS * g + k // PTURNS, k % PTURNS)
                    if k == TURNS // 2:
                        store(2 * g)
                    if k == TURNS - 1:
                        store(2 * g + 1)

            sp.wait_ge(unrotated, PAIRS * (GROUPS + 1))
            sp.dma_start(ssm_out, carry[:, :, :, :].rearrange("p a b c -> p (a b c)")).then_inc(state_out, 16)
            sp.wait_ge(conv_ready, GROUPS)
            sp.dma_start(conv_out, flat(tails[:, :, :])).then_inc(state_out, 16)
            for b in range(2):
                sp.wait_ge(score_out[b], 128 * GROUPS)

            def start(t):
                if t == TILES - 2:
                    load_rows(t + 1)
                if t == TILES - 1:
                    rows_free(t + 1)
                    for f in range(2):
                        half_tile = slice(f * DEC, (f + 1) * DEC)
                        sp.dma_start(x2t[half_tile, :], x2_d[SEQ:SEQ + DEC, :]).then_inc(x2_in, 16)
                        sp.dma_start(rst[half_tile, :], rs_d[SEQ:SEQ + DEC, :]).then_inc(rs_in, 16)

            def end(t):
                if t == TILES:
                    sp.wait_ge(y_ready, t + 2)
                    pass_wait()
                    sp.dma_start(y_sample.rearrange("b p d -> (b p) d"), yt[0:DEC, :]).then_inc(y_out, 16)
                else:
                    store(t)

            last_tiles(sp, start, peer, end)
            sp.wait_ge(y_out, 16 * (TILES + 2))
            sp.wait_ge(state_out, 32)
            for i in range(SLOTS):
                sp.wait_ge(slab_in[i], 16 * (1 + GROUPS * SLABS // SLOTS))
            for i in range(TRIGS):
                sp.wait_ge(trig_in[i], 16 * (1 + (GROUPS - 1) * PAIRS // TRIGS))
            sp.wait_ge(x_in, 32 * (1 + GROUPS))

        @block.tensor
        def _(pe):
            eye = par("eye")

            def a_tile(n, g):
                pe.wait_ge(a_done, A_ALL * g + n + 1)
                return ps_a[:, n % A_BANKS, :]

            def a_emptied(n, g):
                pe.wait_ge(a_done, A_ALL * g + n + 1 + A_BANKS)

            def v_tile(n, g):
                pe.wait_ge(v_done, V_ALL * g + n + 1)
                return ps_v[:, n % V_BANKS, :]

            def slab(s, g):
                pe.wait_ge(slab_in[s % SLOTS], 16 * ((SLABS // SLOTS) * g + s // SLOTS + 1))

            def product(out, s, k0, rhs):
                kt = rhs.shape[1]
                for k in range(kt):
                    w = ring[:, s % SLOTS, (k0 + k) * P:(k0 + k + 1) * P]
                    last = pe.matmul(out[:, 0:N], w, rhs[:, k, :], start=(k == 0), stop=(k == kt - 1))
                return last

            def to_channels(n0, turn, g):
                pe.wait_ge(xh_ready, 2 * g + turn)
                for k in range(DT):
                    out = a_tile(n0 + k, g)
                    for t in range(2):
                        pe.transpose(out[:, t * P:(t + 1) * P], xh[t][:, k * P:(k + 1) * P], eye)
                    pe.transpose(out[:, NP:N], xh[2][:, k * P:(k + 1) * P], eye[0:NS, 0:NS]).then_inc(a_ready, 1)
                a_emptied(n0 + DT - 1, g)

            def b_product(j, g):
                q, t = 32 * (j % 4), j // 4
                for c in range(2):
                    out = v_tile(V_B + 2 * j + c, g)
                    pe.matmul(out[:, 0:N], bst[q:q + 32, c, t, :], uT[q:q + 32, t, :],
                              start=True, stop=True).then_inc(v_ready, 1)

            def c_product(j, g):
                q, t = 32 * (j % 4), j // 4
                if j % 4 == 0 and t:
                    pe.wait_ge(y_summed, CT * g + t)
                pe.wait_ge(unrotated, PAIRS * g + PAIRS + j + 1)
                for c in range(2):
                    last = pe.matmul(ps_y[q:q + 32, 0:N], cst[:, c, j, :], hst[:, j % 2, c, :],
                                     start=(c == 0), stop=(c == 1))
                last.then_inc(c_done, 1)

            def gate(j, g):
                out = a_tile(A_GATE + j, g)
                slab(S_GATE + j, g)
                product(out, S_GATE + j, 0, xnT[:, :, :]).then_inc(a_ready, 1)

            def channel_mean(n, src, g):
                out = v_tile(n, g)
                for c in range(CT):
                    last = pe.matmul(out[:, 0:NC], mean_w[:, :], src[:, c, :], start=(c == 0), stop=(c == CT - 1))
                last.then_inc(v_ready, 1)

            def glu(j, g):
                out = a_tile(A_GLU + j, g)
                slab(S_GLU + j, g)
                product(out, S_GLU + j, 0, yT[:, :, :]).then_inc(a_ready, 1)
                out = v_tile(V_GLU + j, g)
                product(out, S_GLU + j, CT, yT[:, :, :]).then_inc(v_ready, 1)

            def scores(m, g):
                out = a_tile(a_score(m), g)
                a_emptied(a_q(m), g)
                keys = par("keys")[:, (m % 2) * KEYS:(m % 2 + 1) * KEYS]
                for t, (n, width) in enumerate(SPANS):
                    last = pe.matmul(out[0:width, t * KEYS:(t + 1) * KEYS], qT[:, m % 2, n:n + width], keys,
                                     start=True, stop=True)
                last.then_inc(a_ready, 1)

            def mix(k, g):
                if k == T_XN:
                    to_channels(A_XN, 1, g)
                if k in (T_U, T_U + 1):
                    for m in SLABS_OF[k]:
                        out = a_tile(A_U + m, g)
                        slab(m, g)
                        product(out, m, 0, xnT[:, :, :]).then_inc(a_ready, 1)
                if T_CONV <= k < T_SSM:
                    j = k - T_CONV
                    out = a_tile(A_CQ + j, g)
                    slab(S_CONV + 2 * j, g)
                    product(out, S_CONV + 2 * j, 0, xnT[:, :, :]).then_inc(a_ready, 1)
                    out = v_tile(V_CP + j, g)
                    slab(S_CONV + 2 * j + 1, g)
                    product(out, S_CONV + 2 * j + 1, 0, xnT[:, :, :]).then_inc(v_ready, 1)
                if T_SSM <= k < T_SSM + PAIRS:
                    gate(k - T_SSM, g)
                if T_SSM - 1 <= k < T_SSM + PAIRS - 1:
                    if k == T_SSM - 1:
                        a_emptied(A_U + CT - 1, g)
                    b_product(k - T_SSM + 1, g)
                if T_SSM < k <= T_SSM + PAIRS:
                    c_product(k - T_SSM - 1, g)
                if T_GLU <= k < T_GLU + 4:
                    if k == T_GLU:
                        pe.wait_ge(y_gelu, CT * (g + 1))
                    glu(2 * (k - T_GLU), g)
                    glu(2 * (k - T_GLU) + 1, g)
                if k == T_MEAN:
                    pe.wait_ge(conv_ready, g + 1)
                    channel_mean(V_MEAN, acc, g)
                if k == T_VAR:
                    pe.wait_ge(xc_sq, g + 1)
                    channel_mean(V_VAR, sq, g)
                if T_COUT <= k < T_COUT + 4:
                    if k == T_COUT:
                        pe.wait_ge(cs_ready, CT * (g + 1))
                    for j in range(2 * (k - T_COUT), 2 * (k - T_COUT) + 2):
                        out = v_tile(V_COUT + j, g)
                        if j % 2 == 0:
                            slab(S_COUT + j // 2, g)
                        product(out, S_COUT + j // 2, CT * (j % 2), cs[:, :, :]).then_inc(v_ready, 1)
                for j in OUT_OF.get(k, ()):
                    if j == 0:
                        pe.wait_ge(merged_done, DT * (g + 1))
                    out = a_tile(A_OUT + j, g)
                    slab(S_OUT + j, g)
                    product(out, S_OUT + j, 0, merged[:, :, :]).then_inc(a_ready, 1)
                if T_ROWS <= k < T_ROWS + 3:
                    if k == T_ROWS:
                        a_emptied(A_OUT + DT - 1, g)
                    t, (n, width) = k - T_ROWS, SPANS[k - T_ROWS]
                    for h in range(2):
                        out = v_tile(V_TOK + 2 * t + h, g)
                        for m in range(4):
                            last = pe.transpose(out[0:width, m * P:(m + 1) * P], outT[:, 4 * h + m, n:n + width], eye)
                        last.then_inc(v_ready, 1)
                if k == T_XN2:
                    to_channels(A_XN2, 2, g)
                for m in Q_OF.get(k, ()):
                    out = a_tile(a_q(m), g)
                    slab(S_Q + m, g)
                    product(out, S_Q + m, 0, xnT[:, :, :]).then_inc(a_ready, 1)
                    if m:
                        scores(m - 1, g)
                if k == TURNS - 1:
                    scores(2 * HEADS - 1, g)

            def start(t):
                w = DEC if isinstance(t, int) and t == TILES else P
                pe.wait_ge(x2_in, loads_of(t))
                pe.wait_ge(y_ready, t + 1)
                for h in range(2):
                    last = pe.matmul(ps_acc[:, h, :], eye[0:w, :], x2t[0:w, h * 512:(h + 1) * 512],
                                     start=True, stop=False, skip_group_check=True)
                last.then_inc(acc_begun, 1)

            def peer(n, r, last=False):
                for s in range(STEPS * r, STEPS * r + STEPS):
                    slot = s % RING
                    pe.wait_ge(diag_done, PAIR * n + s + 1)
                    for h in range(2):
                        ins = pe.matmul(ps_acc[:, h, :], diag[:, slot, :], rows[:, slot, D + h * 512:D + (h + 1) * 512],
                                        start=False, stop=False, skip_group_check=True)
                    ins.then_inc(slot_free, 1)

            pe.wait_ge(kept_in, 16)
            pe.sem_inc(slot_free, RING)
            pe.sem_inc(acc_begun, 1)
            for k in range(TURNS):
                if k == T_SSM - 1:
                    pe.wait_ge(setup_v, 3)
                    for c in range(2):
                        for t in range(CT):
                            last = pe.transpose(ps_acc[:, c, t * P:(t + 1) * P],
                                                bpad[:, c, 4 * t:4 * t + 4, :].rearrange("p a b -> p (a b)"), eye)
                    last.then_inc(setup_t, 1)
                    pe.wait_ge(setup_b, 1)
                mix(k, 0)
            with pe.Fori(0, GROUPS - 1) as g:
                for k in range(TURNS):
                    mix(k, g + 1)
                    if k % (TURNS // 2) == 0:
                        start(2 * g + k // (TURNS // 2))
                    peer(GPAIRS * g + k // PTURNS, k % PTURNS)
            last_tiles(pe, start, peer, lambda t: None)

        @block.scalar
        def _(act):
            def ready(n, g):
                act.wait_ge(a_ready, A_ALL * g + n + 1)
                return ps_a[:, n % A_BANKS, :]

            def squares():
                act.activation(flat(merged[:, :, :])[:, 0:D], xt[:, 0, :], ACT.Square, accum_out=ssq[:, 0:1])
                act.activation(flat(merged[:, :, :])[:, D:2 * D], xt[:, 1, :], ACT.Square, accum_out=ssq[:, 1:2])
                act.activation(gp[0:NS, 0:D], xt[0:NS, 2, :], ACT.Square, accum_out=ssq[0:NS, 2:3]).then_inc(sq_x, 1)

            def to_channels(n0, name, g):
                for k in range(DT):
                    act.activation(xnT[:, k, :], ready(n0 + k, g)[:, 0:N], ACT.Copy,
                                   scale=par(name)[:, k:k + 1]).then_inc(a_done, 1)

            def v_emptied(n, g):
                act.wait_ge(v_done, V_ALL * g + V_BANKS + n + 1)

            def glu(j, g):
                if j >= 2:
                    v_emptied(V_GLU + j - 2, g)
                act.activation(sig[:, j % 2, :], ready(A_GLU + j, g)[:, 0:N], ACT.Sigmoid).then_inc(a_done, 1)

            def keep_scores(m, g):
                h, b = m // 2, (m // 2) % 2
                cols = slice((m % 2) * KEYS, (m % 2 + 1) * KEYS)
                if m % 2 == 0 and h >= 2:
                    act.wait_ge(score_out[b], 128 * g + 32 * (h // 2))
                src = ready(a_score(m), g)
                act.activation(scsb[:, b, 0:2, cols], src[:, 0:2 * KEYS].rearrange("p (t c) -> p t c", t=2), ACT.Copy)
                act.activation(scsb[0:NS, b, 2, cols], src[0:NS, 2 * KEYS:3 * KEYS], ACT.Copy).then_inc(a_done, 1)
                if m % 2:
                    act.wait_ge(a_done, A_ALL * g + A_BANKS + a_score(m) + 1)
                    act.dma_start(sc_g[g, h], scsb[:, b, 0:2, :]).then_inc(score_out[b], 16)
                    act.dma_start(sc_s[g, h // 4, h % 4], scsb[0:NS, b, 2, :]).then_inc(score_out[b], 16)

            def mix(k, g):
                if k == 0:
                    act.wait_ge(x_in, 32 * (g + 1))
                    squares()
                if k == T_XN:
                    to_channels(A_XN, "norm_mix", g)
                if k == T_U:
                    if not isinstance(g, int):
                        for b in range(2):
                            act.wait_ge(score_out[b], 128 * g)
                if k in (T_U, T_U + 1):
                    for m in SLABS_OF[k]:
                        act.activation(uT[:, m, :], ready(A_U + m, g)[:, 0:N], ACT.Copy).then_inc(a_done, 1)
                if T_CONV <= k < T_SSM:
                    j = k - T_CONV
                    if j >= 2:
                        v_emptied(V_CP + j - 2, g)
                    act.activation(sig[:, j % 2, :], ready(A_CQ + j, g)[:, 0:N], ACT.Sigmoid).then_inc(a_done, 1)
                if T_SSM <= k < T_SSM + PAIRS:
                    m = k - T_SSM
                    act.activation(gates[:, m, :], ready(A_GATE + m, g)[:, 0:N], ACT.Sigmoid,
                                   bias=par("b_gate")[:, m:m + 1]).then_inc(a_done, 1)
                if k == T_GELU:
                    for t in range(CT):
                        act.wait_ge(y_summed, CT * g + t + 1)
                        act.activation(yT[:, t, :], yT[:, t, :], ACT.Gelu).then_inc(y_gelu, 1)
                if T_GLU <= k < T_GLU + 4:
                    glu(2 * (k - T_GLU), g)
                    glu(2 * (k - T_GLU) + 1, g)
                if k == T_MEAN + 1:
                    v_emptied(V_MEAN, g)
                    act.activation(sq[:, :, :], acc[:, :, :], ACT.Square).then_inc(xc_sq, 1)
                if k == T_VAR + 1:
                    v_emptied(V_VAR, g)
                    act.activation(lnr[1][:, 0:NC], lnr[0][:, 0:NC], ACT.Sqrt).then_inc(std_ready, 1)
                if k == T_LN:
                    act.wait_ge(ln_ready, g + 1)
                    for c in range(CT):
                        act.activation(sq[:, c, :], acc[:, c, :], ACT.Sigmoid, bias=par("ln_b")[:, c:c + 1],
                                       scale=par("ln_g")[:, c:c + 1]).then_inc(ln_sig, 1)
                for j in OUT_OF.get(k, ()):
                    act.activation(outT[:, j, :], ready(A_OUT + j, g)[:, 0:N], ACT.Copy).then_inc(a_done, 1)
                if k == T_SQ:
                    v_emptied(V_ALL - 1, g)
                    act.dma_start(x2_g[g], xt[:, 0:2, :]).then_inc(rows_out, 16)
                    act.dma_start(x2_s[g], xt[0:NS, 2, :]).then_inc(rows_out, 16)
                    squares()
                if k == T_XN2:
                    to_channels(A_XN2, "norm_ffn", g)
                    act.wait_ge(xh_ready, 2 * g + 2)
                    for t in range(2):
                        act.dma_start(rs_g[g, t], rstd[:, t:t + 1]).then_inc(rs_out, 16)
                    act.dma_start(rs_s[g], rstd[0:NS, 2:3]).then_inc(rs_out, 16)
                for m in Q_OF.get(k, ()):
                    act.activation(qT[:, m % 2, :], ready(a_q(m), g)[:, 0:N], ACT.Copy).then_inc(a_done, 1)
                    if m:
                        keep_scores(m - 1, g)
                if k == TURNS - 1:
                    keep_scores(2 * HEADS - 1, g)

            def exps(n):
                act.wait_ge(shift_done, 2 * n + 2)
                act.activation(ex[:, :, :], shifted[:, :, :], ACT.Exp).then_inc(exp_done, 1)

            shape = [par("eye")]

            def peer(n, r, last=False):
                for b in range(TB * r, TB * r + TB):
                    cols = slice(b * BATCH, (b + 1) * BATCH)
                    act.wait_ge(dots_done, PB * n + b + 1)
                    act.activation(act_v[:, cols], dots[:, cols], ACT.Gelu).then_inc(gelu_done, 1)
                    act.wait_ge(coef_done, PB * n + b + 1)
                    for s in range(b * BATCH, (b + 1) * BATCH):
                        act.activation(diag[:, s % RING, :], shape[0], ACT.Copy, scale=coef[:, s:s + 1]).then_inc(diag_done, 1)
                if r == PTURNS - 1 and not last:
                    exps(n + 1)

            def start(t):
                if isinstance(t, int) and t == TILES:
                    shape[0] = par("fold")

            def end(t):
                steps = PAIR * (TILES * TPAIRS + SPAIRS) if isinstance(t, int) and t == TILES else PAIR * TPAIRS * (t + 1)
                act.wait_ge(y_out, 16 * t + 16)
                act.wait_ge(slot_free, RING + steps)
                act.activation(yt[:, :], flat(ps_acc[:, :, :]), ACT.Square, accum_out=fin[:, 0:1]).then_inc(y_sq, 1)
                act.wait_ge(y_ms, 1 * t + 1)
                act.activation(fin[:, 2:3], fin[:, 1:2], ACT.Sqrt).then_inc(y_std, 1)

            act.sem_inc(a_done, A_BANKS)
            act.wait_ge(cleared, 1)
            mix(0, 0)
            act.wait_ge(kept_in, 16)
            act.wait_ge(first_in, 16)
            act.activation(sm[:, 0, :], par1("log_step"), ACT.Exp).then_inc(setup_a, 1)
            act.wait_ge(setup_v, 1)
            act.activation(rho[:, :], sm[:, 4, :], ACT.Exp).then_inc(setup_a, 1)
            act.wait_ge(setup_v, 2)
            act.activation(sm[:, 6, :], sm[:, 3, :], ACT.Sin).then_inc(setup_a, 1)
            act.activation(sm[:, 7, :], sm[:, 5, :], ACT.Sin).then_inc(setup_a, 1)
            for k in range(1, TURNS):
                mix(k, 0)
            exps(0)
            with act.Fori(0, GROUPS - 1) as g:
                for k in range(TURNS):
                    mix_first = k in (T_XN, T_XN2, TURNS // 2) or len(Q_OF.get(k, ())) > 1
                    if mix_first:
                        mix(k, g + 1)
                    if k == TURNS // 2:
                        end(2 * g)
                    peer(GPAIRS * g + k // PTURNS, k % PTURNS)
                    if not mix_first:
                        mix(k, g + 1)
                    if k == TURNS - 1:
                        end(2 * g + 1)
            last_tiles(act, start, peer, end)

        @block.vector
        def _(dve):
            count = [0]

            def restart():
                dve.sem_clear(v_chain)
                count[0] = 0

            def mark(ins):
                count[0] += 1
                ins.then_inc(v_chain, 1)
                return count[0]

            def after(n):
                dve.wait_ge(v_chain, n)

            def step(ins):
                after(mark(ins))

            def setup_constants():
                step(dve.memset(ssq[:, :], float(D)))
                dve.memset(half[:, :], -0.5)
                dve.memset(mean_w[:, :], 1.0 / DC)
                dve.memset(tails[:, :, 0:HALO], 0.0).then_inc(cleared, 1)
                dve.memset(bpad[:, :, :, :], 0.0)
                dve.memset(cst[:, :, :, :], 0.0)
                step(dve.memset(carry[:, :, :, :], 0.0))

            def setup_angle():
                dve.wait_ge(kept_in, 16)
                dve.tensor_copy(tails[:, :, HALO:2 * HALO], par("cache").rearrange("p (c k) -> p c k", c=CT))
                dve.wait_ge(first_in, 16)
                dve.tensor_copy(carry[:, 0, :, 1], par1("h0_re"))
                step(dve.tensor_copy(carry[:, 1, :, 1], par1("h0_im")))
                lr, li = par1("lam_re"), par1("lam_im")
                dve.wait_ge(setup_a, 1)
                dve.tensor_tensor(sm[:, 1, :], li, sm[:, 0, :], ALU.mult)
                dve.tensor_tensor(sm[:, 4, :], lr, sm[:, 0, :], ALU.mult).then_inc(setup_v, 1)
                dve.wait_ge(setup_v, 1)
                magic = float(3 * 2 ** 22)
                step(dve.tensor_scalar(sm[:, 2, :], sm[:, 1, :], 0.15915494309189535, magic, ALU.mult, ALU.add))
                step(dve.tensor_scalar(sm[:, 2, :], sm[:, 2, :], magic, None, ALU.subtract))
                step(dve.scalar_tensor_tensor(sm[:, 3, :], sm[:, 2, :], -6.28125, sm[:, 1, :], ALU.mult, ALU.add))
                step(dve.scalar_tensor_tensor(sm[:, 3, :], sm[:, 2, :], -0.0019353071795864769, sm[:, 3, :],
                                              ALU.mult, ALU.add))
                step(dve.tensor_scalar(sm[:, 3, :], sm[:, 3, :], 3.1415925, -3.1415925, ALU.min, ALU.max))
                step(dve.tensor_scalar(sm[:, 5, :], sm[:, 3, :], -1.0, None, ALU.mult))
                step(dve.tensor_tensor(sm[:, 5, :], sm[:, 5, :], sm[:, 3, :], ALU.min))
                dve.tensor_scalar(sm[:, 5, :], sm[:, 5, :], 1.5707963267948966, None, ALU.add).then_inc(setup_v, 1)

            def setup():
                lr, li = par1("lam_re"), par1("lam_im")
                dve.wait_ge(setup_a, 4)
                sin, cos = sm[:, 6, :], sm[:, 7, :]
                dve.tensor_copy(cosT[:, :, 0], cos)
                dve.tensor_copy(sinT[:, :, 0], sin)
                step(dve.tensor_tensor(sm[:, 0, :], rho[:, :], cos, ALU.mult))
                dve.tensor_scalar(sm[:, 0, :], sm[:, 0, :], -1.0, None, ALU.add)
                dve.tensor_tensor(sm[:, 1, :], rho[:, :], sin, ALU.mult)
                dve.tensor_tensor(sm[:, 2, :], lr, lr, ALU.mult)
                step(dve.tensor_tensor(sm[:, 3, :], li, li, ALU.mult))
                step(dve.tensor_tensor(sm[:, 2, :], sm[:, 2, :], sm[:, 3, :], ALU.add))
                step(dve.reciprocal(sm[:, 8, :], sm[:, 2, :]))
                dve.tensor_tensor(sm[:, 2, :], sm[:, 0, :], lr, ALU.mult)
                dve.tensor_tensor(sm[:, 3, :], sm[:, 1, :], li, ALU.mult)
                dve.tensor_tensor(sm[:, 9, :], sm[:, 1, :], lr, ALU.mult)
                step(dve.tensor_tensor(sm[:, 10, :], sm[:, 0, :], li, ALU.mult))
                dve.tensor_tensor(sm[:, 2, :], sm[:, 2, :], sm[:, 3, :], ALU.add)
                step(dve.tensor_tensor(sm[:, 9, :], sm[:, 9, :], sm[:, 10, :], ALU.subtract))
                dve.tensor_tensor(sm[:, 11, :], sm[:, 2, :], sm[:, 8, :], ALU.mult)
                step(dve.tensor_tensor(sm[:, 12, :], sm[:, 9, :], sm[:, 8, :], ALU.mult))
                for half_pair in range(2):
                    part_rows = slice(64 * half_pair, 64 * half_pair + 64)
                    cols = slice(SG * half_pair, SG * half_pair + SG)

                    def v3(name):
                        return par1(name)[part_rows].rearrange("p (j h) -> p j h", j=PAIRS)

                    def bc(n):
                        return sm[part_rows, n, :].unsqueeze(2).to_broadcast([64, PAIRS, SG])

                    tmp = [scratch[part_rows, n * PAIRS * SG:(n + 1) * PAIRS * SG].rearrange("p (j h) -> p j h", j=PAIRS)
                           for n in range(4)]
                    dve.tensor_tensor(tmp[0], v3("b_re"), bc(11), ALU.mult)
                    dve.tensor_tensor(tmp[1], v3("b_im"), bc(12), ALU.mult)
                    dve.tensor_tensor(tmp[2], v3("b_im"), bc(11), ALU.mult)
                    step(dve.tensor_tensor(tmp[3], v3("b_re"), bc(12), ALU.mult))
                    dve.tensor_tensor(bpad[part_rows, 0, :, cols], tmp[0], tmp[1], ALU.subtract)
                    step(dve.tensor_tensor(bpad[part_rows, 1, :, cols], tmp[2], tmp[3], ALU.add))
                    dve.tensor_copy(cst[part_rows, 0, :, cols], v3("c_re"))
                    step(dve.tensor_scalar(cst[part_rows, 1, :, cols], v3("c_im"), -1.0, None, ALU.mult))
                dve.sem_inc(setup_v, 1)
                w = 1
                while w < NP:
                    t0 = scratch[:, 0:PAIRS * w].rearrange("p (j n) -> p j n", j=PAIRS)
                    t1 = scratch[:, PAIRS * w:2 * PAIRS * w].rearrange("p (j n) -> p j n", j=PAIRS)
                    cw = cosT[:, :, w - 1:w].to_broadcast([P, PAIRS, w])
                    sw = sinT[:, :, w - 1:w].to_broadcast([P, PAIRS, w])
                    dve.tensor_tensor(t0, cosT[:, :, 0:w], cw, ALU.mult)
                    step(dve.tensor_tensor(t1, sinT[:, :, 0:w], sw, ALU.mult))
                    step(dve.tensor_tensor(cosT[:, :, w:2 * w], t0, t1, ALU.subtract))
                    dve.tensor_tensor(t0, sinT[:, :, 0:w], cw, ALU.mult)
                    step(dve.tensor_tensor(t1, cosT[:, :, 0:w], sw, ALU.mult))
                    step(dve.tensor_tensor(sinT[:, :, w:2 * w], t0, t1, ALU.add))
                    w *= 2
                dve.tensor_copy(cosT[:, :, NP:N], cosT[:, :, 0:NS])
                dve.tensor_copy(sinT[:, :, NP:N], sinT[:, :, 0:NS]).then_inc(table_done, 1)

            def ready(n, g):
                dve.wait_ge(v_ready, V_ALL * g + n + 1)
                return ps_v[:, n % V_BANKS, :]

            def emptied(n, g):
                dve.wait_ge(v_done, V_ALL * g + V_BANKS + n + 1)

            def mean_square(turn, g):
                dve.wait_ge(sq_x, 2 * g + turn)
                dve.tensor_scalar(rstd[:, :], ssq[:, :], 1.0 / D, EPS, ALU.mult, ALU.add).then_inc(ms_x, 1)

            def normalise(turn, g):
                dve.wait_ge(rs_x, 2 * g + turn)
                for t, (_, w) in enumerate(SPANS):
                    last = dve.tensor_scalar(xh[t], xt[0:w, t, :], rstd[0:w, t:t + 1], None, ALU.mult)
                last.then_inc(xh_ready, 1)

            def scan(j, g):
                re, im = ready(V_B + 2 * j, g), ready(V_B + 2 * j + 1, g)
                if not isinstance(g, int):
                    dve.wait_ge(trig_in[j % TRIGS], 16 * (PAIRS // TRIGS * (g - 1) + j // TRIGS + 1))
                c, s = angles(j, g)
                dve.tensor_tensor(rot[:, 0, :], re[:, 0:N], c, ALU.mult)
                step(dve.tensor_tensor(rot[:, 1, :], im[:, 0:N], s, ALU.mult))
                step(dve.tensor_tensor(rin[:, 0, :], rot[:, 0, :], rot[:, 1, :], ALU.add))
                dve.tensor_tensor(rot[:, 0, :], im[:, 0:N], c, ALU.mult)
                dve.tensor_tensor(rot[:, 1, :], re[:, 0:N], s, ALU.mult).then_inc(v_done, 2)
                emptied(V_B + 2 * j + 1, g)
                b = mark(dve.tensor_tensor(rin[:, 1, :], rot[:, 0, :], rot[:, 1, :], ALU.subtract))
                dve.wait_ge(unrotated, PAIRS * g + PAIRS + j - 1)
                for p in range(2):
                    if p:
                        after(b)
                    for stream, (lo, hi) in enumerate(SEGS):
                        last = dve.tensor_tensor_scan(
                            grot[:, j % 2, p, lo:hi], rho[:, j:j + 1].to_broadcast([P, hi - lo]),
                            rin[:, p, lo:hi], carry[:, p, j, stream:stream + 1], ALU.mult, ALU.add)
                last.then_inc(scanned, 1)

            def skip(t, g):
                dve.wait_ge(c_done, PAIRS * g + 2 + 4 * t + 4)
                dve.scalar_tensor_tensor(yT[:, t, :], uT[:, t, :], par("d_skip")[:, t:t + 1],
                                         ps_y[:, 0:N], ALU.mult, ALU.add).then_inc(y_summed, 1)

            before = [0] * CT

            def tap(k):
                taps = par("conv_w")
                for c in range(CT):
                    src, wk = vbuf[:, c, k:k + NC], taps[:, c * TAPS + k:c * TAPS + k + 1]
                    if k == 0:
                        before[c] = mark(dve.tensor_scalar(acc[:, c, :], src, wk, par("conv_b")[:, c:c + 1],
                                                           ALU.mult, ALU.add))
                    else:
                        after(before[c])
                        last = dve.scalar_tensor_tensor(acc[:, c, :], src, wk, acc[:, c, :], ALU.mult, ALU.add)
                        if k < TAPS - 1:
                            before[c] = mark(last)
                if k == TAPS - 1:
                    last.then_inc(conv_ready, 1)

            def glu(j, g):
                dve.wait_ge(a_done, A_ALL * g + A_BANKS + A_GLU + j + 1)
                src = ready(V_GLU + j, g)
                dve.tensor_tensor(rot[:, j % 2, :], src[:, 0:N], sig[:, j % 2, :], ALU.mult).then_inc(v_done, 1)
                emptied(V_GLU + j, g)
                mark(dve.tensor_tensor(merged[:, j, :], rot[:, j % 2, :], gates[:, j, :], ALU.mult))

            def mix(k, g):
                if k in (T_X + 1, T_SQ + 1):
                    mean_square(1 if k == T_X + 1 else 2, g)
                if k in (T_X + 2, T_SQ + 2):
                    normalise(1 if k == T_X + 2 else 2, g)
                if T_CONV < k <= T_CONV + CT:
                    j = k - T_CONV - 1
                    dve.wait_ge(a_done, A_ALL * g + A_BANKS + A_CQ + j + 1)
                    src = ready(V_CP + j, g)
                    if j == 0:
                        dve.tensor_copy(vbuf[:, :, 0:HALO], tails[:, :, 0:HALO])
                        step(dve.tensor_copy(vbuf[:, :, SOFF:SOFF + HALO], tails[:, :, HALO:2 * HALO]))
                    dve.tensor_tensor(vbuf[:, j, HALO:HALO + NP], src[:, 0:NP], sig[:, j % 2, 0:NP], ALU.mult)
                    dve.tensor_tensor(vbuf[:, j, SOFF + HALO:NV], src[:, NP:N], sig[:, j % 2, NP:N],
                                      ALU.mult).then_inc(v_done, 1)
                    if j == CT - 1:
                        emptied(V_CP + CT - 1, g)
                        dve.tensor_copy(tails[:, :, 0:HALO], vbuf[:, :, NP:NP + HALO])
                        step(dve.tensor_copy(tails[:, :, HALO:2 * HALO], vbuf[:, :, NV - HALO:NV]))
                if T_SSM <= k < T_SSM + PAIRS:
                    if k > T_SSM + 4 and (k - T_SSM) % 4 == 1:
                        skip((k - T_SSM) // 4 - 1, g)
                    scan(k - T_SSM, g)
                if k == T_GELU:
                    skip(CT - 1, g)
                for tap_k in TAPS_OF.get(k, ()):
                    tap(tap_k)
                if T_GLU < k <= T_GLU + 4:
                    glu(2 * (k - T_GLU) - 2, g)
                    glu(2 * (k - T_GLU) - 1, g)
                if k == T_MEAN + 1:
                    dve.wait_ge(conv_ready, g + 1)
                    src = ready(V_MEAN, g)
                    for c in range(CT):
                        last = dve.tensor_tensor(acc[:, c, :], acc[:, c, :], src[:, 0:NC], ALU.subtract)
                    last.then_inc(v_done, 1)
                if k == T_VAR + 1:
                    src = ready(V_VAR, g)
                    dve.tensor_scalar(lnr[0][:, 0:NC], src[:, 0:NC], EPS, None, ALU.add).then_inc(v_done, 1)
                if k == T_LN:
                    dve.wait_ge(std_ready, g + 1)
                    step(dve.reciprocal(lnr[0][:, 0:NC], lnr[1][:, 0:NC]))
                    for c in range(CT):
                        last = dve.tensor_tensor(acc[:, c, :], acc[:, c, :], lnr[0][:, 0:NC], ALU.mult)
                    last.then_inc(ln_ready, 1)
                if k == T_SWISH:
                    dve.wait_ge(ln_ready, g + 1)
                    for c in range(CT):
                        dve.wait_ge(ln_sig, CT * g + c + 1)
                        step(dve.tensor_scalar(acc[:, c, :], acc[:, c, :], par("ln_g")[:, c:c + 1],
                                               par("ln_b")[:, c:c + 1], ALU.mult, ALU.add))
                        dve.tensor_tensor(cs[:, c, 0:NP], acc[:, c, 0:NP], sq[:, c, 0:NP], ALU.mult)
                        dve.tensor_tensor(cs[:, c, NP:N], acc[:, c, SOFF:NC], sq[:, c, SOFF:NC],
                                          ALU.mult).then_inc(cs_ready, 1)
                if T_COUT < k <= T_COUT + 4:
                    for j in range(2 * (k - T_COUT) - 2, 2 * (k - T_COUT)):
                        src = ready(V_COUT + j, g)
                        dve.tensor_tensor(rot[:, j % 2, :], src[:, 0:N], gates[:, DT + j, :], ALU.mult).then_inc(v_done, 1)
                        emptied(V_COUT + j, g)
                        dve.tensor_tensor(merged[:, j, :], merged[:, j, :], rot[:, j % 2, :], ALU.add).then_inc(merged_done, 1)
                if T_ROWS < k <= T_ROWS + 3:
                    t = k - T_ROWS - 1
                    w = SPANS[t][1]
                    for h in range(2):
                        src = ready(V_TOK + 2 * t + h, g)
                        half_rows = xt[0:w, t, h * 512:(h + 1) * 512]
                        dve.tensor_tensor(half_rows, half_rows, src[0:w, :], ALU.add).then_inc(v_done, 1)

            grid = [P, TOPK, TOPK]
            iota = par("iota")

            def key_top(n, a, f):
                if f == 0:
                    dve.wait_ge(score_in[a], 16 * (n + 1))
                    dve.sem_inc(v_passed, 1)
                s = sc[:, a, f * KEYS:(f + 1) * KEYS]
                step(dve.max(topv[:, f, 0:8], s))
                step(dve.max_index(topi[:, f, 0:8], topv[:, f, 0:8], s))
                step(dve.match_replace(s, topv[:, f, 0:8], s, NEG))
                step(dve.max(topv[:, f, 8:16], s))
                step(dve.max_index(topi[:, f, 8:16], topv[:, f, 8:16], s))
                if f == 1:
                    dve.sem_inc(score_used, 1)

            def pair_top(a):
                step(dve.tensor_tensor(cand[:, :, :], topv[:, 0, :].unsqueeze(2).to_broadcast(grid),
                                       topv[:, 1, :].unsqueeze(1).to_broadcast(grid), ALU.add))
                pairs = flat(cand[:, :, :])
                step(dve.max(best[:, 0:8], pairs))
                step(dve.max_index(pos[:, 0:8], best[:, 0:8], pairs))
                step(dve.match_replace(pairs, best[:, 0:8], pairs, NEG))
                step(dve.max(best[:, 8:16], pairs))
                dve.tensor_scalar(shifted[:, a, :], best[:, :], best[:, 0:1], None, ALU.subtract).then_inc(shift_done, 1)
                step(dve.max_index(pos[:, 8:16], best[:, 8:16], pairs))

            def experts_of(a):
                dve.tensor_scalar(hilo[:, 0, :], pos[:, :], 4, None, ALU.logical_shift_right)
                step(dve.tensor_scalar(hilo[:, 1, :], pos[:, :], TOPK - 1, None, ALU.bitwise_and))
                for f in range(2):
                    step(dve.tensor_tensor(hot[:, :, :], hilo[:, f, :].unsqueeze(2).to_broadcast(grid),
                                           iota.unsqueeze(1).to_broadcast(grid), ALU.is_equal))
                    step(dve.tensor_tensor(hot[:, :, :], hot[:, :, :],
                                           topi[:, f, :].unsqueeze(1).to_broadcast(grid), ALU.mult))
                    step(dve.tensor_reduce(part[:, f, :], hot[:, :, :], AXIS, ALU.add))
                dve.scalar_tensor_tensor(idx[:, a, :], part[:, 0, :], float(KEYS), part[:, 1, :],
                                         ALU.mult, ALU.add).then_inc(idx_ready, 1)

            def choose(n, r):
                a, p = divmod(r, PTURNS // 2)
                if p < 2:
                    key_top(n, a, p)
                elif p == 2:
                    pair_top(a)
                else:
                    experts_of(a)

            def weights(n):
                dve.wait_ge(exp_done, n + 1)
                step(dve.tensor_reduce(den[:, 0, :], ex[:, :, :], AXIS, ALU.add))
                step(dve.reciprocal(den[:, 1, :], den[:, 0, :]))
                step(dve.tensor_tensor(soft[:, :, :], ex[:, :, :],
                                       den[:, 1, :].unsqueeze(2).to_broadcast([P, 2, TOPK]), ALU.mult))

            def coefficients(n, batch):
                dve.wait_ge(gelu_done, PB * n + batch + 1)
                cols = slice(batch * BATCH, (batch + 1) * BATCH)
                dve.tensor_tensor(coef[:, cols], act_v[:, cols], flat(soft[:, :, :])[:, cols],
                                  ALU.mult).then_inc(coef_done, 1)

            def peer(n, r, last=False, between=None):
                if r == 0:
                    weights(n)
                for s in range(STEPS * r, STEPS * r + STEPS):
                    slot, b = s % RING, s // BATCH
                    if s % STEPS == BATCH + 1 and not between:
                        coefficients(n, b - 1)
                    dve.wait_ge(landed[slot], 16 * (PAIR // RING * n + s // RING + 1))
                    ins = dve.tensor_tensor_reduce(rows[:, slot, 0:D], rows[:, slot, 0:D], xn[:, :], 1.0, 0.0,
                                                   ALU.mult, ALU.add, dots[:, s:s + 1])
                    if s % BATCH == BATCH - 1:
                        ins.then_inc(dots_done, 1)
                if between:
                    between()
                    coefficients(n, b - 1)
                if not last:
                    choose(n + 1, r)
                coefficients(n, b)

            def start(t):
                dve.wait_ge(x2_in, loads_of(t))
                dve.wait_ge(rs_in, loads_of(t))
                dve.scalar_tensor_tensor(xn[:, :], x2t[:, :], rst[:, 0:1], gf[:, :], ALU.mult, ALU.mult).then_inc(xn_ready, 1)
                dve.wait_ge(xn_ready, 1 * t + 2)
                dve.sem_inc(v_passed, 1)

            def end(t):
                dve.wait_ge(y_sq, 1 * t + 1)
                dve.tensor_scalar(fin[:, 1:2], fin[:, 0:1], 1.0 / D, EPS, ALU.mult, ALU.add).then_inc(y_ms, 1)
                dve.wait_ge(y_std, 1 * t + 1)
                step(dve.reciprocal(fin[:, 3:4], fin[:, 2:3]))
                dve.scalar_tensor_tensor(yt[:, :], flat(ps_acc[:, :, :]), fin[:, 3:4],
                                         gl[:, :], ALU.mult, ALU.mult).then_inc(y_ready, 1)

            setup_constants()
            dve.sem_inc(v_done, V_BANKS)
            dve.sem_inc(y_ready, 1)
            dve.sem_inc(xn_ready, 1)
            mix(0, 0)
            mix(1, 0)
            setup_angle()
            mix(2, 0)
            setup()
            for k in range(3, TURNS):
                if k == T_SSM - 1:
                    dve.wait_ge(setup_t, 1)
                    dve.tensor_copy(bst[:, :, :, :].rearrange("p c t q -> p c (t q)"), ps_acc[:, :, :]).then_inc(setup_b, 1)
                mix(k, 0)
                if T_Q + 4 <= k < T_Q + 4 + PTURNS:
                    choose(0, k - T_Q - 4)
            dve.wait_ge(norms_in, 16)
            with dve.Fori(0, GROUPS - 1) as g:
                restart()
                for k in range(TURNS):
                    mix(k, g + 1)
                    if k % (TURNS // 2) == 0:
                        start(2 * g + k // (TURNS // 2))
                    peer(GPAIRS * g + k // PTURNS, k % PTURNS,
                         between=(lambda: end(2 * g)) if k == TURNS // 2 else None)
                    if k == TURNS - 1:
                        end(2 * g + 1)

            def v_peer(n, r, last=False):
                if r == 0:
                    restart()
                peer(n, r, last)

            last_tiles(dve, start, v_peer, end)

        @block.gpsimd
        def _(pool):
            count = [0]

            def mark(ins):
                count[0] += 1
                ins.then_inc(p_chain, 1)
                return count[0]

            def rotate_back(j, g):
                pool.wait_ge(scanned, PAIRS * g + j + 1)
                b = j % 2
                c, s = angles(j, g)
                mark(pool.tensor_tensor(prod[:, 0, :], grot[:, b, 0, :], c, ALU.mult))
                re = mark(pool.tensor_tensor(prod[:, 1, :], grot[:, b, 1, :], s, ALU.mult))
                pool.wait_ge(c_done, PAIRS * g + j + 1)
                pool.wait_ge(p_chain, re)
                first_half = mark(pool.tensor_tensor(hst[:, b, 0, :], prod[:, 0, :], prod[:, 1, :], ALU.subtract))
                pool.wait_ge(p_chain, first_half)
                mark(pool.tensor_tensor(prod[:, 0, :], grot[:, b, 0, :], s, ALU.mult))
                im = mark(pool.tensor_tensor(prod[:, 1, :], grot[:, b, 1, :], c, ALU.mult))
                pool.wait_ge(p_chain, im)
                end = mark(pool.tensor_tensor(hst[:, b, 1, :], prod[:, 0, :], prod[:, 1, :], ALU.add))
                pool.wait_ge(p_chain, end)
                pool.tensor_copy(carry[:, :, j, :], hst[:, b, :, NP - 1:N:NS]).then_inc(unrotated, 1)

            def mix(k, g):
                if k in (T_X + 1, T_SQ + 1):
                    turn = 1 if k == T_X + 1 else 2
                    pool.wait_ge(ms_x, 2 * g + turn)
                    pool.tensor_tensor(rstd[:, :], rstd[:, :], half[:, 0:1].to_broadcast([P, 3]),
                                       ALU.pow).then_inc(rs_x, 1)
                if T_SSM <= k < T_SSM + PAIRS:
                    rotate_back(k - T_SSM, g)

            def gather(n, r):
                for s in range(STEPS * r, STEPS * r + STEPS):
                    slot, (a, k) = s % RING, divmod(s, TOPK)
                    if k == 0:
                        pool.wait_ge(idx_ready, 2 * n + a + 1)
                    pool.wait_ge(slot_free, PAIR * n + s + 1)
                    pool.sem_inc(gathers, 1)
                    pool.indirect_dma_start(
                        out=rows[:, slot, :], out_offset=None, in_=experts,
                        in_offset=bass.IndirectOffsetOnAxis(ap=idx[:, a, k:k + 1], axis=0),
                    ).then_inc(landed[slot], 16)

            def next_gathers(n, r, last=False):
                if r < PTURNS - 2:
                    gather(n, r + 2)
                elif not last:
                    gather(n + 1, r + 2 - PTURNS)

            pool.sem_inc(unrotated, PAIRS)
            pool.sem_inc(c_done, 2)
            for k in range(TURNS):
                mix(k, 0)
            pool.wait_ge(trig_stored, 16)
            gather(0, 0)
            gather(0, 1)
            with pool.Fori(0, GROUPS - 1) as g:
                pool.sem_clear(p_chain)
                count[0] = 0
                for k in range(TURNS):
                    mix(k, g + 1)
                    next_gathers(GPAIRS * g + k // PTURNS, k % PTURNS)
            last_tiles(pool, lambda t: None, next_gathers, lambda t: None)

def _lay_out(inputs):
    import numpy as np

    def a(name):
        return np.asarray(inputs[name])

    def state_major(x):
        return x.reshape(PAIRS, P).T

    def channel_major(x):
        return x.reshape(-1, P).T

    def tiles(w):
        k, m = w.shape
        return w.reshape(k // P, P, m // P, P).transpose(2, 1, 0, 3)

    fold = np.zeros((P, P), np.float32)
    fold[np.arange(P), np.arange(P) % DEC] = 1.0
    parts = {
        "lam_re": state_major(a("ssm_lambda_re")), "lam_im": state_major(a("ssm_lambda_im")),
        "log_step": state_major(np.repeat(a("ssm_log_step").reshape(-1), 64)),
        "h0_re": state_major(a("state_ssm_re")), "h0_im": state_major(a("state_ssm_im")),
        "b_re": a("ssm_b_re").reshape(PAIRS, P, SG).transpose(1, 0, 2).reshape(P, -1),
        "b_im": a("ssm_b_im").reshape(PAIRS, P, SG).transpose(1, 0, 2).reshape(P, -1),
        "c_re": a("ssm_c_re").reshape(PAIRS, 2, SG, 64).transpose(1, 3, 0, 2).reshape(P, -1),
        "c_im": a("ssm_c_im").reshape(PAIRS, 2, SG, 64).transpose(1, 3, 0, 2).reshape(P, -1),
        "d_skip": channel_major(a("ssm_d")), "norm_mix": channel_major(a("norm_mix")),
        "norm_ffn": channel_major(a("norm_ffn")), "b_gate": channel_major(a("b_gate")),
        "conv_w": a("conv_w").reshape(TAPS, CT, P).transpose(2, 1, 0).reshape(P, -1),
        "conv_b": channel_major(a("conv_b")), "ln_g": channel_major(a("conv_ln_g")),
        "ln_b": channel_major(a("conv_ln_b")),
        "cache": a("cache_conv").reshape(HALO, CT, P).transpose(2, 1, 0).reshape(P, -1),
        "eye": np.eye(P, dtype=np.float32), "fold": fold,
        "iota": np.tile(np.arange(TOPK, dtype=np.float32), (P, 1)),
        "keys": np.concatenate([a("peer_keys1")[0].T, a("peer_keys2")[0].T], axis=1),
    }
    kept = np.concatenate([parts[name] for name, _ in KEPT], axis=1)
    first = np.concatenate([parts[name] for name, _ in FIRST], axis=1)
    w_in = tiles(a("w_in")[0])
    glu = tiles(a("w_ssm_glu")[0])
    cout = tiles(a("w_conv_out")[0])
    order = [0, 1, 2, 3, 8, 4, 9, 5, 10, 6, 11, 7, *range(12, 28)]
    slabs = [w_in[m] for m in order]
    slabs += [np.concatenate([glu[DT + j], glu[j]], axis=1) for j in range(DT)]
    slabs += [np.concatenate([cout[2 * j], cout[2 * j + 1]], axis=1) for j in range(DT // 2)]
    slabs += list(tiles(a("w_out")[0])) + list(tiles(a("peer_w_q")[0]))
    slabs = np.stack([s.reshape(P, D) for s in slabs])
    return kept, first, slabs


def kernel(**inputs):
    import numpy as np
    import concourse.bacc as bacc
    from concourse.bass_utils import run_bass_kernel_spmd

    kept, first, slabs = _lay_out(inputs)
    experts = np.concatenate([np.asarray(inputs["peer_u"])[0], np.asarray(inputs["peer_v"])[0]], axis=1)
    arrays = {
        "in_x_prompt": np.asarray(inputs["x_prompt"]), "in_x_sample": np.asarray(inputs["x_sample"]),
        "in_kept": kept, "in_first": first, "in_slabs": slabs, "in_experts": experts,
        "in_g_ffn": np.asarray(inputs["norm_ffn"]), "in_g_final": np.asarray(inputs["norm_final"]).reshape(1, D),
    }
    arrays = {k: np.ascontiguousarray(v) for k, v in arrays.items()}
    outs = {"out_y_prompt": (1, SEQ, D), "out_y_sample": (1, DEC, D), "out_ssm": (P, 4 * PAIRS),
            "out_conv": (P, 2 * CT * HALO)}

    nc = bacc.Bacc("TRN2", target_bir_lowering=False, num_devices=1)
    d = {k: nc.dram_tensor(k, v.shape, F32, kind="ExternalInput").ap() for k, v in arrays.items()}
    d |= {k: nc.dram_tensor(k, s, F32, kind="ExternalOutput").ap() for k, s in outs.items()}
    x2_d = nc.dram_tensor("x2_rows", (SEQ + DEC, D), F32, kind="Internal").ap()
    rs_d = nc.dram_tensor("inverse_roots", (SEQ + DEC, 1), F32, kind="Internal").ap()
    score_d = nc.dram_tensor("score_rows", (BLOCKS, P, 2 * KEYS), F32, kind="Internal").ap()
    trig_d = nc.dram_tensor("trig_rows", (PAIRS, P, 2 * N), F32, kind="Internal").ap()
    program(nc, d["in_x_prompt"], d["in_x_sample"], d["in_kept"], d["in_first"], d["in_slabs"], d["in_experts"],
            d["in_g_ffn"], d["in_g_final"], x2_d, rs_d, score_d, trig_d,
            d["out_y_prompt"], d["out_y_sample"], d["out_ssm"], d["out_conv"])
    r = run_bass_kernel_spmd(nc, [arrays], core_ids=[0]).results[0]

    ssm = np.asarray(r["out_ssm"]).reshape(P, 2, PAIRS, 2).transpose(3, 1, 2, 0).reshape(2, 2, 1, 1, 2 * PAIRS, 64)
    conv = np.asarray(r["out_conv"]).reshape(P, CT, 2, HALO).transpose(2, 3, 1, 0).reshape(2, 1, 1, HALO, DC)
    return (r["out_y_prompt"], r["out_y_sample"], ssm[0, 0], ssm[0, 1], conv[0], ssm[1, 0], ssm[1, 1], conv[1])
```
